# Optimizing a Trainium2 kernel written in Bass

```python
import jax, jax.numpy as jnp
from jax import lax
import numpy as np

D_MODEL = 1024
BATCH = 1
SEQ = 256
DEPTH = 2

A_HEADS = 4
A_DK = 128
A_DV = 128
A_KD = A_HEADS * A_DK
A_WIDTH = A_HEADS * A_DV
A_CHUNK = 64
B_Q_HEADS = 8
B_KV_HEADS = 2
B_HEAD_DIM = 64
B_WIDTH = B_Q_HEADS * B_HEAD_DIM
B_KV_WIDTH = B_KV_HEADS * B_HEAD_DIM
WINDOW = 128
ROPE_DIM = B_HEAD_DIM // 4
ROPE_THETA = 500000.0
AB_IN_WIDTH = 2 * A_KD + 2 * A_WIDTH + B_WIDTH + 2 * B_KV_WIDTH
AB_OUT_WIDTH = A_WIDTH + B_WIDTH
POOL_WINDOWS = (2, 4, 8, 16)
POOL_GROUPS = 4
POOL_GROUP = D_MODEL // POOL_GROUPS
D_FF = 2816
CONV_WIDTH = 3
N_EVEN = (DEPTH + 1) // 2
N_ODD = DEPTH // 2
ALPHA = (2.0 * DEPTH) ** 0.25
BETA = (8.0 * DEPTH) ** -0.25
LN_EPS = 1e-5
RMS_EPS = 1e-6


F32 = jnp.float32

def _layer_norm(x, g, b):
    xf = x.astype(F32)
    mu = xf.mean(-1, keepdims=True)
    var = jnp.mean(jnp.square(xf - mu), -1, keepdims=True)
    return ((xf - mu) * lax.rsqrt(var + LN_EPS) * g + b).astype(x.dtype)

def _rope(x, cos, sin):
    half = ROPE_DIM // 2
    x1 = x[..., :half].astype(F32)
    x2 = x[..., half:ROPE_DIM].astype(F32)
    r1 = x1 * cos - x2 * sin
    r2 = x2 * cos + x1 * sin
    return jnp.concatenate([r1.astype(x.dtype), r2.astype(x.dtype), x[..., ROPE_DIM:]], -1)

def _hgrn2(q, fz, i, lb):
    Bn, T = q.shape[:2]
    fzf = fz.astype(F32)
    f = lb + (1.0 - lb) * jax.nn.sigmoid(fzf)
    logf = jnp.log(f)
    k = (1.0 - lb) * jax.nn.sigmoid(-fzf)
    nc = T // A_CHUNK

    def to_chunks(a):
        a = a.reshape(Bn, nc, A_CHUNK, A_HEADS, a.shape[-1])
        return a.transpose(1, 0, 3, 2, 4)

    qc, kc, vc, gc = (to_chunks(a) for a in (q.astype(F32), k, i.astype(F32), logf))
    causal = jnp.tril(jnp.ones((A_CHUNK, A_CHUNK), bool))[:, :, None]

    def step(S, inp):
        qb, kb, vb, gb = inp
        b = jnp.cumsum(gb, axis=2)
        o_inter = jnp.einsum('bhtk,bhkv->bhtv', qb * jnp.exp(b), S)
        diff = b[:, :, :, None, :] - b[:, :, None, :, :]
        decay = jnp.exp(jnp.where(causal, diff, -jnp.inf))
        att = jnp.einsum('bhtk,bhsk,bhtsk->bhts', qb, kb, decay)
        o = o_inter + jnp.einsum('bhts,bhsv->bhtv', att, vb)
        b_last = b[:, :, -1:, :]
        S = jnp.exp(b_last[:, :, 0])[..., None] * S + jnp.einsum(
            'bhsk,bhsv->bhkv', kb * jnp.exp(b_last - b), vb)
        return S, o

    S0 = jnp.zeros((Bn, A_HEADS, A_DK, A_DV), F32)
    _, o = lax.scan(step, S0, (qc, kc, vc, gc))
    return o.transpose(1, 0, 3, 2, 4).reshape(Bn, T, A_HEADS, A_DV)

def _swa(q, k, v, sinks):
    Bn, T = q.shape[:2]
    nb = T // WINDOW
    G = B_Q_HEADS // B_KV_HEADS
    qb = q.reshape(Bn, nb, WINDOW, B_KV_HEADS, G, B_HEAD_DIM)

    def band(a):
        a = a.reshape(Bn, nb, WINDOW, B_KV_HEADS, B_HEAD_DIM)
        prev = jnp.pad(a, ((0, 0), (1, 0), (0, 0), (0, 0), (0, 0)))[:, :-1]
        return jnp.concatenate([prev, a], axis=2)

    kb, vb = band(k), band(v)
    s = jnp.einsum('bnqhgd,bnkhd->bnhgqk', qb, kb).astype(F32) * (B_HEAD_DIM ** -0.5)
    qi = jnp.arange(WINDOW)[:, None] + WINDOW
    ki = jnp.arange(2 * WINDOW)[None, :]
    rel = qi - ki
    allowed = (rel >= 0) & (rel < WINDOW)
    blk = jnp.arange(nb)[:, None, None]
    valid = allowed[None] & ((blk > 0) | (ki[None] >= WINDOW))
    s = jnp.where(valid[None, :, None, None], s, -jnp.inf)
    sink = sinks.astype(F32).reshape(B_KV_HEADS, G)[None, None, :, :, None, None]
    m = jnp.maximum(s.max(-1, keepdims=True), sink)
    p = jnp.exp(s - m)
    p = p / (p.sum(-1, keepdims=True) + jnp.exp(sink - m))
    o = jnp.einsum('bnhgqk,bnkhd->bnqhgd', p.astype(v.dtype), vb)
    return o.reshape(Bn, T, B_WIDTH)

def _even_mixer(h, w_in, w_out, lb, norm_g, sinks, cos, sin):
    Bn, T, _ = h.shape
    z = h @ w_in
    widths = [A_KD, A_KD, A_WIDTH, A_WIDTH, B_WIDTH, B_KV_WIDTH, B_KV_WIDTH]
    idx = np.cumsum(widths)[:-1].tolist()
    aq, af, ai, ag, bq, bk, bv = jnp.split(z, idx, axis=-1)
    oa = _hgrn2(aq.reshape(Bn, T, A_HEADS, A_DK), af.reshape(Bn, T, A_HEADS, A_DK),
                ai.reshape(Bn, T, A_HEADS, A_DV), lb.reshape(A_HEADS, A_DK))
    oa = oa * lax.rsqrt(jnp.mean(oa * oa, -1, keepdims=True) + RMS_EPS) * norm_g
    oa = oa.reshape(Bn, T, A_WIDTH).astype(h.dtype) * jax.nn.silu(ag)
    q = _rope(bq.reshape(Bn, T, B_Q_HEADS, B_HEAD_DIM), cos, sin)
    k = _rope(bk.reshape(Bn, T, B_KV_HEADS, B_HEAD_DIM), cos, sin)
    v = bv.reshape(Bn, T, B_KV_HEADS, B_HEAD_DIM)
    ob = _swa(q, k, v, sinks).astype(h.dtype)
    return jnp.concatenate([oa, ob], axis=-1) @ w_out

def _pool_mixer(h, w_grp, scale):
    Bn, T, D = h.shape
    hf = h.astype(F32).reshape(Bn, T, POOL_GROUPS, POOL_GROUP)
    t = jnp.arange(T)
    outs = []
    for gi, w in enumerate(POOL_WINDOWS):
        xg = hf[:, :, gi]
        cs = jnp.cumsum(jnp.pad(xg, ((0, 0), (w, 0), (0, 0))), axis=1)
        win_sum = cs[:, w:] - cs[:, :T]
        cnt = jnp.minimum(t + 1, w).astype(F32)[None, :, None]
        outs.append(win_sum / cnt - xg)
    pooled = jnp.stack(outs, axis=2).astype(h.dtype)
    y = jnp.einsum('btgc,gcd->btgd', pooled, w_grp)
    return y.reshape(Bn, T, D) * scale

def _conv_ffn(h, w_up, conv_w, conv_b, w_down):
    T = h.shape[1]
    u, v = jnp.split(h @ w_up, 2, axis=-1)
    up = jnp.pad(u, ((0, 0), (CONV_WIDTH - 1, 0), (0, 0)))
    uc = conv_b
    for j in range(CONV_WIDTH):
        uc = uc + up[:, j:j + T] * conv_w[j]
    return (jax.nn.silu(uc) * v) @ w_down

def first_inputs(seed: int = 0) -> dict:
    key = jax.random.key(seed)
    ks = jax.random.split(key, 20)
    n = jax.random.normal
    D = D_MODEL
    x = n(ks[0], (BATCH, SEQ, D), F32)
    c = n(ks[1], (BATCH, D), F32)
    offs = jax.random.randint(ks[2], (BATCH, 1), 0, 4096, dtype=jnp.int32)
    positions = offs + jnp.arange(SEQ, dtype=jnp.int32)[None, :]
    ada_w = n(ks[3], (DEPTH, D, 6 * D), F32) * D ** -0.5
    ada_b = 0.02 * n(ks[4], (DEPTH, 6 * D), F32)
    ln_g = 1.0 + 0.02 * n(ks[5], (DEPTH, 2, D), F32)
    ln_b = 0.02 * n(ks[6], (DEPTH, 2, D), F32)
    ab_w_in = n(ks[7], (N_EVEN, D, AB_IN_WIDTH), F32) * D ** -0.5
    ab_w_out = n(ks[8], (N_EVEN, AB_OUT_WIDTH, D), F32) * (AB_OUT_WIDTH ** -0.5 * BETA)
    hgrn_lb_raw = 0.5 * n(ks[9], (N_EVEN, A_KD), F32)
    hgrn_norm_g = 1.0 + 0.02 * n(ks[10], (N_EVEN, A_DV), F32)
    attn_sinks = 0.5 * n(ks[11], (N_EVEN, B_Q_HEADS), F32)
    pool_w = n(ks[12], (N_ODD, POOL_GROUPS, POOL_GROUP, POOL_GROUP), F32) * (POOL_GROUP ** -0.5 * BETA)
    pool_scale = 1.0 + 0.02 * n(ks[13], (N_ODD, D), F32)
    ffn_w_up = n(ks[14], (DEPTH, D, 2 * D_FF), F32) * D ** -0.5
    ffn_conv_w = n(ks[15], (DEPTH, CONV_WIDTH, D_FF), F32) * CONV_WIDTH ** -0.5
    ffn_conv_b = 0.02 * n(ks[16], (DEPTH, D_FF), F32)
    ffn_w_down = n(ks[17], (DEPTH, D_FF, D), F32) * (D_FF ** -0.5 * BETA)
    return {"x": x, "c": c, "positions": positions, "ada_w": ada_w, "ada_b": ada_b,
            "ln_g": ln_g, "ln_b": ln_b, "ab_w_in": ab_w_in, "ab_w_out": ab_w_out,
            "hgrn_lb_raw": hgrn_lb_raw, "hgrn_norm_g": hgrn_norm_g, "attn_sinks": attn_sinks,
            "pool_w": pool_w, "pool_scale": pool_scale, "ffn_w_up": ffn_w_up,
            "ffn_conv_w": ffn_conv_w, "ffn_conv_b": ffn_conv_b, "ffn_w_down": ffn_w_down}

def first_block(x, c, positions, ada_w, ada_b, ln_g, ln_b, ab_w_in, ab_w_out,
              hgrn_lb_raw, hgrn_norm_g, attn_sinks, pool_w, pool_scale,
              ffn_w_up, ffn_conv_w, ffn_conv_b, ffn_w_down):
    lb_p = jax.nn.softmax(hgrn_lb_raw.astype(F32), axis=0)
    lower_bounds = jnp.cumsum(lb_p, axis=0) - lb_p[0]
    inv_freq = ROPE_THETA ** (-jnp.arange(0, ROPE_DIM, 2, dtype=F32) / ROPE_DIM)
    ang = positions.astype(F32)[..., None] * inv_freq
    cos = jnp.cos(ang)[:, :, None, :]
    sin = jnp.sin(ang)[:, :, None, :]
    c_act = jax.nn.silu(c)
    for l in range(DEPTH):
        mod = c_act @ ada_w[l] + ada_b[l]
        sh1, sc1, g1, sh2, sc2, g2 = [m[:, None, :] for m in jnp.split(mod, 6, axis=-1)]
        h = x * (1.0 + sc1) + sh1
        if l % 2 == 0:
            e = l // 2
            y = _even_mixer(h, ab_w_in[e], ab_w_out[e], lower_bounds[e], hgrn_norm_g[e],
                            attn_sinks[e], cos, sin)
        else:
            o = l // 2
            y = _pool_mixer(h, pool_w[o], pool_scale[o])
        x = _layer_norm(ALPHA * x + g1 * y, ln_g[l, 0], ln_b[l, 0])
        h = x * (1.0 + sc2) + sh2
        y = _conv_ffn(h, ffn_w_up[l], ffn_conv_w[l], ffn_conv_b[l], ffn_w_down[l])
        x = _layer_norm(ALPHA * x + g2 * y, ln_g[l, 1], ln_b[l, 1])
    return x


GRID_W = 64
CTX_LEN = 256
H_M = 4
DH_M = 128
M_W = H_M * DH_M
H_A = 8
H_KV = 2
DH_A = 64
A_Q = H_A * DH_A
A_KV = H_KV * DH_A
GQA_GROUP = H_A // H_KV
WIN_BLOCK = 128
ROPE_THETA_2 = 10000.0
AB_WIDTHS = (M_W, M_W, M_W, M_W, 4 * H_M, A_Q, A_KV, A_KV)
MIX_W = M_W + A_Q
H_C = 4
DK_C = 128
DV_C = 256
C_K = H_C * DK_C
C_V = H_C * DV_C
GATE_RANK = 16
GATE_TAU = 16.0
C_WIDTHS = (C_K, C_K, C_V, C_V, 2 * GATE_RANK)
CHUNK = 64
N_KEYS = 128
N_EXPERTS = N_KEYS * N_KEYS
PEER_HEADS = 8
PEER_TOPK = 16
PEER_KEY_DIM = 256
PEER_HALF = PEER_KEY_DIM // 2
PEER_CHUNK = 128
N_EVEN_2 = (DEPTH + 1) // 2
N_ODD_2 = DEPTH // 2
DEEPNORM_ALPHA = (2 * DEPTH) ** 0.25
DEEPNORM_BETA = (8 * DEPTH) ** -0.25


def _layernorm(x, w, b):
    xf = x.astype(jnp.float32)
    mu = xf.mean(-1, keepdims=True)
    var = jnp.mean(jnp.square(xf - mu), -1, keepdims=True)
    return ((xf - mu) * lax.rsqrt(var + LN_EPS)).astype(x.dtype) * w + b

def _split(a, widths):
    idx = np.cumsum(widths)[:-1].tolist()
    return jnp.split(a, idx, axis=-1)

def _heads(a, h):
    b, s = a.shape[:2]
    return a.reshape(b, s, h, -1).transpose(0, 2, 1, 3)

def _head_norm(h, w):
    hf = h.astype(jnp.float32)
    hf = hf * lax.rsqrt(jnp.mean(hf * hf, -1, keepdims=True) + LN_EPS)
    b, nh, s, d = h.shape
    return hf.transpose(0, 2, 1, 3).reshape(b, s, nh * d) * w

def _to_chunks(a):
    b, h, s = a.shape[:3]
    a = a.reshape((b, h, s // CHUNK, CHUNK) + a.shape[3:])
    return jnp.moveaxis(a, 2, 0)

def _from_chunks(a):
    a = jnp.moveaxis(a, 0, 2)
    return a.reshape(a.shape[:2] + (-1,) + a.shape[4:])

def _mlstm_scan(q, k, v, log_i, log_f, state):
    causal = jnp.tril(jnp.ones((CHUNK, CHUNK), bool))

    def step(carry, inp):
        c_st, n_st, m_st = carry
        qc, kc, vc, li, lf = inp
        cum = jnp.cumsum(lf, axis=-1)
        dmat = cum[..., :, None] - cum[..., None, :] + li[..., None, :]
        dmat = jnp.where(causal, dmat, -jnp.inf)
        m_inter = cum + m_st[..., None]
        m_t = jnp.maximum(m_inter, dmat.max(-1))
        w = jnp.exp(dmat - m_t[..., None]) * jnp.einsum('bhtd,bhsd->bhts', qc, kc)
        a_inter = jnp.exp(m_inter - m_t)
        num = a_inter[..., None] * jnp.einsum('bhtd,bhde->bhte', qc, c_st) + jnp.einsum('bhts,bhse->bhte', w, vc)
        den = a_inter * jnp.einsum('bhtd,bhd->bht', qc, n_st) + w.sum(-1)
        h = num / jnp.maximum(jnp.abs(den), jnp.exp(-m_t))[..., None]
        total = cum[..., -1]
        decay_s = total[..., None] - cum + li
        m_new = jnp.maximum(total + m_st, decay_s.max(-1))
        ws = jnp.exp(decay_s - m_new[..., None])
        a_st = jnp.exp(total + m_st - m_new)
        c_st = a_st[..., None, None] * c_st + jnp.einsum('bhs,bhsd,bhse->bhde', ws, kc, vc)
        n_st = a_st[..., None] * n_st + jnp.einsum('bhs,bhsd->bhd', ws, kc)
        return (c_st, n_st, m_new), h

    state, hs = lax.scan(step, state, tuple(_to_chunks(a) for a in (q, k, v, log_i, log_f)))
    return _from_chunks(hs), state

def _gla_scan(q, k, v, log_a, state):
    causal = jnp.tril(jnp.ones((CHUNK, CHUNK), bool))

    def step(st, inp):
        qc, kc, vc, la = inp
        cum = jnp.cumsum(la, axis=2)
        rel = cum[:, :, :, None, :] - cum[:, :, None, :, :]
        rel = jnp.where(causal[:, :, None], rel, -jnp.inf)
        scores = jnp.einsum('bhtk,bhsk,bhtsk->bhts', qc, kc, jnp.exp(rel))
        out = jnp.einsum('bhtk,bhkv->bhtv', qc * jnp.exp(cum), st) + jnp.einsum('bhts,bhsv->bhtv', scores, vc)
        total = cum[:, :, -1:, :]
        st = jnp.exp(total[:, :, 0, :, None]) * st + jnp.einsum('bhsk,bhsv->bhkv', kc * jnp.exp(total - cum), vc)
        return st, out

    state, outs = lax.scan(step, state, tuple(_to_chunks(a) for a in (q, k, v, log_a)))
    return _from_chunks(outs), state

def _directional(scan_fn, ctx_seq, lat_seq, init, reverse):
    if reverse:
        ctx_seq = tuple(jnp.flip(a, 2) for a in ctx_seq)
        lat_seq = tuple(jnp.flip(a, 2) for a in lat_seq)
    h_ctx, state = scan_fn(*ctx_seq, init)
    h_lat, _ = scan_fn(*lat_seq, state)
    if reverse:
        h_ctx, h_lat = jnp.flip(h_ctx, 2), jnp.flip(h_lat, 2)
    return h_ctx, h_lat

def _axial_rope(s):
    rows = s // GRID_W
    row = jnp.repeat(jnp.arange(rows), GRID_W).astype(jnp.float32)
    col = jnp.tile(jnp.arange(GRID_W), rows).astype(jnp.float32)
    n_freq = DH_A // 4
    inv = ROPE_THETA_2 ** (-jnp.arange(n_freq, dtype=jnp.float32) / n_freq)
    ang = jnp.concatenate([row[:, None] * inv, col[:, None] * inv], -1)
    return jnp.cos(ang), jnp.sin(ang)

def _rope_2(x, cos, sin):
    xf = x.astype(jnp.float32)
    x1, x2 = xf[..., 0::2], xf[..., 1::2]
    c = cos[None, :, None, :]
    sn = sin[None, :, None, :]
    return jnp.stack([x1 * c - x2 * sn, x1 * sn + x2 * c], -1).reshape(x.shape).astype(x.dtype)

def _window_attention(q, k, v, k_ctx, v_ctx, sink):
    b, s = q.shape[:2]
    nb = s // WIN_BLOCK
    lc = k_ctx.shape[1]
    qb = jnp.moveaxis(q.reshape(b, nb, WIN_BLOCK, H_KV, GQA_GROUP, DH_A), 1, 0)

    def bands(a):
        ap = jnp.pad(a, ((0, 0), (WIN_BLOCK, WIN_BLOCK), (0, 0), (0, 0))).reshape(b, nb + 2, WIN_BLOCK, H_KV, DH_A)
        return jnp.moveaxis(jnp.concatenate([ap[:, :-2], ap[:, 1:-1], ap[:, 2:]], 2), 1, 0)

    kw, vw = bands(k), bands(v)
    qi = jnp.arange(WIN_BLOCK)[:, None]
    kj = jnp.arange(3 * WIN_BLOCK)[None, :]
    key_pos = jnp.arange(nb)[:, None, None] * WIN_BLOCK + kj - WIN_BLOCK
    valid = (jnp.abs(kj - WIN_BLOCK - qi) <= WINDOW) & (key_pos >= 0) & (key_pos < s)
    scale = DH_A ** -0.5
    sink_l = sink.reshape(H_KV, GQA_GROUP).astype(jnp.float32)

    def block(args):
        qn, kn, vn, mask = args
        s_ctx = jnp.einsum('bqhgd,bchd->bhgqc', qn, k_ctx).astype(jnp.float32) * scale
        s_win = jnp.einsum('bqhgd,bkhd->bhgqk', qn, kn).astype(jnp.float32) * scale
        s_win = jnp.where(mask, s_win, -jnp.inf)
        sink_col = jnp.broadcast_to(sink_l[None, :, :, None, None], s_ctx.shape[:-1] + (1,))
        p = jax.nn.softmax(jnp.concatenate([sink_col, s_ctx, s_win], -1), -1).astype(qn.dtype)
        return (jnp.einsum('bhgqc,bchd->bqhgd', p[..., 1:1 + lc], v_ctx)
                + jnp.einsum('bhgqk,bkhd->bqhgd', p[..., 1 + lc:], vn))

    out = lax.map(block, (qb, kw, vw, valid))
    return jnp.moveaxis(out, 0, 1).reshape(b, s, H_A, DH_A)

def _context_attention(q, k, v, sink):
    b, lc = q.shape[:2]
    qg = q.reshape(b, lc, H_KV, GQA_GROUP, DH_A)
    sc = jnp.einsum('bqhgd,bkhd->bhgqk', qg, k).astype(jnp.float32) * DH_A ** -0.5
    sink_col = jnp.broadcast_to(sink.reshape(H_KV, GQA_GROUP).astype(jnp.float32)[None, :, :, None, None],
                                sc.shape[:-1] + (1,))
    p = jax.nn.softmax(jnp.concatenate([sink_col, sc], -1), -1)[..., 1:].astype(q.dtype)
    return jnp.einsum('bhgqk,bkhd->bqhgd', p, v).reshape(b, lc, H_A, DH_A)

def _ab_streams(h, w_in, gate_b):
    q_m, k_m, v_m, o_m, g_m, q_a, k_a, v_a = _split(h @ w_in, AB_WIDTHS)
    b, s = h.shape[:2]
    g = g_m.reshape(b, s, 2, 2, H_M).astype(jnp.float32) + gate_b.astype(jnp.float32)
    mlstm = (_heads(q_m, H_M).astype(jnp.float32),
             _heads(k_m, H_M).astype(jnp.float32) * DH_M ** -0.5,
             _heads(v_m, H_M).astype(jnp.float32))
    gates = [(g[:, :, d, 0].transpose(0, 2, 1), jax.nn.log_sigmoid(g[:, :, d, 1]).transpose(0, 2, 1))
             for d in range(2)]
    attn = (q_a.reshape(b, s, H_A, DH_A), k_a.reshape(b, s, H_KV, DH_A), v_a.reshape(b, s, H_KV, DH_A))
    return mlstm, gates, o_m, attn

def _merge_ab(m, o, a, norm_w, w_out):
    hm = _head_norm(m, norm_w).astype(o.dtype) * jax.nn.sigmoid(o)
    cat = jnp.concatenate([hm, a.reshape(a.shape[0], a.shape[1], A_Q)], -1)
    return cat @ w_out

def _mixer_ab(hl, hc, w_in, gate_b, norm_w, sink, w_out, ctx_out):
    ml, gl, ol, (ql, kl, vl) = _ab_streams(hl, w_in, gate_b)
    mc, gc, oc, (qc, kc, vc) = _ab_streams(hc, w_in, gate_b)
    b = hl.shape[0]
    init = (jnp.zeros((b, H_M, DH_M, DH_M), jnp.float32), jnp.zeros((b, H_M, DH_M), jnp.float32),
            jnp.zeros((b, H_M), jnp.float32))
    outs = [_directional(_mlstm_scan, mc + gc[d], ml + gl[d], init, d == 1) for d in range(2)]
    cos, sin = _axial_rope(hl.shape[1])
    a_lat = _window_attention(_rope_2(ql, cos, sin), _rope_2(kl, cos, sin), vl, kc, vc, sink)
    y_lat = _merge_ab(outs[0][1] + outs[1][1], ol, a_lat, norm_w, w_out)
    if not ctx_out:
        return y_lat, None
    y_ctx = _merge_ab(outs[0][0] + outs[1][0], oc, _context_attention(qc, kc, vc, sink), norm_w, w_out)
    return y_lat, y_ctx

def _c_streams(h, w_in, gate_up, gate_b):
    q, k, v, g, low = _split(h @ w_in, C_WIDTHS)
    b, s = h.shape[:2]
    qkv = (_heads(q, H_C).astype(jnp.float32) * DK_C ** -0.5,
           _heads(k, H_C).astype(jnp.float32),
           _heads(v, H_C).astype(jnp.float32))
    low = low.reshape(b, s, 2, GATE_RANK)
    log_a = [_heads(jax.nn.log_sigmoid((low[:, :, d] @ gate_up[d] + gate_b[d]).astype(jnp.float32)) / GATE_TAU, H_C)
             for d in range(2)]
    return qkv, log_a, g

def _merge_c(h, g, norm_w, w_out):
    return (_head_norm(h, norm_w).astype(g.dtype) * jax.nn.silu(g)) @ w_out

def _mixer_c(hl, hc, w_in, gate_up, gate_b, norm_w, w_out, ctx_out):
    sl, al, gl = _c_streams(hl, w_in, gate_up, gate_b)
    sc, ac, gc = _c_streams(hc, w_in, gate_up, gate_b)
    init = jnp.zeros((hl.shape[0], H_C, DK_C, DV_C), jnp.float32)
    outs = [_directional(_gla_scan, sc + (ac[d],), sl + (al[d],), init, d == 1) for d in range(2)]
    y_lat = _merge_c(outs[0][1] + outs[1][1], gl, norm_w, w_out)
    if not ctx_out:
        return y_lat, None
    return y_lat, _merge_c(outs[0][0] + outs[1][0], gc, norm_w, w_out)

def _peer(h, wq, keys, u, v):
    shape = h.shape
    tokens = h.reshape(-1, PEER_CHUNK, shape[-1])

    def block(hb):
        tc = hb.shape[0]
        q = (hb @ wq).reshape(tc, PEER_HEADS, 2, PEER_HALF)
        s = jnp.einsum('thpk,hpnk->thpn', q, keys)
        s_top, i_top = lax.top_k(s, PEER_TOPK)
        cand = s_top[:, :, 0, :, None] + s_top[:, :, 1, None, :]
        cid = i_top[:, :, 0, :, None] * N_KEYS + i_top[:, :, 1, None, :]
        best, pos = lax.top_k(cand.reshape(tc, PEER_HEADS, -1), PEER_TOPK)
        eid = jnp.take_along_axis(cid.reshape(tc, PEER_HEADS, -1), pos, -1)
        g = jax.nn.softmax(best.astype(jnp.float32), -1).astype(hb.dtype)
        act = jax.nn.gelu(jnp.einsum('td,thed->the', hb, u[eid]), approximate=False)
        return jnp.einsum('the,thed->td', g * act, v[eid])

    return lax.map(block, tokens).reshape(shape)

def second_inputs(seed: int = 0) -> dict:
    key = jax.random.key(seed)
    ks = jax.random.split(key, 26)
    f32 = jnp.float32

    def nrm(k, shape, s):
        return jax.random.normal(k, shape, f32) * s

    d = D_MODEL
    f_bias = 3.0 + 3.0 * jnp.arange(H_M, dtype=f32) / (H_M - 1)
    gate_offset = jnp.stack([jnp.zeros((H_M,), f32), f_bias])[None, None]
    return {
        "x": nrm(ks[0], (BATCH, SEQ, d), 1.0),
        "c": nrm(ks[1], (BATCH, d), 1.0),
        "ctx": nrm(ks[2], (BATCH, CTX_LEN, d), 1.0),
        "c_ctx": nrm(ks[3], (d,), 1.0),
        "w_mod": nrm(ks[4], (DEPTH, d, 6 * d), 0.5 * d ** -0.5),
        "b_mod": nrm(ks[5], (DEPTH, 6 * d), 0.02),
        "ln_w": 1.0 + nrm(ks[6], (DEPTH, 2, d), 0.02),
        "ln_b": nrm(ks[7], (DEPTH, 2, d), 0.02),
        "ab_w_in": nrm(ks[8], (N_EVEN_2, d, sum(AB_WIDTHS)), d ** -0.5),
        "ab_gate_b": nrm(ks[9], (N_EVEN_2, 2, 2, H_M), 0.1) + gate_offset,
        "ab_norm_w": 1.0 + nrm(ks[10], (N_EVEN_2, M_W), 0.02),
        "ab_sink": nrm(ks[11], (N_EVEN_2, H_A), 0.5),
        "ab_w_out": nrm(ks[12], (N_EVEN_2, MIX_W, d), DEEPNORM_BETA * MIX_W ** -0.5),
        "gla_w_in": nrm(ks[13], (N_ODD_2, d, sum(C_WIDTHS)), d ** -0.5),
        "gla_gate_up": nrm(ks[14], (N_ODD_2, 2, GATE_RANK, C_K), GATE_RANK ** -0.5),
        "gla_gate_b": 1.0 + nrm(ks[15], (N_ODD_2, 2, C_K), 0.5),
        "gla_norm_w": 1.0 + nrm(ks[16], (N_ODD_2, C_V), 0.02),
        "gla_w_out": nrm(ks[17], (N_ODD_2, C_V, d), DEEPNORM_BETA * C_V ** -0.5),
        "peer_wq": nrm(ks[18], (DEPTH, d, PEER_HEADS * PEER_KEY_DIM), d ** -0.5),
        "peer_keys": nrm(ks[19], (DEPTH, PEER_HEADS, 2, N_KEYS, PEER_HALF), PEER_HALF ** -0.5),
        "peer_u": nrm(ks[20], (DEPTH, N_EXPERTS, d), d ** -0.5),
        "peer_v": nrm(ks[21], (DEPTH, N_EXPERTS, d), DEEPNORM_BETA * (PEER_HEADS * PEER_TOPK) ** -0.5),
    }

def second_block(x, c, ctx, c_ctx, w_mod, b_mod, ln_w, ln_b, ab_w_in, ab_gate_b, ab_norm_w, ab_sink, ab_w_out,
              gla_w_in, gla_gate_up, gla_gate_b, gla_norm_w, gla_w_out, peer_wq, peer_keys, peer_u, peer_v):
    for layer in range(DEPTH):
        last = layer == DEPTH - 1
        j = layer // 2
        mod_l = jax.nn.silu(c) @ w_mod[layer] + b_mod[layer]
        mod_c = jax.nn.silu(c_ctx) @ w_mod[layer] + b_mod[layer]
        sh1, sc1, g1, sh2, sc2, g2 = jnp.split(mod_l[:, None, :], 6, axis=-1)
        csh1, csc1, cg1, csh2, csc2, cg2 = jnp.split(mod_c, 6)
        hl = x * (1.0 + sc1) + sh1
        hc = ctx * (1.0 + csc1) + csh1
        if layer % 2 == 0:
            y_lat, y_ctx = _mixer_ab(hl, hc, ab_w_in[j], ab_gate_b[j], ab_norm_w[j], ab_sink[j], ab_w_out[j], not last)
        else:
            y_lat, y_ctx = _mixer_c(hl, hc, gla_w_in[j], gla_gate_up[j], gla_gate_b[j], gla_norm_w[j], gla_w_out[j],
                                    not last)
        x = _layernorm(DEEPNORM_ALPHA * x + g1 * y_lat, ln_w[layer, 0], ln_b[layer, 0])
        f_lat = _peer(x * (1.0 + sc2) + sh2, peer_wq[layer], peer_keys[layer], peer_u[layer], peer_v[layer])
        x = _layernorm(DEEPNORM_ALPHA * x + g2 * f_lat, ln_w[layer, 1], ln_b[layer, 1])
        if not last:
            ctx = _layernorm(DEEPNORM_ALPHA * ctx + cg1 * y_ctx, ln_w[layer, 0], ln_b[layer, 0])
            f_ctx = _peer(ctx * (1.0 + csc2) + csh2, peer_wq[layer], peer_keys[layer], peer_u[layer], peer_v[layer])
            ctx = _layernorm(DEEPNORM_ALPHA * ctx + cg2 * f_ctx, ln_w[layer, 1], ln_b[layer, 1])
    return x


def setup_inputs(seed=0):
    out = dict(first_inputs(seed))
    for name, value in second_inputs(seed + 1).items():
        if name != "x":
            out[name + "_2"] = value
    return out


def reference(
    x, c, positions, ada_w, ada_b, ln_g, ln_b, ab_w_in, ab_w_out, hgrn_lb_raw, hgrn_norm_g,
    attn_sinks, pool_w, pool_scale, ffn_w_up, ffn_conv_w, ffn_conv_b, ffn_w_down, c_2, ctx_2,
    c_ctx_2, w_mod_2, b_mod_2, ln_w_2, ln_b_2, ab_w_in_2, ab_gate_b_2, ab_norm_w_2, ab_sink_2,
    ab_w_out_2, gla_w_in_2, gla_gate_up_2, gla_gate_b_2, gla_norm_w_2, gla_w_out_2, peer_wq_2,
    peer_keys_2, peer_u_2, peer_v_2,
):
    x = first_block(
        x, c, positions, ada_w, ada_b, ln_g, ln_b, ab_w_in, ab_w_out, hgrn_lb_raw, hgrn_norm_g,
        attn_sinks, pool_w, pool_scale, ffn_w_up, ffn_conv_w, ffn_conv_b, ffn_w_down,
    )
    return second_block(
        x, c_2, ctx_2, c_ctx_2, w_mod_2, b_mod_2, ln_w_2, ln_b_2, ab_w_in_2, ab_gate_b_2,
        ab_norm_w_2, ab_sink_2, ab_w_out_2, gla_w_in_2, gla_gate_up_2, gla_gate_b_2,
        gla_norm_w_2, gla_w_out_2, peer_wq_2, peer_keys_2, peer_u_2, peer_v_2,
    )


_drawn_inputs = setup_inputs


def setup_inputs(seed=0):
    import zlib

    import numpy as np

    out = dict(_drawn_inputs(seed))
    spreads = {}
    factors = {'ada_b': 2.78,
     'hgrn_norm_g': 8.0,
     'attn_sinks': 8.0,
     'pool_scale': 8.0,
     'ffn_conv_b': 8.0,
     'b_mod_2': 6.262,
     'ab_norm_w_2': 8.0,
     'ab_sink_2': 8.0,
     'gla_gate_up_2': 3.499,
     'gla_gate_b_2': 2.741,
     'gla_norm_w_2': 8.0,
     'peer_wq_2': 7.605,
     'peer_keys_2': 7.685,
     'peer_u_2': 8.0,
     'peer_v_2': 7.586}
    for name, (base, spread) in spreads.items():
        noise = np.random.default_rng([zlib.crc32(name.encode()), seed]).standard_normal(out[name].shape)
        drawn = base * np.exp(spread * noise) if base else spread * noise
        out[name] = __import__('jax').numpy.asarray(drawn.astype(out[name].dtype))
    for name, factor in factors.items():
        out[name] = (out[name] * factor).astype(out[name].dtype)
    return out
```

```python
from contextlib import ExitStack

import numpy as np

import concourse.bass as bass
from concourse import mybir
from concourse.alu_op_type import AluOpType as ALU

ACT = mybir.ActivationFunctionType
AX = mybir.AxisListType
F32 = mybir.dt.float32
I32 = mybir.dt.int32
U32 = mybir.dt.uint32

P = 128
D = 1024
KD = D // P
T = 256
NT = T // P
H = 4
D_FF = 2816
KF = D_FF // P
LEVELS = 7
A_HEADS, A_DIM, GQA = 8, 64, 4
N_KEYS, PEER_H, TOPK = 128, 8, 16
POOL_WINDOWS = (2, 4, 8, 16)
ALPHA = float((2.0 * 2) ** 0.25)
LN_EPS, RMS_EPS = 1e-5, 1e-6
LN_MIN = 2.0 ** -64
MASKED = -1e30
EVEN_PI_1, EVEN_PI_2 = 6.28125, 0.001934051513671875
EVEN_PI_3 = 2 * np.pi - EVEN_PI_1 - EVEN_PI_2
ROUND = 12582912.0


class Stage:

    def __init__(self, nc, name):
        self.nc, self.name, self.ctx, self.sems = nc, name, ExitStack(), []

    def __enter__(self):
        return self

    def __exit__(self, *_):
        self.nc.clear_and_free_semaphores(self.sems)
        self.nc.all_engine_barrier()
        self.ctx.close()

    def sb(self, name, shape, dt=F32):
        return self.ctx.enter_context(self.nc.sbuf_tensor(f"{self.name}_{name}", shape, dt))[:]

    def ps(self, name, shape):
        return self.ctx.enter_context(self.nc.psum_tensor(f"{self.name}_{name}", shape, F32))[:]

    def sem(self, name):
        s = self.nc.alloc_semaphore(f"{self.name}_{name}")
        self.sems.append(s)
        return s


class Steps:

    def __init__(self, eng, sem):
        self.eng, self.sem, self.n = eng, sem, 0

    def done(self, ins):
        ins.then_inc(self.sem, 1)
        self.n = self.n + 1

    def wait(self):
        self.eng.wait_ge(self.sem, self.n)

    def link(self, ins):
        self.done(ins)
        self.wait()


def each_chunk(eng, first, count, ring, body):
    turns = count // ring
    if turns >= 2:
        with eng.Fori(0, turns) as i:
            for r in range(ring):
                body(first + r + i * ring, (first + r) % ring, (first + r) // ring + i)
    else:
        turns = 0
    for m in range(first + turns * ring, first + count):
        body(m, m % ring, m // ring)


def bcast(ap, n):
    return ap.unsqueeze(2).broadcast_to([ap.shape[0], ap.shape[1], n])


def over(ap, n):
    return ap.unsqueeze(1).broadcast_to([ap.shape[0], n, ap.shape[1]])


def load(nc, name, pairs):
    with Stage(nc, name) as st:
        s_loaded = st.sem("loaded")
        with nc.Block() as block:
            @block.sync
            def _(sp):
                for dst, src in pairs:
                    sp.dma_start(dst, src).then_inc(s_loaded, 16)
                sp.wait_ge(s_loaded, 16 * len(pairs))


def project(nc, name, weights, kc, rhs, t, segments, ring=4):
    with Stage(nc, name) as st:
        total = sum(n for n, _, _ in segments)
        banks = min(4, ring)
        wt = st.sb("weights", [P, ring, kc * P])
        acc = st.ps("acc", [P, 4, 512])
        s_loaded = [st.sem(f"loaded{r}") for r in range(ring)]
        s_summed = st.sem("summed")
        s_taken = st.sem("taken")

        with nc.Block() as block:
            @block.sync
            def _(sp):
                def fetch(m, slot):
                    src = weights[m] if isinstance(m, int) else weights[bass.ds(m, 1)].rearrange("a p c -> p (a c)")
                    sp.dma_start(wt[:, slot, :], src).then_inc(s_loaded[slot], 16)

                for m in range(min(ring, total)):
                    fetch(m, m)
                if total > ring:
                    def body(m, slot, turn):
                        sp.wait_ge(s_summed, m - (ring - 1))
                        fetch(m, slot)
                    each_chunk(sp, ring, total - ring, ring, body)

            @block.tensor
            def _(pe):
                def body(m, slot, turn):
                    pe.wait_ge(s_loaded[slot], (turn + 1) * 16)
                    pe.wait_ge(s_taken, m + 1)
                    bank = slot % banks
                    for k in range(kc):
                        ins = nc.tensor.matmul(acc[:, bank, 0:t], wt[:, slot, k * P:(k + 1) * P], rhs[:, k, :],
                                               start=(k == 0), stop=(k == kc - 1))
                    ins.then_inc(s_summed, 1)
                each_chunk(pe, 0, total, ring, body)

            def takes(eng, kind):
                if kind == "scalar":
                    eng.sem_inc(s_taken, banks)
                first = 0
                for n, who, evacuate in segments:
                    if who == kind:
                        def body(m, slot, turn):
                            eng.wait_ge(s_summed, m + 1)
                            evacuate(m, m - first, acc[:, slot % banks, 0:t]).then_inc(s_taken, 1)
                        each_chunk(eng, first, n, ring, body)
                    first += n

            @block.scalar
            def _(act):
                takes(act, "scalar")

            @block.vector
            def _(dve):
                takes(dve, "vector")


def copy_to(nc, dst):
    def evacuate(m, index, psum):
        return nc.scalar.activation(dst[:, bass.ds(index, 1), :], psum.unsqueeze(1), ACT.Copy)
    return evacuate


def add_residual(nc, z, gate, scaled):
    def evacuate(m, index, psum):
        for n in range(gate.shape[2]):
            half = slice(n * T, (n + 1) * T)
            ins = nc.vector.scalar_tensor_tensor(
                z[:, bass.ds(index, 1), half], psum[:, half].unsqueeze(1), gate[:, bass.ds(index, 1), n],
                scaled[:, bass.ds(index, 1), half], ALU.mult, ALU.add)
        return ins
    return evacuate


def token_major(nc, name, weights, n, xt, t, dst):
    with Stage(nc, name) as st:
        tiles = t // P
        groups = [(a, min(a + 512, n)) for a in range(0, n, 512)]
        wt = st.sb("weights", [P, 4, n])
        acc = st.ps("acc", [P, tiles * len(groups), 512])
        s_loaded = [st.sem(f"loaded{r}") for r in range(4)]
        s_used, s_copied = st.sem("used"), st.sem("copied")
        with nc.Block() as block:
            @block.sync
            def _(sp):
                for k in range(KD):
                    if k >= 4:
                        sp.wait_ge(s_used, k - 3)
                    sp.dma_start(wt[:, k % 4, :], weights[k]).then_inc(s_loaded[k % 4], 16)

            @block.tensor
            def _(pe):
                for k in range(KD):
                    pe.wait_ge(s_loaded[k % 4], 16 * (k // 4 + 1))
                    for i in range(tiles):
                        for g, (a, b) in enumerate(groups):
                            ins = nc.tensor.matmul(acc[:, i * len(groups) + g, 0:b - a], xt[:, k, i * P:(i + 1) * P],
                                                   wt[:, k % 4, a:b], start=(k == 0), stop=(k == KD - 1))
                    ins.then_inc(s_used, 1)

            @block.scalar
            def _(act):
                act.wait_ge(s_used, KD)
                for i in range(tiles):
                    for g, (a, b) in enumerate(groups):
                        nc.scalar.activation(dst[:, i, a:b], acc[:, i * len(groups) + g, 0:b - a],
                                             ACT.Copy).then_inc(s_copied, 1)


def modulate(nc, name, h, x, mods, shift, halves, scale_x):
    with Stage(nc, name) as st:
        s_act, s_dve = st.sem("act"), st.sem("dve")
        n = len(halves)
        with nc.Block() as block:
            @block.scalar
            def _(act):
                for k in range(0, KD, 2):
                    for i, c in enumerate(halves):
                        half = slice(i * T, (i + 1) * T)
                        nc.scalar.activation(h[:, k, half], x[:, k, half], ACT.Identity,
                                             bias=mods[:, shift + k, c:c + 1],
                                             scale=mods[:, shift + KD + k, c:c + 1]).then_inc(s_act, 1)

            @block.vector
            def _(dve):
                for k in range(1, KD, 2):
                    for i, c in enumerate(halves):
                        half = slice(i * T, (i + 1) * T)
                        nc.vector.tensor_scalar(h[:, k, half], x[:, k, half], mods[:, shift + KD + k, c:c + 1],
                                                mods[:, shift + k, c:c + 1], ALU.mult, ALU.add).then_inc(s_dve, 1)
                if scale_x:
                    dve.wait_ge(s_act, KD // 2 * n)
                    dve.wait_ge(s_dve, KD // 2 * n)
                    nc.vector.tensor_scalar(x[:], x[:], ALPHA, None, ALU.mult).then_inc(s_dve, 1)


def layer_norm(nc, name, x, z, sq, t, gain, bias, mean_of_d):
    with Stage(nc, name) as st:
        ps_mean, ps_var = st.ps("mean", [P, 512]), st.ps("var", [P, 512])
        rstd = st.sb("rstd", [P, t])
        s_mean, s_var, s_centred, s_squared = st.sem("mean"), st.sem("var"), st.sem("centred"), st.sem("squared")
        s_step, s_root, s_scaled = st.sem("step"), st.sem("root"), st.sem("scaled")
        with nc.Block() as block:
            @block.tensor
            def _(pe):
                for k in range(KD):
                    ins = nc.tensor.matmul(ps_mean[:, 0:t], mean_of_d, z[:, k, :], start=(k == 0), stop=(k == KD - 1))
                ins.then_inc(s_mean, 1)
                for k in range(KD):
                    pe.wait_ge(s_squared, k + 1)
                    ins = nc.tensor.matmul(ps_var[:, 0:t], mean_of_d, sq[:, k, :], start=(k == 0), stop=(k == KD - 1))
                ins.then_inc(s_var, 1)

            @block.vector
            def _(dve):
                step = Steps(dve, s_step)
                dve.wait_ge(s_mean, 1)
                for k in range(KD):
                    nc.vector.tensor_tensor(z[:, k, :], z[:, k, :], ps_mean[:, 0:t], ALU.subtract).then_inc(s_centred, 1)
                dve.wait_ge(s_var, 1)
                step.link(nc.vector.tensor_scalar(rstd[:], ps_var[:, 0:t], LN_EPS, None, ALU.add))
                step.link(nc.vector.reciprocal(rstd[:], rstd[:]))
                dve.wait_ge(s_root, 1)
                for k in range(KD):
                    nc.vector.tensor_tensor(z[:, k, :], z[:, k, :], rstd[:], ALU.mult).then_inc(s_scaled, 1)

            @block.scalar
            def _(act):
                for k in range(KD):
                    act.wait_ge(s_centred, k + 1)
                    nc.scalar.activation(sq[:, k, :], z[:, k, :], ACT.Square).then_inc(s_squared, 1)
                act.wait_ge(s_step, 2)
                nc.scalar.activation(rstd[:], rstd[:], ACT.Sqrt).then_inc(s_root, 1)
                for k in range(KD):
                    act.wait_ge(s_scaled, k + 1)
                    nc.scalar.activation(x[:, k, :], z[:, k, :], ACT.Identity, bias=bias[:, k:k + 1],
                                         scale=gain[:, k:k + 1])


def modulation(nc, name, c, weights, bias, mods, bias_sb):
    n = c.shape[2]
    with Stage(nc, name + "_silu") as st:
        s_silu = st.sem("silu")
        act_c = st.sb("act_c", [P, KD, n])
        with nc.Block() as block:
            @block.scalar
            def _(act):
                nc.scalar.activation(act_c[:], c, ACT.Silu).then_inc(s_silu, 1)
        project(nc, name, weights, KD, act_c, n, [(6 * KD, "scalar", copy_to(nc, mods))], ring=8)
        s_b = st.sem("bias")
        with nc.Block() as block:
            @block.vector
            def _(dve):
                nc.vector.tensor_tensor(mods[:], mods[:], bcast(bias_sb, n), ALU.add).then_inc(s_b, 1)
                dve.wait_ge(s_b, 1)
                for first in (KD, 4 * KD):
                    nc.vector.tensor_scalar(mods[:, first:first + KD, :], mods[:, first:first + KD, :], 1.0, None, ALU.add)


def conv_ffn(nc, name, h, w_up, conv, w_down, z, gate, scaled):
    ring = 4
    with Stage(nc, name) as st:
        hidden = st.sb("hidden", [P, KF, T])
        with Stage(nc, name + "_up") as up:
            wt = up.sb("weights", [P, ring, KD * P])
            acc = up.ps("acc", [P, 4, 512])
            ubuf = up.sb("u", [P, 2, T + 2])
            cbuf, sbuf = up.sb("c", [P, 2, T]), up.sb("s", [P, 2, T])
            s_loaded = [up.sem(f"loaded{r}") for r in range(ring)]
            s_summed, s_taken, s_zero = up.sem("summed"), up.sem("taken"), up.sem("zero")
            s_u, s_tap, s_silu, s_hidden = up.sem("u"), up.sem("tap"), up.sem("silu"), up.sem("hidden")
            with nc.Block() as block:
                @block.sync
                def _(sp):
                    def fetch(m, slot):
                        src = w_up[m] if isinstance(m, int) else w_up[bass.ds(m, 1)].rearrange("a p c -> p (a c)")
                        sp.dma_start(wt[:, slot, :], src).then_inc(s_loaded[slot], 16)
                    for m in range(ring):
                        fetch(m, m)

                    def body(m, slot, turn):
                        sp.wait_ge(s_summed, m - (ring - 1))
                        fetch(m, slot)
                    each_chunk(sp, ring, 2 * KF - ring, ring, body)

                @block.tensor
                def _(pe):
                    def body(m, slot, turn):
                        pe.wait_ge(s_loaded[slot], (turn + 1) * 16)
                        pe.wait_ge(s_taken, m + 1)
                        for k in range(KD):
                            ins = nc.tensor.matmul(acc[:, slot, 0:T], wt[:, slot, k * P:(k + 1) * P], h[:, k, :],
                                                   start=(k == 0), stop=(k == KD - 1))
                        ins.then_inc(s_summed, 1)
                    each_chunk(pe, 0, 2 * KF, ring, body)

                @block.scalar
                def _(act):
                    act.sem_inc(s_taken, 4)
                    act.wait_ge(s_zero, 1)

                    def body(f, b, turn):
                        act.wait_ge(s_summed, f * 2 + 1)
                        act.wait_ge(s_tap, f * 3 + 3)
                        nc.scalar.activation(ubuf[:, b, 2:2 + T], acc[:, 2 * b, 0:T], ACT.Copy).then_inc(s_u, 1)
                        act.wait_ge(s_u, f + 1)
                        act.sem_inc(s_taken, 1)
                        act.wait_ge(s_tap, f * 3 + 9)
                        nc.scalar.activation(sbuf[:, b, :], cbuf[:, b, :], ACT.Silu).then_inc(s_silu, 1)
                        act.wait_ge(s_hidden, f + 1)
                        act.sem_inc(s_taken, 1)
                    each_chunk(act, 0, KF, 2, body)

                @block.vector
                def _(dve):
                    nc.vector.memset(ubuf[:], 0.0).then_inc(s_zero, 1)
                    dve.sem_inc(s_tap, 6)

                    def body(f, b, turn):
                        dve.wait_ge(s_u, f + 1)
                        nc.vector.tensor_scalar(cbuf[:, b, :], ubuf[:, b, 0:T], conv[:, bass.ds(f, 1), 0],
                                                conv[:, bass.ds(f, 1), 3], ALU.mult, ALU.add).then_inc(s_tap, 1)
                        for j in (1, 2):
                            dve.wait_ge(s_tap, f * 3 + 6 + j)
                            nc.vector.scalar_tensor_tensor(cbuf[:, b, :], ubuf[:, b, j:j + T], conv[:, bass.ds(f, 1), j],
                                                           cbuf[:, b, :], ALU.mult, ALU.add).then_inc(s_tap, 1)
                        dve.wait_ge(s_silu, f + 1)
                        dve.wait_ge(s_summed, f * 2 + 2)
                        nc.vector.tensor_tensor(hidden[:, bass.ds(f, 1), :], sbuf[:, b:b + 1, :],
                                                acc[:, 2 * b + 1:2 * b + 2, 0:T], ALU.mult).then_inc(s_hidden, 1)
                    each_chunk(dve, 0, KF, 2, body)
        project(nc, name + "_down", w_down, KF, hidden, T, [(KD, "vector", add_residual(nc, z, gate, scaled))], ring=2)


def decayed_scores(nc, name, q, k, directions, masks, at, off, ctx=None):
    with Stage(nc, name) as st:
        nd, last = len(directions), LEVELS + 1 + (ctx is not None)
        qd, kd = st.sb("qd", [P, 2, H, T]), st.sb("kd", [P, 2, H, T])
        near, far, exp_near, exp_far = (st.sb(n, [P, H, T]) for n in ("near", "far", "exp_near", "exp_far"))
        zeros = st.sb("zeros", [P, T])
        acc = st.ps("acc", [P, 2, H * NT, P])
        ctx_acc = st.ps("ctx_acc", [P, 2, H, T]) if ctx else None
        s_init, s_ready, s_scored, s_kept, s_exp, s_grown = (
            st.sem(n) for n in ("init", "ready", "scored", "kept", "exp", "grown"))
        plan = [(0, 0)] + [(d, level) for d in range(nd) for level in range(1, last + 1)]
        grown = lambda d, level: 2 * (d * last + level)
        kept = lambda n: sum(level <= LEVELS + 1 for _, level in plan[:n + 1])

        def halves(ap, size):
            return ap.rearrange("p h (b c s) -> p (h b) c s", c=2, s=size)

        def sides(d):
            return (0, 1) if directions[d][1] else (1, 0)

        with nc.Block() as block:
            @block.vector
            def _(dve):
                init = Steps(dve, s_init)
                init.done(nc.vector.memset(at, 0.0))
                init.done(nc.vector.memset(zeros[:], 0.0))
                init.done(nc.vector.memset(qd[:, 1], 0.0))
                init.link(nc.vector.memset(kd[:, 1], 0.0))
                nc.vector.tensor_scalar(qd[:, 0], q, float(nd), None, ALU.mult).then_inc(s_ready, 1)
                nc.vector.tensor_copy(kd[:, 0], k).then_inc(s_ready, 1)

                def keep(n):
                    d, level = plan[n]
                    if level > LEVELS + 1:
                        return
                    dve.wait_ge(s_scored, n + 1)
                    if level == LEVELS + 1:
                        ins = nc.vector.tensor_copy(off[d], acc[:, n % 2, 0:H, :])
                    else:
                        if n >= 1:
                            dve.wait_ge(s_kept, kept(n - 1))
                        ins = nc.vector.copy_predicated(at, over(masks[d][:, level, :], H * NT), acc[:, n % 2])
                    ins.then_inc(s_kept, 1)

                for n, (d, level) in enumerate(plan):
                    if n == 0:
                        continue
                    g, backwards = directions[d]
                    tc, sc = sides(d)
                    if level == 1:
                        nc.vector.tensor_copy(near[:], g).then_inc(s_grown, 1)
                        nc.vector.memset(far[:], 0.0).then_inc(s_grown, 1)
                        dve.wait_ge(s_grown, grown(d, 1))
                    b, size = n % 2, 2 ** (level - 1)
                    dve.wait_ge(s_exp, 2 * n)
                    if n >= 2:
                        dve.wait_ge(s_scored, n - 1)
                        dve.wait_ge(s_ready, 2 * n)
                    if level <= LEVELS + 1:
                        nc.vector.tensor_tensor(halves(qd[:, b], size)[:, :, tc], halves(q, size)[:, :, tc],
                                                halves(exp_near[:], size)[:, :, tc], ALU.mult).then_inc(s_ready, 1)
                        nc.vector.tensor_tensor(halves(kd[:, b], size)[:, :, sc], halves(k, size)[:, :, sc],
                                                halves(exp_far[:], size)[:, :, sc], ALU.mult).then_inc(s_ready, 1)
                    else:
                        nc.vector.tensor_tensor(qd[:, b], q, exp_near[:], ALU.mult).then_inc(s_ready, 1)
                        nc.vector.tensor_tensor(kd[:, b], ctx[0], exp_far[:], ALU.mult).then_inc(s_ready, 1)
                    if level < last:
                        near_h, far_h = halves(near[:], size), halves(far[:], size)
                        edge = 0 if backwards else size - 1
                        blocks = H * T // (2 * size)
                        total = lambda c: near_h[:, :, c, edge:edge + 1].broadcast_to([P, blocks, size])
                        if level <= LEVELS:
                            nc.vector.tensor_tensor(far_h[:, :, sc], far_h[:, :, sc], total(tc),
                                                    ALU.add).then_inc(s_grown, 1)
                        else:
                            cg = ctx[1][d]
                            init.link(nc.vector.memset(far[:], 0.0))
                            for h in range(H):
                                out, src = ((far[:, h, 1:T], cg[:, h, 0:T - 1]) if backwards else
                                            (far[:, h, T - 2::-1], cg[:, h, T - 1:0:-1]))
                                ins = nc.vector.tensor_tensor_scan(out, zeros[:, 0:T - 1], src, 0.0, ALU.add, ALU.add)
                            ins.then_inc(s_grown, 1)
                        dve.wait_ge(s_grown, grown(d, level) + 1)
                        nc.vector.tensor_tensor(near_h[:, :, tc], near_h[:, :, tc], total(sc),
                                                ALU.add).then_inc(s_grown, 1)
                        dve.wait_ge(s_grown, grown(d, level + 1))
                    keep(n - 1)
                keep(len(plan) - 1)

            @block.scalar
            def _(act):
                for n, (d, level) in enumerate(plan):
                    if n == 0:
                        continue
                    tc, sc = sides(d)
                    act.wait_ge(s_grown, grown(d, level))
                    act.wait_ge(s_ready, 2 * n)
                    if level <= LEVELS + 1:
                        size = 2 ** (level - 1)
                        pairs = [(halves(a[:], size)[:, :, c], halves(b[:], size)[:, :, c])
                                 for a, b, c in ((exp_near, near, tc), (exp_far, far, sc))]
                    else:
                        pairs = [(exp_near[:], near[:]), (exp_far[:], far[:])]
                    for out, src in pairs:
                        nc.scalar.activation(out, src, ACT.Exp).then_inc(s_exp, 1)
                if ctx:
                    act.wait_ge(s_scored, len(plan))
                    for i in range(2):
                        nc.scalar.activation(ctx[2][:, i], ctx_acc[:, i], ACT.Copy)

            @block.tensor
            def _(pe):
                for n, (d, level) in enumerate(plan):
                    b = n % 2
                    pe.wait_ge(s_ready, 2 * n + 2)
                    if n >= 2:
                        pe.wait_ge(s_kept, kept(n - 2))
                    for h in range(H):
                        if level <= LEVELS:
                            for i in range(NT):
                                tile = slice(i * P, (i + 1) * P)
                                ins = nc.tensor.matmul(acc[:, b, h * NT + i, :], kd[:, b, h, tile], qd[:, b, h, tile],
                                                       start=True, stop=True)
                        elif level == LEVELS + 1:
                            tc, sc = sides(d)
                            ins = nc.tensor.matmul(acc[:, b, h, :], kd[:, b, h, sc * P:(sc + 1) * P],
                                                   qd[:, b, h, tc * P:(tc + 1) * P], start=True, stop=True)
                        else:
                            for i in range(2):
                                ins = nc.tensor.matmul(ctx_acc[:, i, h, :], kd[:, b, h, i * P:(i + 1) * P], qd[:, b, h, :],
                                                       start=(d == 0 and h % 2 == 0), stop=(d == nd - 1),
                                                       skip_group_check=True)
                    ins.then_inc(s_scored, 1)


def weighted_values(nc, name, v, width, at, off, out, ctx=None):
    with Stage(nc, name) as st:
        chunks = H * width // P
        acc = st.ps("acc", [P, chunks, T])
        s_summed = st.sem("summed")
        with nc.Block() as block:
            @block.tensor
            def _(pe):
                for c in range(chunks):
                    h, cols = c * P // width, slice(c * P, (c + 1) * P)
                    for i in range(NT):
                        tile = slice(i * P, (i + 1) * P)
                        terms = [(v[i], at[:, h * NT + i, :])]
                        if i == 1:
                            terms.append((v[0], off[0][:, h, :]))
                        elif len(off) > 1:
                            terms.append((v[1], off[1][:, h, :]))
                        if ctx:
                            terms += [(ctx[0][j], ctx[1][:, j, h, tile]) for j in range(2)]
                        for n, (value, score) in enumerate(terms):
                            ins = nc.tensor.matmul(acc[:, c, tile], value[:, cols], score,
                                                   start=(n == 0), stop=(n == len(terms) - 1))
                    ins.then_inc(s_summed, 1)

            @block.scalar
            def _(act):
                for c in range(chunks):
                    act.wait_ge(s_summed, c // 2 * 2 + 2)
                    nc.scalar.activation(out[:, c, :], acc[:, c, :], ACT.Copy)


def head_norm(nc, name, o, y, gate, weight, per_head, t, eps, mean_of_p):
    with Stage(nc, name) as st:
        chunks = o.shape[1]
        heads = chunks // per_head
        in_bank = 512 // t
        sq, rstd = st.sb("sq", [P, 2, t]), st.sb("rstd", [P, heads, t])
        acc = st.ps("acc", [P, heads, t])
        s_squared, s_mean, s_step, s_root, s_weighted = (st.sem(n) for n in ("squared", "mean", "step", "root", "weighted"))
        with nc.Block() as block:
            @block.scalar
            def _(act):
                for c in range(chunks):
                    if c >= 2:
                        act.wait_ge(s_mean, c - 1)
                    nc.scalar.activation(sq[:, c % 2, :], o[:, c, :], ACT.Square).then_inc(s_squared, 1)
                act.wait_ge(s_step, 2 * heads)
                nc.scalar.activation(rstd[:], rstd[:], ACT.Sqrt).then_inc(s_root, 1)

            @block.tensor
            def _(pe):
                for c in range(chunks):
                    pe.wait_ge(s_squared, c + 1)
                    nc.tensor.matmul(acc[:, c // per_head, :], mean_of_p, sq[:, c % 2, :], start=(c % per_head == 0),
                                     stop=(c % per_head == per_head - 1)).then_inc(s_mean, 1)

            @block.vector
            def _(dve):
                step = Steps(dve, s_step)
                for h in range(heads):
                    dve.wait_ge(s_mean, (h // in_bank + 1) * in_bank * per_head)
                    step.link(nc.vector.tensor_scalar(rstd[:, h, :], acc[:, h, :], 1.0 / per_head, eps, ALU.mult, ALU.add))
                    step.done(nc.vector.reciprocal(rstd[:, h, :], rstd[:, h, :]))
                for c in range(chunks):
                    nc.vector.scalar_tensor_tensor(y[:, c, :], o[:, c, :], weight(c), gate[:, c, :],
                                                   ALU.mult, ALU.mult).then_inc(s_weighted, 1)
                dve.wait_ge(s_root, 1)
                for c in range(chunks):
                    dve.wait_ge(s_weighted, c + 1)
                    nc.vector.tensor_tensor(y[:, c, :], y[:, c, :], rstd[:, c // per_head, :], ALU.mult)


def rope(nc, name, qk, perm_t, cos, sin):
    with Stage(nc, name) as st:
        chunks = qk.shape[1]
        acc = st.ps("acc", [P, chunks + 1, T])
        turned = st.sb("turned", [P, chunks, T])
        s_perm, s_turned, s_cos = st.sem("perm"), st.sem("turned"), st.sem("cos")
        with nc.Block() as block:
            @block.tensor
            def _(pe):
                for c in range(chunks):
                    nc.tensor.matmul(acc[:, c, :], perm_t, qk[:, c, :], start=True, stop=True).then_inc(s_perm, 1)

            @block.vector
            def _(dve):
                dve.wait_ge(s_perm, chunks)
                nc.vector.tensor_tensor(turned[:], acc[:, 0:chunks, :], over(sin, chunks), ALU.mult).then_inc(s_turned, 1)
                nc.vector.tensor_tensor(qk, qk, over(cos, chunks), ALU.mult).then_inc(s_cos, 1)
                dve.wait_ge(s_turned, 1)
                dve.wait_ge(s_cos, 1)
                nc.vector.tensor_tensor(qk, qk, turned[:], ALU.add)


def rope_tables(nc, name, positions, inv_freq, cos, sin):
    with Stage(nc, name) as st:
        pos, ang, turns, cosine = st.sb("pos", [P, T]), st.sb("ang", [P, T]), st.sb("turns", [P, T]), st.sb("cosine", [P, T])
        s_step = st.sem("step")
        with nc.Block() as block:
            @block.vector
            def _(dve):
                step = Steps(dve, s_step)
                step.link(nc.vector.tensor_copy(pos[:], positions))
                step.link(nc.vector.tensor_scalar(ang[:], pos[:], inv_freq, None, ALU.mult))
                step.link(nc.vector.tensor_scalar(turns[:], ang[:], float(0.5 / np.pi), ROUND, ALU.mult, ALU.add))
                step.link(nc.vector.tensor_scalar(turns[:], turns[:], ROUND, None, ALU.subtract))
                for part in (EVEN_PI_1, EVEN_PI_2, EVEN_PI_3):
                    step.link(nc.vector.scalar_tensor_tensor(ang[:], turns[:], -float(part), ang[:], ALU.mult, ALU.add))
                step.link(nc.vector.tensor_scalar(cosine[:], ang[:], float(np.pi / 2), None, ALU.add))
                step.link(nc.vector.tensor_scalar(turns[:], cosine[:], float(np.pi), float(-2 * np.pi), ALU.is_gt, ALU.mult))
                step.link(nc.vector.tensor_tensor(cosine[:], cosine[:], turns[:], ALU.add))
                for a in (ang, cosine):
                    step.link(nc.vector.tensor_scalar(a[:], a[:], 3.1415925, -3.1415925, ALU.min, ALU.max))

            @block.scalar
            def _(act):
                act.wait_ge(s_step, 12)
                nc.scalar.activation(sin, ang[:], ACT.Sin)
                nc.scalar.activation(cos, cosine[:], ACT.Sin)


def attention(nc, name, tiles, sinks, o, ident):
    with Stage(nc, name) as st:
        scores = st.ps("scores", [P, GQA, 512])
        turned = st.ps("turned", [P, GQA, 4, P])
        p, pt = st.sb("p", [P, GQA, 512]), st.sb("pt", [P, GQA, 4, P])
        m, sink, denom = st.sb("m", [P, GQA]), st.sb("sink", [P, GQA]), st.sb("denom", [P, GQA])
        o_tok = st.sb("o_tok", [P, A_HEADS * A_DIM])
        (s_scores, s_step, s_exp, s_p, s_turned, s_pt, s_values, s_o, s_back, s_out) = (
            st.sem(n) for n in ("scores", "step", "exp", "p", "turned", "pt", "values", "o", "back", "out"))
        items = [(i, g) for i in range(len(tiles)) for g in range(2)]

        with nc.Block() as block:
            @block.tensor
            def _(pe):
                for n, (i, g) in enumerate(items):
                    q, ks, vs, mask, cols = tiles[i]
                    rows = slice(g * A_DIM, (g + 1) * A_DIM)
                    if n >= 1:
                        pe.wait_ge(s_o, n)
                    if g == 0 and i >= 1:
                        pe.wait_ge(s_out, i)
                    for c in range(GQA):
                        at = 0
                        for kt in ks:
                            w = kt.shape[1]
                            ins = nc.tensor.matmul(scores[:, c, at:at + w], q(c)[rows], kt[rows], start=True, stop=True)
                            at += w
                    ins.then_inc(s_scores, 1)
                    pe.wait_ge(s_p, n + 1)
                    for c in range(GQA):
                        for j in range(len(vs)):
                            ins = nc.tensor.transpose(turned[:, c, j, :], p[:, c, j * P:(j + 1) * P], ident)
                    ins.then_inc(s_turned, 1)
                    pe.wait_ge(s_pt, n + 1)
                    for c in range(GQA):
                        for j, v in enumerate(vs):
                            ins = nc.tensor.matmul(scores[:, 0, c * A_DIM:(c + 1) * A_DIM], pt[:, c, j, :], v[:, g, :],
                                                   start=(j == 0), stop=(j == len(vs) - 1))
                    ins.then_inc(s_values, 1)
                    if g == 1:
                        pe.wait_ge(s_o, n + 1)
                        for c in range(GQA):
                            ins = nc.tensor.transpose(scores[:, 1, c * P:(c + 1) * P], o_tok[:, c * P:(c + 1) * P], ident)
                        ins.then_inc(s_back, 1)

            @block.vector
            def _(dve):
                step = Steps(dve, s_step)
                for n, (i, g) in enumerate(items):
                    q, ks, vs, mask, cols = tiles[i]
                    w = len(vs) * P
                    pw, sk = p[:, :, 0:w], sinks[:, g * GQA:(g + 1) * GQA]
                    dve.wait_ge(s_scores, n + 1)
                    if n >= 1:
                        dve.wait_ge(s_turned, n)
                    if mask is None:
                        step.link(nc.vector.tensor_scalar(pw, scores[:, :, 0:w], A_DIM ** -0.5, None, ALU.mult))
                    else:
                        for c in range(GQA):
                            ins = nc.vector.scalar_tensor_tensor(p[:, c, 0:w], scores[:, c, 0:w], A_DIM ** -0.5, mask,
                                                                 ALU.mult, ALU.add)
                        step.link(ins)
                    step.link(nc.vector.tensor_reduce(m[:], pw, AX.X, ALU.max))
                    step.link(nc.vector.tensor_tensor(m[:], m[:], sk, ALU.max))
                    step.done(nc.vector.tensor_tensor(sink[:], sk, m[:], ALU.subtract))
                    step.link(nc.vector.tensor_tensor(pw, pw, bcast(m[:], w), ALU.subtract))
                    dve.wait_ge(s_exp, 2 * n + 2)
                    step.link(nc.vector.tensor_reduce(denom[:], pw, AX.X, ALU.add))
                    step.link(nc.vector.tensor_tensor(denom[:], denom[:], sink[:], ALU.add))
                    step.link(nc.vector.reciprocal(denom[:], denom[:]))
                    nc.vector.tensor_tensor(pw, pw, bcast(denom[:], w), ALU.mult).then_inc(s_p, 1)

            @block.scalar
            def _(act):
                for n, (i, g) in enumerate(items):
                    q, ks, vs, mask, cols = tiles[i]
                    w = len(vs) * P
                    act.wait_ge(s_step, 8 * n + 5)
                    nc.scalar.activation(p[:, :, 0:w], p[:, :, 0:w], ACT.Exp).then_inc(s_exp, 1)
                    nc.scalar.activation(sink[:], sink[:], ACT.Exp).then_inc(s_exp, 1)
                    act.wait_ge(s_turned, n + 1)
                    if n >= 1:
                        act.wait_ge(s_values, n)
                    nc.scalar.activation(pt[:, :, 0:len(vs), :], turned[:, :, 0:len(vs), :], ACT.Copy).then_inc(s_pt, 1)
                    act.wait_ge(s_values, n + 1)
                    if g == 0 and i >= 1:
                        act.wait_ge(s_back, i)
                    nc.scalar.activation(o_tok[:, g * 256:(g + 1) * 256], scores[:, 0, 0:256], ACT.Copy).then_inc(s_o, 1)
                    if g == 1:
                        act.wait_ge(s_back, i + 1)
                        nc.scalar.activation(o[:, :, cols], scores[:, 1, :].rearrange("p (c t) -> p c t", c=GQA),
                                             ACT.Copy).then_inc(s_out, 1)


def pool_mixer(nc, name, h, w_pool, scale, inv_count, z, gate, scaled):
    with Stage(nc, name) as st:
        pad = max(POOL_WINDOWS)
        a, b = st.sb("a", [P, KD, pad + T]), st.sb("b", [P, KD, pad + T])
        w = st.sb("w", [P, KD, 2, P])
        gs = st.sb("gs", [P, KD])
        acc = st.ps("acc", [P, KD, T])
        s_loaded, s_step, s_summed = st.sem("loaded"), st.sem("step"), st.sem("summed")
        with nc.Block() as block:
            @block.sync
            def _(sp):
                sp.dma_start(w[:], w_pool).then_inc(s_loaded, 16)

            @block.vector
            def _(dve):
                step = Steps(dve, s_step)
                step.done(nc.vector.memset(a[:, :, 0:pad], 0.0))
                step.done(nc.vector.memset(b[:, :, 0:pad], 0.0))
                step.done(nc.vector.tensor_tensor(gs[:], gate[:, :, 0], scale, ALU.mult))
                step.link(nc.vector.tensor_copy(a[:, :, pad:], h))
                src, dst, size = a, b, 1
                for g, window in enumerate(POOL_WINDOWS):
                    ks = slice(2 * g, KD)
                    step.link(nc.vector.tensor_tensor(dst[:, ks, pad:], src[:, ks, pad:],
                                                      src[:, ks, pad - size:pad + T - size], ALU.add))
                    size *= 2
                    own = slice(2 * g, 2 * g + 2)
                    step.link(nc.vector.tensor_tensor(src[:, own, pad:], dst[:, own, pad:], over(inv_count[:, g, :], 2), ALU.mult))
                    step.link(nc.vector.tensor_tensor(h[:, own, :], src[:, own, pad:], h[:, own, :], ALU.subtract))
                    src, dst = dst, src
                dve.wait_ge(s_summed, 1)
                for m in range(KD):
                    nc.vector.scalar_tensor_tensor(z[:, m, :], acc[:, m, :], gs[:, m:m + 1], scaled[:, m, :],
                                                   ALU.mult, ALU.add)

            @block.tensor
            def _(pe):
                pe.wait_ge(s_loaded, 16)
                pe.wait_ge(s_step, 4 + 3 * len(POOL_WINDOWS))
                for m in range(KD):
                    for j in range(2):
                        ins = nc.tensor.matmul(acc[:, m, :], w[:, m, j, :], h[:, m // 2 * 2 + j, :], start=(j == 0), stop=(j == 1))
                ins.then_inc(s_summed, 1)


def log_sigmoid_rows(nc, name, h, w_gates, gate_b, rows, u_cols, ident):
    with Stage(nc, name) as st:
        acc = st.ps("acc", [P, 4, 512])
        cols = st.ps("cols", [P, 2, 4, H])
        gates = [[st.sb(f"gate{d}{i}", [H, 2 * T]) for i in range(2)] for d in range(2)]
        tmp = [[st.sb(f"tmp{d}{i}", [H, 2 * T]) for i in range(2)] for d in range(2)]
        u = [st.sb(f"u{d}", [H, 2 * T]) for d in range(2)]
        zeros = st.sb("zeros", [H, 2 * T])
        s_summed, s_step, s_act, s_u, s_cols = (st.sem(n) for n in ("summed", "step", "act", "u", "cols"))
        with nc.Block() as block:
            @block.tensor
            def _(pe):
                for n in range(4):
                    for k in range(KD):
                        ins = nc.tensor.matmul(acc[0:H, n, :], w_gates[:, k, n * H:(n + 1) * H], h[:, k, :],
                                               start=(k == 0), stop=(k == KD - 1))
                ins.then_inc(s_summed, 1)
                pe.wait_ge(s_u, 2)
                for d in range(2):
                    for i in range(4):
                        ins = nc.tensor.transpose(cols[:, d, i, :], u[d][:, i * P:(i + 1) * P], ident[0:H, 0:H])
                ins.then_inc(s_cols, 1)

            @block.vector
            def _(dve):
                step = Steps(dve, s_step)
                step.done(nc.vector.memset(zeros[:], 0.0))
                dve.wait_ge(s_summed, 1)
                for d in range(2):
                    for i in range(2):
                        n = 2 * d + i
                        step.link(nc.vector.tensor_scalar(gates[d][i][:], acc[0:H, n, :], gate_b[:, n:n + 1], None, ALU.add))
                    step.link(nc.vector.scalar_tensor_tensor(tmp[d][0][:], gates[d][1][:], -1.0, gates[d][1][:], ALU.mult, ALU.min))
                for d in range(2):
                    li, lf, cum, big = gates[d][0], gates[d][1], tmp[d][0], rows[d][0]
                    dve.wait_ge(s_act, 2 * d + 2)
                    step.link(nc.vector.scalar_tensor_tensor(lf[:], lf[:], 0.0, tmp[d][1][:], ALU.min, ALU.subtract))

                    def scan(out, src, op):
                        start = 0.0
                        for a in (0, T):
                            if d == 0:
                                o, s, end = out[:, a:a + T], src[:, a:a + T], out[:, T - 1:T]
                            else:
                                o = out[:, a + T - 1:(a - 1 if a else None):-1]
                                s, end = src[:, a + T - 1:(a - 1 if a else None):-1], out[:, 0:1]
                            step.link(nc.vector.tensor_tensor_scan(o, zeros[:, 0:T], s, start, ALU.add, op))
                            start = end
                    scan(cum, lf, ALU.add)
                    nc.vector.tensor_tensor(u[d][:], li[:], cum[:], ALU.subtract).then_inc(s_u, 1)
                    dve.wait_ge(s_u, d + 1)
                    scan(big, u[d], ALU.max)
                    step.link(nc.vector.tensor_tensor(rows[d][1][:], cum[:], big[:], ALU.add))
                dve.wait_ge(s_cols, 1)
                for d in range(2):
                    nc.vector.tensor_copy(u_cols[:, :, d, :], cols[:, d])

            @block.scalar
            def _(act):
                for d in range(2):
                    act.wait_ge(s_step, 4 + 3 * d)
                    nc.scalar.activation(tmp[d][1][:], tmp[d][0][:], ACT.Exp).then_inc(s_act, 1)
                    act.wait_ge(s_act, 2 * d + 1)
                    nc.scalar.activation(tmp[d][1][:], tmp[d][1][:], ACT.Ln, bias=1.0).then_inc(s_act, 1)


def mlstm(nc, name, q, k, v, rows, u_cols, masks, select, ones, out):
    with Stage(nc, name) as st:
        qk = st.ps("qk", [P, 3, 512])
        row = st.ps("row", [P, 2, 512])
        num, den = st.ps("num", [P, 512]), st.ps("den", [P, 512])
        w_all, w_lat = st.sb("w_all", [P, 2, 2 * T]), st.sb("w_lat", [P, 2, T])
        floor, part = st.sb("floor", [P, 2 * T]), st.sb("part", [P, 2 * T])
        s_qk, s_row, s_arg, s_exp, s_w, s_num, s_div, s_out = (
            st.sem(n) for n in ("qk", "row", "arg", "exp", "w", "num", "div", "out"))
        items = [(h, d) for h in range(H) for d in range(2)]
        EXPS = 7
        with nc.Block() as block:
            @block.tensor
            def _(pe):
                for n, (h, d) in enumerate(items):
                    if n >= 1:
                        pe.wait_ge(s_exp, EXPS * n)
                        pe.wait_ge(s_arg, 2 * n)
                    for i in range(2):
                        ins = nc.tensor.matmul(row[:, i, :], select[:, h, :], rows[d][i][:], start=True, stop=True)
                    ins.then_inc(s_row, 1)
                    if d == 0:
                        if n >= 1:
                            pe.wait_ge(s_w, 2 * n)
                        for s in range(2):
                            nc.tensor.matmul(qk[:, s, :], k[:, h, s * P:(s + 1) * P], q[:, h, :], start=True, stop=True)
                        for s in range(2):
                            ins = nc.tensor.matmul(qk[:, 2, s * T:(s + 1) * T], k[:, h, (s + 2) * P:(s + 3) * P],
                                                   q[:, h, T:], start=True, stop=True)
                        ins.then_inc(s_qk, 1)
                    pe.wait_ge(s_w, 2 * n + 2)
                    if n >= 1:
                        pe.wait_ge(s_out, n)
                    for acc, value in ((num, None), (den, ones)):
                        for s in range(2):
                            lhs = v[:, s, h * P:(h + 1) * P] if value is None else value
                            nc.tensor.matmul(acc[:], lhs, w_all[:, s, :], start=(s == 0), stop=False, skip_group_check=True)
                        for s in range(2):
                            lhs = v[:, s + 2, h * P:(h + 1) * P] if value is None else value
                            ins = nc.tensor.matmul(acc[:, T:], lhs, w_lat[:, s, :], start=False, stop=(s == 1),
                                                   skip_group_check=True)
                    ins.then_inc(s_num, 1)

            @block.vector
            def _(dve):
                for n, (h, d) in enumerate(items):
                    dve.wait_ge(s_row, n + 1)
                    if n >= 1:
                        dve.wait_ge(s_num, n)
                    nc.vector.tensor_tensor(w_all[:, :, 0:T], masks[:, d], over(row[:, 0, 0:T], 2), ALU.subtract).then_inc(s_arg, 1)
                    nc.vector.tensor_tensor(w_lat[:], masks[:, d], over(row[:, 0, T:], 2), ALU.subtract).then_inc(s_arg, 1)
                    dve.wait_ge(s_exp, EXPS * (n + 1))
                    dve.wait_ge(s_qk, h + 1)
                    nc.vector.scalar_tensor_tensor(w_all[:], qk[:, 0:2, :], P ** -0.5, w_all[:], ALU.mult, ALU.mult).then_inc(s_w, 1)
                    nc.vector.scalar_tensor_tensor(w_lat[:], qk[:, 2, :].rearrange("p (s t) -> p s t", s=2), P ** -0.5,
                                                   w_lat[:], ALU.mult, ALU.mult).then_inc(s_w, 1)
                    dve.wait_ge(s_num, n + 1)
                    nc.vector.tensor_tensor(floor[:], den[:], floor[:], ALU.max).then_inc(s_div, 1)
                    dve.wait_ge(s_div, 3 * n + 1)
                    nc.vector.scalar_tensor_tensor(floor[:], den[:], -1.0, floor[:], ALU.mult, ALU.max).then_inc(s_div, 1)
                    dve.wait_ge(s_div, 3 * n + 2)
                    nc.vector.reciprocal(floor[:], floor[:]).then_inc(s_div, 1)
                    dve.wait_ge(s_div, 3 * n + 3)
                    if d == 0:
                        nc.vector.tensor_tensor(out[:, h, :], num[:], floor[:], ALU.mult).then_inc(s_out, 1)
                    else:
                        nc.vector.tensor_tensor(part[:], num[:], floor[:], ALU.mult).then_inc(s_out, 1)
                        dve.wait_ge(s_out, n + 1)
                        nc.vector.tensor_tensor(out[:, h, :], out[:, h, :], part[:], ALU.add)

            @block.scalar
            def _(act):
                for n, (h, d) in enumerate(items):
                    u = lambda s: u_cols[:, s, d, h:h + 1]
                    act.wait_ge(s_row, n + 1)
                    if n >= 1:
                        act.wait_ge(s_num, n)
                        act.wait_ge(s_out, n)
                    nc.scalar.activation(floor[:], row[:, 1, :], ACT.Exp, scale=-1.0).then_inc(s_exp, 1)
                    act.wait_ge(s_arg, 2 * n + 2)
                    for s in range(2):
                        nc.scalar.activation(w_all[:, s, T:], row[:, 0, T:], ACT.Exp, bias=u(s), scale=-1.0).then_inc(s_exp, 1)
                    for s in range(2):
                        nc.scalar.activation(w_all[:, s, 0:T], w_all[:, s, 0:T], ACT.Exp, bias=u(s)).then_inc(s_exp, 1)
                        nc.scalar.activation(w_lat[:, s, :], w_lat[:, s, :], ACT.Exp, bias=u(s + 2)).then_inc(s_exp, 1)


def gla_decays(nc, name, low, gate_up, gate_b, la):
    with Stage(nc, name) as st:
        acc = st.ps("acc", [P, H, 2 * T])
        z, e = st.sb("z", [P, H, 2 * T]), st.sb("e", [P, H, 2 * T])
        s_summed, s_z, s_abs, s_log, s_la = (st.sem(n) for n in ("summed", "z", "abs", "log", "la"))
        with nc.Block() as block:
            @block.tensor
            def _(pe):
                for d in range(2):
                    if d:
                        pe.wait_ge(s_z, d * H)
                    for h in range(H):
                        nc.tensor.matmul(acc[:, h, :], gate_up[:, d, h * P:(h + 1) * P], low[:, d, :],
                                         start=True, stop=True).then_inc(s_summed, 1)

            @block.vector
            def _(dve):
                for d in range(2):
                    if d:
                        dve.wait_ge(s_la, 2)
                    for h in range(H):
                        dve.wait_ge(s_summed, d * H + h + 1)
                        nc.vector.tensor_scalar(z[:, h, :], acc[:, h, :], gate_b[:, d, h:h + 1], None, ALU.add).then_inc(s_z, 1)
                    dve.wait_ge(s_z, (d + 1) * H)
                    nc.vector.scalar_tensor_tensor(e[:], z[:], -1.0, z[:], ALU.mult, ALU.min).then_inc(s_abs, 1)
                    dve.wait_ge(s_log, 2 * d + 2)
                    nc.vector.scalar_tensor_tensor(z[:], z[:], 0.0, e[:], ALU.min, ALU.subtract).then_inc(s_abs, 1)
                    dve.wait_ge(s_abs, 2 * d + 2)
                    for segment in range(2):
                        nc.vector.tensor_scalar(la[d][segment], z[:, :, segment * T:(segment + 1) * T], 1.0 / 16, None,
                                                ALU.mult).then_inc(s_la, 1)

            @block.scalar
            def _(act):
                for d in range(2):
                    act.wait_ge(s_abs, 2 * d + 1)
                    nc.scalar.activation(e[:], e[:], ACT.Exp).then_inc(s_log, 1)
                    act.wait_ge(s_log, 2 * d + 1)
                    nc.scalar.activation(e[:], e[:], ACT.Ln, bias=1.0).then_inc(s_log, 1)


def select_experts(nc, name, q, keys, tile, chosen, iota, ident):
    with Stage(nc, name) as st:
        n_half = 2 * PEER_H
        acc = st.ps("acc", [P, n_half, N_KEYS])
        turned = st.ps("turned", [P, 3, P])
        s, s2 = st.sb("s", [P, n_half, N_KEYS]), st.sb("s2", [P, n_half, N_KEYS])
        top, index = st.sb("top", [P, n_half, TOPK]), st.sb("index", [P, n_half, TOPK], U32)
        key_no = st.sb("key_no", [P, n_half, TOPK])
        cand, cand2 = (st.sb(n, [P, PEER_H, TOPK * TOPK]) for n in ("cand", "cand2"))
        best, pos = st.sb("best", [P, PEER_H, TOPK]), st.sb("pos", [P, PEER_H, TOPK], U32)
        part, part_f = st.sb("part", [P, 2, P], U32), st.sb("part_f", [P, 2, P])
        hit = st.sb("hit", [P, P, TOPK])
        pick = st.sb("pick", [P, 3, P])
        total = st.sb("total", [P, PEER_H])
        s_scores, s_copied, s_step, s_cmp, s_exp, s_turned = (st.sem(n) for n in ("scores", "copied", "step", "cmp", "exp", "turned"))
        cols = slice(tile * P, (tile + 1) * P)

        with nc.Block() as block:
            @block.tensor
            def _(pe):
                for m in range(n_half):
                    nc.tensor.matmul(acc[:, m, :], q[:, m, cols], keys[:, m, :], start=True, stop=True).then_inc(s_scores, 1)
                pe.wait_ge(s_cmp, 1)
                for i in range(3):
                    ins = nc.tensor.transpose(turned[:, i, :], pick[:, i, :], ident)
                ins.then_inc(s_turned, 1)

            @block.scalar
            def _(act):
                for m in range(0, n_half, 4):
                    act.wait_ge(s_scores, m + 4)
                    nc.scalar.activation(s[:, m:m + 4, :], acc[:, m:m + 4, :], ACT.Copy).then_inc(s_copied, 1)
                act.wait_ge(s_exp, 1)
                nc.scalar.activation(best[:], best[:], ACT.Exp).then_inc(s_exp, 1)
                act.wait_ge(s_turned, 1)
                for i in range(3):
                    nc.scalar.activation(chosen[i][:, cols], turned[:, i, :], ACT.Copy)

            @block.vector
            def _(dve):
                step = Steps(dve, s_step)

                def best16(values, rest, groups, out, where, ready):
                    for m in range(groups):
                        ready(m)
                        step.done(nc.vector.max(out[:, m, 0:8], values[:, m, :]))
                    step.wait()
                    for m in range(groups):
                        step.done(nc.vector.max_index(where[:, m, 0:8], out[:, m, 0:8], values[:, m, :]))
                        step.done(nc.vector.match_replace(rest[:, m, :], out[:, m, 0:8], values[:, m, :], float(-3.4e38)))
                    step.wait()
                    for m in range(groups):
                        step.done(nc.vector.max(out[:, m, 8:16], rest[:, m, :]))
                    step.wait()
                    for m in range(groups):
                        step.done(nc.vector.max_index(where[:, m, 8:16], out[:, m, 8:16], rest[:, m, :]))
                    step.wait()

                best16(s, s2, n_half, top, index, lambda m: dve.wait_ge(s_copied, m // 4 + 1))
                step.done(nc.vector.tensor_copy(key_no[:], index[:]))
                pair = top[:].rearrange("p (h c) r -> p h c r", c=2)
                first = pair[:, :, 0, :].unsqueeze(3).broadcast_to([P, PEER_H, TOPK, TOPK])
                second = pair[:, :, 1, :].unsqueeze(2).broadcast_to([P, PEER_H, TOPK, TOPK])
                step.link(nc.vector.tensor_tensor(cand[:].rearrange("p h (a b) -> p h a b", a=TOPK), first, second, ALU.add))
                best16(cand, cand2, PEER_H, best, pos, lambda m: None)
                flat = pos[:].rearrange("p h r -> p (h r)")
                step.done(nc.vector.tensor_scalar(part[:, 0, :], flat, 4, None, ALU.logical_shift_right))
                step.link(nc.vector.tensor_scalar(part[:, 1, :], flat, TOPK - 1, None, ALU.bitwise_and))
                step.link(nc.vector.tensor_copy(part_f[:], part[:]))
                step.link(nc.vector.tensor_copy(total[:], best[:, :, 0]))
                nc.vector.tensor_tensor(best[:], best[:], bcast(total[:], TOPK), ALU.subtract).then_inc(s_exp, 1)
                numbers = key_no[:].rearrange("p (h c) r -> p h c r", c=2)
                for c in range(2):
                    step.link(nc.vector.tensor_tensor(hit[:], bcast(part_f[:, c, :], TOPK), over(iota[:, 0:TOPK], P), ALU.is_equal))
                    hit4 = hit[:].rearrange("p (h r) a -> p h r a", h=PEER_H)
                    step.link(nc.vector.tensor_tensor(hit4, hit4, numbers[:, :, c, :].unsqueeze(2).broadcast_to(
                        [P, PEER_H, TOPK, TOPK]), ALU.mult))
                    step.link(nc.vector.tensor_reduce(pick[:, c, :], hit[:], AX.X, ALU.add))
                dve.wait_ge(s_exp, 2)
                step.link(nc.vector.tensor_reduce(total[:], best[:], AX.X, ALU.add))
                step.link(nc.vector.reciprocal(total[:], total[:]))
                nc.vector.tensor_tensor(pick[:, 2, :].rearrange("p (h r) -> p h r", h=PEER_H), best[:],
                                        bcast(total[:], TOPK), ALU.mult).then_inc(s_cmp, 1)


def spread_weights(nc, name, chosen, iota, gmat):
    with Stage(nc, name) as st:
        n_tok = 8
        rows = st.sb("rows", [P, 2, n_tok, N_KEYS])
        cols = st.sb("cols", [P, 2, n_tok, N_KEYS])
        acc = st.ps("acc", [P, 2, n_tok, N_KEYS])
        s_hit, s_rows, s_cols, s_summed, s_taken = (st.sem(n) for n in ("hit", "rows", "cols", "summed", "taken"))
        steps = T // n_tok
        which = lambda i, t: chosen[i][:, bass.ds(t, n_tok)].unsqueeze(2).broadcast_to([P, n_tok, N_KEYS])
        with nc.Block() as block:
            @block.vector
            def _(dve):
                dve.sem_inc(s_summed, 2)
                with dve.Fori(0, steps // 2) as i:
                    for b in range(2):
                        n = i * 2 + b
                        dve.wait_ge(s_summed, n + 1)
                        nc.vector.tensor_tensor(rows[:, b], over(iota, n_tok), which(0, n * n_tok), ALU.is_equal).then_inc(s_hit, 1)
                        nc.vector.tensor_tensor(cols[:, b], over(iota, n_tok), which(1, n * n_tok), ALU.is_equal).then_inc(s_cols, 1)

            @block.gpsimd
            def _(pool):
                with pool.Fori(0, steps // 2) as i:
                    for b in range(2):
                        n = i * 2 + b
                        pool.wait_ge(s_hit, n + 1)
                        nc.gpsimd.tensor_tensor(rows[:, b], rows[:, b], which(2, n * n_tok), ALU.mult).then_inc(s_rows, 1)

            @block.tensor
            def _(pe):
                with pe.Fori(0, steps // 2) as i:
                    for b in range(2):
                        n = i * 2 + b
                        pe.wait_ge(s_rows, n + 1)
                        pe.wait_ge(s_cols, n + 1)
                        pe.wait_ge(s_taken, n + 1)
                        for t in range(n_tok):
                            ins = nc.tensor.matmul(acc[:, b, t, :], rows[:, b, t, :], cols[:, b, t, :], start=True, stop=True)
                        ins.then_inc(s_summed, 1)

            @block.scalar
            def _(act):
                act.sem_inc(s_taken, 2)
                with act.Fori(0, steps // 2) as i:
                    for b in range(2):
                        n = i * 2 + b
                        act.wait_ge(s_summed, n + 3)
                        nc.scalar.activation(gmat[:, bass.ds(n * n_tok, n_tok), :], acc[:, b], ACT.Copy).then_inc(s_taken, 1)


def dense_experts(nc, name, h, w_u, w_v, gmat, z, gate, scaled):
    with Stage(nc, name) as st:
        u, v = st.sb("u", [P, 2, KD * P]), st.sb("v", [P, 2, D])
        act_sb, x_sb = st.sb("act", [P, 2, T]), st.sb("x", [P, 2, T])
        score = st.ps("score", [P, 2, 512])
        acc = st.ps("acc", [P, KD, T])
        s_u, s_v = [st.sem(f"u{r}") for r in range(2)], [st.sem(f"v{r}") for r in range(2)]
        s_score, s_gelu, s_x, s_y = (st.sem(n) for n in ("score", "gelu", "x", "y"))

        def run(eng, body):
            body(0, 0, 0)
            body(1, 1, 0)
            with eng.Fori(1, N_KEYS // 2) as i:
                for r in range(2):
                    body(i * 2 + r, r, i)

        def first(j):
            return isinstance(j, int) and j < 2

        with nc.Block() as block:
            @block.sync
            def _(sp):
                def body(j, slot, turn):
                    if not first(j):
                        sp.wait_ge(s_score, j - 1)
                    sp.dma_start(u[:, slot, :], w_u[bass.ds(j, 1)].rearrange("a p c -> p (a c)")).then_inc(s_u[slot], 16)
                    if not first(j):
                        sp.wait_ge(s_y, j - 1)
                    sp.dma_start(v[:, slot, :], w_v[:, bass.ds(j, 1), :].rearrange("p a c -> p (a c)")).then_inc(s_v[slot], 16)
                run(sp, body)

            @block.tensor
            def _(pe):
                def scores(j, slot, turn):
                    pe.wait_ge(s_u[slot], turn * 16 + 16)
                    if not first(j):
                        pe.wait_ge(s_gelu, j - 1)
                    for k in range(KD):
                        ins = nc.tensor.matmul(score[:, slot, 0:T], u[:, slot, k * P:(k + 1) * P], h[:, k, :],
                                               start=(k == 0), stop=(k == KD - 1))
                    ins.then_inc(s_score, 1)

                def outputs(j, slot, turn, start=False, stop=False):
                    pe.wait_ge(s_v[slot], turn * 16 + 16)
                    pe.wait_ge(s_x, j + 1)
                    for m in range(KD):
                        ins = nc.tensor.matmul(acc[:, m, :], v[:, slot, m * P:(m + 1) * P], x_sb[:, slot, :],
                                               start=start and m % 2 == 0, stop=stop, skip_group_check=True)
                    ins.then_inc(s_y, 1)

                scores(0, 0, 0)
                scores(1, 1, 0)
                outputs(0, 0, 0, start=True)
                with pe.Fori(1, N_KEYS // 2) as i:
                    scores(i * 2, 0, i)
                    outputs(i * 2 - 1, 1, i - 1)
                    scores(i * 2 + 1, 1, i)
                    outputs(i * 2, 0, i)
                outputs(N_KEYS - 1, 1, N_KEYS // 2 - 1, stop=True)

            @block.scalar
            def _(act):
                def body(j, slot, turn):
                    act.wait_ge(s_score, j + 1)
                    if not first(j):
                        act.wait_ge(s_x, j - 1)
                    nc.scalar.activation(act_sb[:, slot, :], score[:, slot, 0:T], ACT.Gelu).then_inc(s_gelu, 1)
                run(act, body)

            @block.vector
            def _(dve):
                def body(j, slot, turn):
                    dve.wait_ge(s_gelu, j + 1)
                    if not first(j):
                        dve.wait_ge(s_y, j - 1)
                    nc.vector.tensor_tensor(x_sb[:, slot, :].unsqueeze(2), act_sb[:, slot, :].unsqueeze(2),
                                            gmat[:, :, bass.ds(j, 1)], ALU.mult).then_inc(s_x, 1)
                run(dve, body)
                dve.wait_ge(s_y, N_KEYS)
                for m in range(KD):
                    nc.vector.scalar_tensor_tensor(z[:, m, :], acc[:, m, :], gate[:, m, :], scaled[:, m, :], ALU.mult, ALU.add)


def peer(nc, name, h, w_q, keys_dram, w_u, w_v, z, gate, scaled, iota, ident):
    with Stage(nc, name) as st:
        chosen = [st.sb(f"chosen{i}", [P, T]) for i in range(3)]
        with Stage(nc, name + "_pick") as sel:
            q, keys = sel.sb("q", [P, 2 * PEER_H, T]), sel.sb("keys", [P, 2 * PEER_H, N_KEYS])
            load(nc, name + "_keys", [(keys[:], keys_dram)])
            project(nc, name + "_q", w_q, KD, h, T, [(2 * PEER_H, "scalar", copy_to(nc, q))])
            for tile in range(NT):
                select_experts(nc, f"{name}_select{tile}", q, keys, tile, chosen, iota, ident)
        gmat = st.sb("gmat", [P, T, N_KEYS])
        spread_weights(nc, name + "_spread", chosen, iota, gmat)
        dense_experts(nc, name + "_dense", h, w_u, w_v, gmat, z, gate, scaled)


VECTORS = [("c", KD), ("ada_b", 2 * 6 * KD), ("ln_g", 4 * KD), ("ln_b", 4 * KD), ("lb_raw", H), ("norm_g", 1),
           ("pool_scale", KD), ("conv", 2 * KF * 4), ("sinks", A_HEADS), ("c_2", KD * 2), ("b_mod_2", 2 * 6 * KD),
           ("ln_w_2", 4 * KD), ("ln_b_2", 4 * KD), ("ab_norm_w_2", H), ("sinks_2", A_HEADS), ("gla_gate_b_2", 2 * H),
           ("gla_norm_w_2", KD)]
CONSTANTS = [("ones", P), ("mean_of_p", P), ("mean_of_d", P), ("ident", P), ("iota", P)]
Q_ORDER = [h for c in range(GQA) for h in (c, GQA + c)]


def offsets(fields):
    at, out = 0, {}
    for name, n in fields:
        out[name] = (at, at + n)
        at += n
    return out, at


def first_block(nc, d, x, vec, con):
    with Stage(nc, "first") as blk:
        mods = blk.sb("mods", [P, 6 * KD, 1])
        h = blk.sb("h", [P, KD, T])
        sq = blk.sb("sq", [P, KD, T])
        c = vec("c").unsqueeze(2)
        ln = lambda layer, i: (vec("ln_g")[:, (2 * layer + i) * KD:(2 * layer + i + 1) * KD],
                               vec("ln_b")[:, (2 * layer + i) * KD:(2 * layer + i + 1) * KD])
        conv = lambda layer: vec("conv").rearrange("p (l f j) -> p l f j", l=2, j=4)[:, layer]

        modulation(nc, "mod0", c, d["ada_w"][0], vec("ada_b")[:, 0:6 * KD], mods, vec("ada_b")[:, 0:6 * KD])
        modulate(nc, "h00", h, x, mods, 0, (0,), True)
        even_mixer(nc, d, h, x, mods, vec, con)
        layer_norm(nc, "ln00", x, h, sq, T, *ln(0, 0), con("mean_of_d"))
        modulate(nc, "h01", h, x, mods, 3 * KD, (0,), True)
        conv_ffn(nc, "ffn0", h, d["w_up"][0], conv(0), d["w_down"][0], sq, mods[:, 5 * KD:, :], x)
        layer_norm(nc, "ln01", x, sq, h, T, *ln(0, 1), con("mean_of_d"))

        modulation(nc, "mod1", c, d["ada_w"][1], vec("ada_b")[:, 6 * KD:], mods, vec("ada_b")[:, 6 * KD:])
        modulate(nc, "h10", h, x, mods, 0, (0,), True)
        with Stage(nc, "poolmix") as st:
            inv_count = st.sb("inv_count", [P, len(POOL_WINDOWS), T])
            load(nc, "load_pool", [(inv_count[:], d["inv_count"])])
            pool_mixer(nc, "pool", h, d["pool_w"], vec("pool_scale"), inv_count, sq, mods[:, 2 * KD:3 * KD, :], x)
        layer_norm(nc, "ln10", x, sq, h, T, *ln(1, 0), con("mean_of_d"))
        modulate(nc, "h11", h, x, mods, 3 * KD, (0,), True)
        conv_ffn(nc, "ffn1", h, d["w_up"][1], conv(1), d["w_down"][1], sq, mods[:, 5 * KD:, :], x)
        layer_norm(nc, "ln11", x, sq, h, T, *ln(1, 1), con("mean_of_d"))


def hgrn_gates(nc, name, f, k, g, lb_raw):
    with Stage(nc, name) as st:
        share, lb, rest = st.sb("share", [P, H]), st.sb("lb", [P, H]), st.sb("rest", [P, H])
        s_step, s_sig, s_exp, s_clamped = st.sem("step"), st.sem("sig"), st.sem("exp"), st.sem("clamped")
        with nc.Block() as block:
            @block.scalar
            def _(act):
                nc.scalar.activation(k, f, ACT.Sigmoid, scale=-1.0).then_inc(s_sig, 1)
                act.wait_ge(s_sig, 1)
                nc.scalar.activation(f, f, ACT.Sigmoid).then_inc(s_sig, 1)
                act.wait_ge(s_step, 1)
                nc.scalar.activation(share[:], share[:], ACT.Exp).then_inc(s_exp, 1)
                act.wait_ge(s_clamped, 1)
                nc.scalar.activation(g, f, ACT.Ln)

            @block.vector
            def _(dve):
                step = Steps(dve, s_step)
                step.done(nc.vector.tensor_tensor(share[:], lb_raw, lb_raw, ALU.subtract))
                dve.wait_ge(s_exp, 1)
                step.link(nc.vector.reciprocal(lb[:], share[:]))
                step.link(nc.vector.tensor_tensor(share[:], share[:], lb[:], ALU.mult))
                step.link(nc.vector.tensor_tensor(lb[:], share[:], share[:], ALU.subtract))
                step.link(nc.vector.tensor_scalar(rest[:], lb[:], -1.0, 1.0, ALU.mult, ALU.add))
                dve.wait_ge(s_sig, 2)
                for h in range(H):
                    step.done(nc.vector.tensor_scalar(k[:, h, :], k[:, h, :], rest[:, h:h + 1], None, ALU.mult))
                    step.done(nc.vector.tensor_scalar(f[:, h, :], f[:, h, :], rest[:, h:h + 1], lb[:, h:h + 1], ALU.mult, ALU.add))
                step.wait()
                nc.vector.tensor_scalar(f, f, LN_MIN, None, ALU.max).then_inc(s_clamped, 1)


def even_mixer(nc, d, h, x, mods, vec, con):
    with Stage(nc, "mixer") as mix:
        cat = mix.sb("cat", [P, KD, T])
        qk = mix.sb("qk", [P, GQA + 1, T])
        v = mix.sb("v", [P, NT, 2 * P + 3 * P])
        with Stage(nc, "hgrn") as st:
            q, f, gate, k, g = (st.sb(n, [P, H, T]) for n in ("q", "f", "gate", "k", "g"))
            o = st.sb("o", [P, H, T])
            at, off = st.sb("at", [P, H * NT, P]), st.sb("off", [P, H, P])
            masks = st.sb("masks", [P, LEVELS + 1, P], I32)

            def silu_to(m, index, psum):
                return nc.scalar.activation(gate[:, bass.ds(index, 1), :], psum.unsqueeze(1), ACT.Silu)
            project(nc, "ab_in", d["ab_w_in"], KD, h, T,
                    [(H, "scalar", copy_to(nc, q)), (H, "scalar", copy_to(nc, f)), (H, "scalar", silu_to),
                     (GQA + 1, "scalar", copy_to(nc, qk))])
            token_major(nc, "ab_v", d["ab_w_v"], 5 * P, h, T, v)
            load(nc, "load_levels", [(masks[:], d["levels"][0])])
            hgrn_gates(nc, "gates", f[:], k[:], g[:], vec("lb_raw"))
            decayed_scores(nc, "hgrn_scores", q[:], k[:], [(g[:], False)], [masks], at[:], [off[:]])
            weighted_values(nc, "hgrn_values", [v[:, i, 0:4 * P] for i in range(NT)], P, at, [off], o)
            head_norm(nc, "hgrn_norm", o, cat[:, 0:H, :], gate, lambda c: vec("norm_g"), 1, T, RMS_EPS, con("mean_of_p"))
        with Stage(nc, "swa") as st:
            positions, cos, sin = st.sb("positions", [P, T], I32), st.sb("cos", [P, T]), st.sb("sin", [P, T])
            perm, inv_freq, mask = st.sb("perm", [P, P]), st.sb("inv_freq", [P, 1]), st.sb("mask", [P, 2 * P])
            load(nc, "load_swa", [(positions[:], d["positions"]), (perm[:], d["perm"]), (inv_freq[:], d["inv_freq"]),
                                  (mask[:], d["swa_mask"])])
            rope_tables(nc, "tables", positions[:], inv_freq[:], cos[:], sin[:])
            rope(nc, "rope", qk[:], perm[:], cos[:], sin[:])
            values = [v[:, i, 4 * P:5 * P].rearrange("p (g e) -> p g e", g=2) for i in range(NT)]
            attention(nc, "swa_attention",
                      [(lambda c: qk[:, c, 0:P], [qk[:, GQA, 0:P]], values[0:1], mask[:, P:2 * P], slice(0, P)),
                       (lambda c: qk[:, c, P:2 * P], [qk[:, GQA, :]], values, mask[:], slice(P, 2 * P))],
                      vec("sinks"), cat[:, H:, :], con("ident"))
        project(nc, "ab_out", d["ab_w_out"], KD, cat, T, [(KD, "vector", add_residual(nc, h, mods[:, 2 * KD:3 * KD, :], x))])


def second_block(nc, d, x_first, out, vec, con):
    with Stage(nc, "second") as blk:
        mods = blk.sb("mods2", [P, 6 * KD, 2])
        x, h = blk.sb("x2", [P, KD, 2 * T]), blk.sb("h2", [P, KD, 2 * T])
        lat = slice(T, 2 * T)
        c = vec("c_2").rearrange("p (k n) -> p k n", n=2)
        ln = lambda layer, i: (vec("ln_w_2")[:, (2 * layer + i) * KD:(2 * layer + i + 1) * KD],
                               vec("ln_b_2")[:, (2 * layer + i) * KD:(2 * layer + i + 1) * KD])
        bias = lambda layer: vec("b_mod_2")[:, layer * 6 * KD:(layer + 1) * 6 * KD]
        load(nc, "load_ctx", [(x[:, :, 0:T], d["ctx"])])
        s_x = blk.sem("x")
        with nc.Block() as block:
            @block.vector
            def _(dve):
                nc.vector.tensor_copy(x[:, :, lat], x_first).then_inc(s_x, 1)

        modulation(nc, "mod2", c, d["w_mod"][0], bias(0), mods, bias(0))
        modulate(nc, "h20", h, x, mods, 0, (0, 1), True)
        mixer_ab(nc, d, h, x, mods, vec, con)
        with Stage(nc, "norm20") as st:
            layer_norm(nc, "ln20", x, h, st.sb("sq", [P, KD, 2 * T]), 2 * T, *ln(0, 0), con("mean_of_d"))
        modulate(nc, "h21", h, x, mods, 3 * KD, (0, 1), True)
        for i, part in enumerate((slice(0, T), lat)):
            peer(nc, f"peer0{i}", h[:, :, part], d["peer_wq"][0], d["peer_keys"][0], d["peer_u"][0], d["peer_v"][0],
                 h[:, :, part], mods[:, 5 * KD:, i:i + 1], x[:, :, part], con("iota"), con("ident"))
        with Stage(nc, "norm21") as st:
            layer_norm(nc, "ln21", x, h, st.sb("sq", [P, KD, 2 * T]), 2 * T, *ln(0, 1), con("mean_of_d"))

        modulation(nc, "mod3", c, d["w_mod"][1], bias(1), mods, bias(1))
        modulate(nc, "h30", h, x, mods, 0, (0, 1), True)
        mixer_c(nc, d, h, x, mods, vec, con)
        with Stage(nc, "norm30") as st:
            layer_norm(nc, "ln30", x[:, :, lat], h[:, :, lat], st.sb("sq", [P, KD, T]), T, *ln(1, 0), con("mean_of_d"))
        modulate(nc, "h31", h[:, :, lat], x[:, :, lat], mods, 3 * KD, (1,), True)
        peer(nc, "peer1", h[:, :, lat], d["peer_wq"][1], d["peer_keys"][1], d["peer_u"][1], d["peer_v"][1],
             h[:, :, lat], mods[:, 5 * KD:, 1:2], x[:, :, lat], con("iota"), con("ident"))
        with Stage(nc, "norm31") as st:
            layer_norm(nc, "ln31", x[:, :, lat], h[:, :, lat], st.sb("sq", [P, KD, T]), T, *ln(1, 1), con("mean_of_d"))
        store(nc, "store", out, x[:, :, lat])


def store(nc, name, out, src):
    with Stage(nc, name) as st:
        s_stored = st.sem("stored")
        with nc.Block() as block:
            @block.sync
            def _(sp):
                sp.dma_start(out, src).then_inc(s_stored, 16)
                sp.wait_ge(s_stored, 16)


def mixer_ab(nc, d, h, x, mods, vec, con):
    lat = slice(T, 2 * T)
    with Stage(nc, "mixab") as mix:
        cat = mix.sb("cat", [P, KD, 2 * T])
        qk = mix.sb("qk", [P, GQA + 1, 2 * T])
        v = mix.sb("v", [P, 2 * NT, 5 * P])
        with Stage(nc, "mlstm") as st:
            q, k, gate, o = (st.sb(n, [P, H, 2 * T]) for n in ("q", "k", "gate", "o"))
            rows = [[st.sb(f"row{a}{b}", [H, 2 * T]) for b in range(2)] for a in range(2)]
            u_cols = st.sb("u_cols", [P, 4, 2, H])
            w_gates, gate_b = st.sb("w_gates", [P, KD, 4 * H]), st.sb("gate_b", [H, 4])
            masks, select = st.sb("masks", [P, 2, NT, T]), st.sb("select", [H, H, P])

            def sigmoid_to(m, index, psum):
                return nc.scalar.activation(gate[:, bass.ds(index, 1), :], psum.unsqueeze(1), ACT.Sigmoid)
            project(nc, "ab2_in", d["ab_w_in_2"], KD, h, 2 * T,
                    [(H, "scalar", copy_to(nc, q)), (H, "scalar", copy_to(nc, k)), (H, "scalar", sigmoid_to),
                     (GQA + 1, "scalar", copy_to(nc, qk))])
            token_major(nc, "ab2_v", d["ab_w_v_2"], 5 * P, h, 2 * T, v)
            load(nc, "load_gates", [(w_gates[:], d["ab_w_gates_2"]), (gate_b[:], d["ab_gate_b_2"]),
                                    (masks[:], d["causal"]), (select[:], d["select"])])
            log_sigmoid_rows(nc, "gate_rows", h, w_gates, gate_b, rows, u_cols, con("ident"))
            mlstm(nc, "mlstm_scan", q, k, v, rows, u_cols, masks, select, con("ones"), o)
            head_norm(nc, "mlstm_norm", o, cat[:, 0:H, :], gate, lambda c: vec("ab_norm_w_2")[:, c:c + 1], 1, 2 * T,
                      LN_EPS, con("mean_of_p"))
        with Stage(nc, "window") as st:
            perm, tables, mask = st.sb("perm", [P, P]), st.sb("tables", [P, 2, T]), st.sb("mask", [P, NT, 2 * T])
            load(nc, "load_window", [(perm[:], d["perm_2"]), (tables[:], d["axial"]), (mask[:], d["window"])])
            rope(nc, "rope2", qk[:, :, lat], perm[:], tables[:, 0, :], tables[:, 1, :])
            values = [v[:, i, 4 * P:5 * P].rearrange("p (g e) -> p g e", g=2) for i in range(2 * NT)]
            tiles = [(lambda c, a=i * P: qk[:, c, a:a + P], [qk[:, GQA, 0:T]] + [qk[:, GQA, lat]] * (i >= NT),
                      values if i >= NT else values[0:NT], mask[:, i - NT, :] if i >= NT else None, slice(i * P, (i + 1) * P))
                     for i in range(2 * NT)]
            attention(nc, "window_attention", tiles, vec("sinks_2"), cat[:, H:, :], con("ident"))
        project(nc, "ab2_out", d["ab_w_out_2"], KD, cat, 2 * T,
                [(KD, "vector", add_residual(nc, h, mods[:, 2 * KD:3 * KD, :], x))])


def mixer_c(nc, d, h, x, mods, vec, con):
    lat = slice(T, 2 * T)
    with Stage(nc, "mixc") as mix:
        gate = mix.sb("gate", [P, KD, T])
        o = mix.sb("o", [P, KD, T])
        with Stage(nc, "gla") as st:
            q = st.sb("q", [P, H, T])
            k = [st.sb(f"k{i}", [P, H, T]) for i in range(2)]
            v = st.sb("v", [P, 2 * NT, KD * P])
            la = [[st.sb(f"la{a}{b}", [P, H, T]) for b in range(2)] for a in range(2)]

            def k_to(m, index, psum):
                nc.scalar.activation(k[0][:, bass.ds(index, 1), :], psum[:, 0:T].unsqueeze(1), ACT.Copy)
                return nc.scalar.activation(k[1][:, bass.ds(index, 1), :], psum[:, lat].unsqueeze(1), ACT.Copy)

            def scaled_to(m, index, psum):
                return nc.scalar.activation(q[:, bass.ds(index, 1), :], psum.unsqueeze(1), ACT.Copy, scale=P ** -0.5)

            def silu_to(m, index, psum):
                return nc.scalar.activation(gate[:, bass.ds(index, 1), :], psum.unsqueeze(1), ACT.Silu)
            project(nc, "gla_k", d["gla_w_k_2"], KD, h, 2 * T, [(H, "scalar", k_to)])
            project(nc, "gla_qg", d["gla_w_qg_2"], KD, h[:, :, lat], T, [(H, "scalar", scaled_to), (KD, "scalar", silu_to)])
            token_major(nc, "gla_v", d["gla_w_v_2"], KD * P, h, 2 * T, v)
            with Stage(nc, "decays") as dec:
                w_low, low = dec.sb("w_low", [P, KD, 32]), dec.sb("low", [16, 2, 2 * T])
                gate_up = dec.sb("gate_up", [16, 2, H * P])
                acc = dec.ps("acc", [P, 2, 2 * T])
                s_low, s_copied = dec.sem("low"), dec.sem("copied")
                load(nc, "load_low", [(w_low[:], d["gla_w_low_2"]), (gate_up[:], d["gla_gate_up_2"])])
                with nc.Block() as block:
                    @block.tensor
                    def _(pe):
                        for n in range(2):
                            for kc in range(KD):
                                ins = nc.tensor.matmul(acc[0:16, n, :], w_low[:, kc, n * 16:(n + 1) * 16], h[:, kc, :],
                                                       start=(kc == 0), stop=(kc == KD - 1))
                        ins.then_inc(s_low, 1)

                    @block.scalar
                    def _(act):
                        act.wait_ge(s_low, 1)
                        nc.scalar.activation(low[:], acc[0:16], ACT.Copy).then_inc(s_copied, 1)
                gla_decays(nc, "gla_decays", low, gate_up, vec("gla_gate_b_2").rearrange("p (d h) -> p d h", d=2),
                           [[a[:] for a in row] for row in la])
            with Stage(nc, "scores") as sc:
                at, offs = sc.sb("at", [P, H * NT, P]), [sc.sb(f"off{i}", [P, H, P]) for i in range(2)]
                ctx_at = sc.sb("ctx_at", [P, 2, H, T])
                masks = [sc.sb(f"masks{i}", [P, LEVELS + 1, P], I32) for i in range(2)]
                load(nc, "load_levels2", [(masks[0][:], d["levels"][0]), (masks[1][:], d["levels"][1])])
                decayed_scores(nc, "gla_scores", q[:], k[1][:], [(la[0][1][:], False), (la[1][1][:], True)], masks, at[:],
                               [a[:] for a in offs], (k[0][:], [la[0][0], la[1][0]], ctx_at))
                weighted_values(nc, "gla_values", [v[:, NT + i, :] for i in range(NT)], 2 * P, at, offs, o,
                                ([v[:, i, :] for i in range(NT)], ctx_at))
        y = mix.sb("y", [P, KD, T])
        head_norm(nc, "gla_norm", o, y, gate, lambda c: vec("gla_norm_w_2")[:, c:c + 1], 2, T, LN_EPS, con("mean_of_p"))
        project(nc, "gla_out", d["gla_w_out_2"], KD, y, T,
                [(KD, "vector", add_residual(nc, h[:, :, lat], mods[:, 2 * KD:3 * KD, 1:2], x[:, :, lat]))])


def program(nc, d, out):
    vec_at, n_vec = offsets(VECTORS)
    con_at, n_con = offsets(CONSTANTS)
    with Stage(nc, "all") as st:
        vectors, constants = st.sb("vectors", [P, n_vec]), st.sb("constants", [P, n_con])
        x = st.sb("x", [P, KD, T])
        vec = lambda name: vectors[:, vec_at[name][0]:vec_at[name][1]]
        con = lambda name: constants[:, con_at[name][0]:con_at[name][1]]
        load(nc, "load_all", [(vectors[:], d["vectors"]), (constants[:], d["constants"]), (x[:], d["x"])])
        first_block(nc, d, x, vec, con)
        second_block(nc, d, x[:], out, vec, con)


def columns(v):
    return np.ascontiguousarray(np.reshape(v, (-1, P)).T)


def chunked(w):
    kc, mo = w.shape[0] // P, w.shape[1] // P
    return np.ascontiguousarray(w.reshape(kc, P, mo, P).transpose(2, 1, 0, 3).reshape(mo, P, kc * P))


def feature_major(x):
    return np.ascontiguousarray(x.reshape(x.shape[0], -1, P).transpose(2, 1, 0))


def constants_of_shapes():
    f = np.float32
    i = np.arange(P)
    con = np.concatenate([np.ones((P, P)), np.full((P, P), 1 / P), np.full((P, P), 1 / D), np.eye(P),
                          np.broadcast_to(i, (P, P))], 1).astype(f)
    s, t = i[:, None], i[None, :]
    levels = np.zeros((2, P, LEVELS + 1, P), np.int32)
    levels[:, :, 0, :] = s == t
    for level in range(1, LEVELS + 1):
        half = 2 ** (level - 1)
        same = s // (2 * half) == t // (2 * half)
        levels[0, :, level, :] = same & (s // half % 2 == 0) & (t // half % 2 == 1)
        levels[1, :, level, :] = levels[0, :, level, :].T
    masked = lambda keep: np.where(keep, 0.0, MASKED).astype(f)
    rel = s + P - np.arange(2 * P)[None, :]
    swa_mask = masked((rel >= 0) & (rel < P))
    tt = np.arange(T)
    causal = np.stack([masked((tt[:, None] <= tt[None, :])), masked(tt[:, None] >= tt[None, :])])
    causal = causal.reshape(2, NT, P, T).transpose(2, 0, 1, 3)
    window = np.zeros((NT, P, 2 * T), f)
    window[:, :, T:] = masked(np.abs(tt[:, None] - tt[None, :]) <= P).reshape(NT, P, T)
    select = np.zeros((H, H, P), f)
    select[np.arange(H), np.arange(H), :] = 1
    inv_count = np.stack([1.0 / np.minimum(tt + 1, w) for w in POOL_WINDOWS]).astype(f)
    dim = i % A_DIM
    rope_dim = A_DIM // 4
    inv = f(500000.0) ** (-np.arange(0, rope_dim, 2, dtype=f) / f(rope_dim))
    inv_freq = np.where(dim < rope_dim, inv[dim % (rope_dim // 2)], 0.0).astype(f)[:, None]
    perm = np.zeros((P, P), f)
    for r in range(P):
        if dim[r] < rope_dim // 2:
            perm[r, r + rope_dim // 2] = -1
        elif dim[r] < rope_dim:
            perm[r, r - rope_dim // 2] = 1
    n_freq = A_DIM // 4
    inv2 = f(10000.0) ** (-np.arange(n_freq, dtype=f) / f(n_freq))
    ang = np.concatenate([(tt // 64).astype(f)[:, None] * inv2, (tt % 64).astype(f)[:, None] * inv2], -1).astype(f)
    axial = np.stack([np.cos(ang).T[dim // 2], np.sin(ang).T[dim // 2]], 1).astype(f)
    perm_2 = np.zeros((P, P), f)
    perm_2[i[0::2], i[1::2]] = -1
    perm_2[i[1::2], i[0::2]] = 1
    return {"constants": con, "levels": levels, "swa_mask": swa_mask, "causal": causal,
            "window": window.transpose(1, 0, 2), "select": select,
            "inv_count": np.broadcast_to(inv_count, (P,) + inv_count.shape), "inv_freq": inv_freq,
            "perm": perm.T, "axial": axial, "perm_2": perm_2.T}


def lay_out(a):
    w = {}
    w["x"], w["ctx"] = feature_major(a["x"][0]), feature_major(a["ctx_2"][0])
    w["positions"] = np.broadcast_to(a["positions"], (P, T))
    w["ada_w"] = np.stack([chunked(m) for m in a["ada_w"]])
    w["w_mod"] = np.stack([chunked(m) for m in a["w_mod_2"]])
    heads = lambda m: m.reshape(m.shape[0], A_HEADS, A_DIM)[:, Q_ORDER].reshape(m.shape[0], -1)
    cut = lambda m, widths: np.split(m, np.cumsum(widths)[:-1], axis=1)
    aq, af, ai, ag, bq, bk, bv = cut(a["ab_w_in"][0], [512, 512, 512, 512, 512, 128, 128])
    w["ab_w_in"] = chunked(np.concatenate([aq, af, ag, heads(bq), bk], 1))
    w["ab_w_v"] = np.concatenate([ai, bv], 1).reshape(KD, P, -1)
    w["ab_w_out"] = chunked(a["ab_w_out"][0])
    w["pool_w"] = a["pool_w"][0].reshape(4, 2, P, 2, P).transpose(2, 0, 3, 1, 4).reshape(P, KD, 2, P)
    up = a["ffn_w_up"].reshape(2, D, 2, KF, P).transpose(0, 1, 3, 2, 4).reshape(2, D, -1)
    w["w_up"] = np.stack([chunked(m) for m in up])
    w["w_down"] = np.stack([chunked(m) for m in a["ffn_w_down"]])
    mq, mk, mv, mo, mg, q2, k2, v2 = cut(a["ab_w_in_2"][0], [512, 512, 512, 512, 16, 512, 128, 128])
    w["ab_w_in_2"] = chunked(np.concatenate([mq, mk, mo, heads(q2), k2], 1))
    w["ab_w_v_2"] = np.concatenate([mv, v2], 1).reshape(KD, P, -1)
    w["ab_w_gates_2"] = mg.reshape(KD, P, 16).transpose(1, 0, 2)
    w["ab_gate_b_2"] = a["ab_gate_b_2"][0].reshape(4, H).T
    w["ab_w_out_2"] = chunked(a["ab_w_out_2"][0])
    gq, gk, gv, gg, glow = cut(a["gla_w_in_2"][0], [512, 512, 1024, 1024, 32])
    w["gla_w_k_2"], w["gla_w_qg_2"] = chunked(gk), chunked(np.concatenate([gq, gg], 1))
    w["gla_w_v_2"] = gv.reshape(KD, P, -1)
    w["gla_w_low_2"] = glow.reshape(KD, P, 32).transpose(1, 0, 2)
    w["gla_gate_up_2"] = a["gla_gate_up_2"][0].transpose(1, 0, 2)
    w["gla_w_out_2"] = chunked(a["gla_w_out_2"][0])
    w["peer_wq"] = np.stack([chunked(m) for m in a["peer_wq_2"]])
    w["peer_keys"] = a["peer_keys_2"].reshape(2, 2 * PEER_H, N_KEYS, P).transpose(0, 3, 1, 2)
    w["peer_u"] = a["peer_u_2"].reshape(2, N_KEYS, N_KEYS, KD, P).transpose(0, 2, 4, 3, 1).reshape(2, N_KEYS, P, D)
    w["peer_v"] = a["peer_v_2"].reshape(2, N_KEYS, N_KEYS, D)
    spread = lambda v: np.broadcast_to(np.reshape(v, (1, -1)), (P, np.size(v)))
    conv = np.concatenate([a["ffn_conv_w"], a["ffn_conv_b"][:, None, :]], 1)
    vectors = {
        "c": columns(a["c"]), "ada_b": columns(a["ada_b"]), "ln_g": columns(a["ln_g"]), "ln_b": columns(a["ln_b"]),
        "lb_raw": columns(a["hgrn_lb_raw"]), "norm_g": columns(a["hgrn_norm_g"]), "pool_scale": columns(a["pool_scale"]),
        "conv": conv.reshape(2, 4, KF, P).transpose(3, 0, 2, 1).reshape(P, -1), "sinks": spread(a["attn_sinks"]),
        "c_2": np.stack([columns(a["c_ctx_2"]), columns(a["c_2"])], 2).reshape(P, -1), "b_mod_2": columns(a["b_mod_2"]),
        "ln_w_2": columns(a["ln_w_2"]), "ln_b_2": columns(a["ln_b_2"]), "ab_norm_w_2": columns(a["ab_norm_w_2"]),
        "sinks_2": spread(a["ab_sink_2"]), "gla_gate_b_2": columns(a["gla_gate_b_2"]),
        "gla_norm_w_2": columns(a["gla_norm_w_2"])}
    w["vectors"] = np.concatenate([vectors[name] for name, _ in VECTORS], 1)
    w.update(constants_of_shapes())
    return {name: np.ascontiguousarray(v) for name, v in w.items()}


def kernel(**inputs):
    import concourse.bacc as bacc
    from concourse.bass_utils import run_bass_kernel_spmd

    arrays = lay_out({name: np.asarray(v) for name, v in inputs.items()})
    nc = bacc.Bacc("TRN2", target_bir_lowering=False, num_devices=1)
    d = {name: nc.dram_tensor(f"in_{name}", v.shape, mybir.dt.from_np(v.dtype), kind="ExternalInput").ap()
         for name, v in arrays.items()}
    out = nc.dram_tensor("out", (P, KD, T), F32, kind="ExternalOutput").ap()
    program(nc, d, out)
    run = run_bass_kernel_spmd(nc, [{f"in_{name}": v for name, v in arrays.items()}], core_ids=[0])
    y = np.asarray(run.results[0]["out"])
    return np.ascontiguousarray(y.transpose(2, 1, 0).reshape(1, T, D))
```

```python
from contextlib import ExitStack

import numpy as np

import concourse.bass as bass
from concourse import mybir
from concourse.alu_op_type import AluOpType as ALU

ACT = mybir.ActivationFunctionType
AX = mybir.AxisListType
F32 = mybir.dt.float32
I32 = mybir.dt.int32
U32 = mybir.dt.uint32
F32R = mybir.dt.float32r

P = 128
D = 1024
KD = D // P
T = 256
NT = T // P
H = 4
D_FF = 2816
KF = D_FF // P
LEVELS = 7
A_HEADS, A_DIM, GQA = 8, 64, 4
N_KEYS, PEER_H, TOPK = 128, 8, 16
POOL_WINDOWS = (2, 4, 8, 16)
ALPHA = float((2.0 * 2) ** 0.25)
LN_EPS, RMS_EPS = 1e-5, 1e-6
LN_MIN = 2.0 ** -64
MASKED = -1e30
EVEN_PI_1, EVEN_PI_2 = 6.28125, 0.001934051513671875
EVEN_PI_3 = 2 * np.pi - EVEN_PI_1 - EVEN_PI_2
ROUND = 12582912.0


class Stage:

    def __init__(self, nc, name):
        self.nc, self.name, self.ctx, self.sems = nc, name, ExitStack(), []

    def __enter__(self):
        return self

    def __exit__(self, *_):
        self.nc.clear_and_free_semaphores(self.sems)
        self.nc.all_engine_barrier()
        self.ctx.close()

    def sb(self, name, shape, dt=F32):
        return self.ctx.enter_context(self.nc.sbuf_tensor(f"{self.name}_{name}", shape, dt))[:]

    def ps(self, name, shape):
        return self.ctx.enter_context(self.nc.psum_tensor(f"{self.name}_{name}", shape, F32))[:]

    def sem(self, name):
        s = self.nc.alloc_semaphore(f"{self.name}_{name}")
        self.sems.append(s)
        return s


class Steps:

    def __init__(self, eng, sem):
        self.eng, self.sem, self.n = eng, sem, 0

    def done(self, ins):
        ins.then_inc(self.sem, 1)
        self.n = self.n + 1

    def wait(self):
        self.eng.wait_ge(self.sem, self.n)

    def link(self, ins):
        self.done(ins)
        self.wait()


def each_chunk(eng, first, count, ring, body):
    turns = count // ring
    if turns >= 2:
        with eng.Fori(0, turns) as i:
            for r in range(ring):
                body(first + r + i * ring, (first + r) % ring, (first + r) // ring + i)
    else:
        turns = 0
    for m in range(first + turns * ring, first + count):
        body(m, m % ring, m // ring)


def bcast(ap, n):
    return ap.unsqueeze(2).broadcast_to([ap.shape[0], ap.shape[1], n])


def over(ap, n):
    return ap.unsqueeze(1).broadcast_to([ap.shape[0], n, ap.shape[1]])


def load(nc, name, pairs):
    with Stage(nc, name) as st:
        s_loaded = st.sem("loaded")
        with nc.Block() as block:
            @block.sync
            def _(sp):
                for dst, src in pairs:
                    sp.dma_start(dst, src).then_inc(s_loaded, 16)
                sp.wait_ge(s_loaded, 16 * len(pairs))


def products(nc, out, lhs, rhs, start, stop):
    for n, (a, b) in enumerate(((lhs[0], rhs[0]), (lhs[0], rhs[1]), (lhs[1], rhs[0]))):
        ins = nc.tensor.matmul(out, a, b, start=start and n == 0, stop=stop and n == 2, skip_group_check=True)
    return ins


def part(pair, *index):
    return tuple(a[index] for a in pair)


def split(nc, name, src, pair):
    with Stage(nc, name) as st:
        s_hi = st.sem("hi")
        chunks = src.shape[1]
        with nc.Block() as block:
            @block.scalar
            def _(act):
                for k in range(chunks):
                    nc.scalar.activation(pair[0][:, k], src[:, k], ACT.Copy).then_inc(s_hi, 1)

            @block.vector
            def _(dve):
                for k in range(chunks):
                    dve.wait_ge(s_hi, k + 1)
                    nc.vector.tensor_tensor(pair[1][:, k], src[:, k], pair[0][:, k].bitcast(F32), ALU.subtract)


def project(nc, name, weights, kc, rhs, t, segments):
    with Stage(nc, name) as st:
        total = sum(n for n, _ in segments)
        pieces = 1 if kc <= KD else 2
        banks, width = 4 // pieces, kc // pieces
        raw = st.sb("raw", [P, 4, width * P])
        w = st.sb("hi", [P, 4, width * P], F32R), st.sb("lo", [P, 4, width * P], F32R)
        acc = st.ps("acc", [P, banks, 512])
        s_loaded = [st.sem(f"loaded{r}") for r in range(4)]
        s_hi, s_lo, s_used, s_summed, s_taken = (st.sem(n) for n in ("hi", "lo", "used", "summed", "taken"))

        with nc.Block() as block:
            @block.sync
            def _(sp):
                def fetch(m, bank, turn):
                    for i in range(pieces):
                        slot = bank * pieces + i
                        if not isinstance(m, int) or m >= banks:
                            sp.wait_ge(s_lo, m * pieces + i - 3)
                        cols = slice(i * width * P, (i + 1) * width * P)
                        src = weights[bass.ds(m, 1), :, cols].rearrange("a p c -> p (a c)")
                        sp.dma_start(raw[:, slot, :], src).then_inc(s_loaded[slot], 16)
                for m in range(min(banks, total)):
                    fetch(m, m, 0)
                if total > banks:
                    each_chunk(sp, banks, total - banks, banks, fetch)

            @block.vector
            def _(dve):
                def body(m, bank, turn):
                    for i in range(pieces):
                        slot = bank * pieces + i
                        dve.wait_ge(s_hi, m * pieces + i + 1)
                        nc.vector.tensor_tensor(w[1][:, slot, :], raw[:, slot, :], w[0][:, slot, :].bitcast(F32),
                                                ALU.subtract).then_inc(s_lo, 1)
                each_chunk(dve, 0, total, banks, body)

            @block.tensor
            def _(pe):
                pe.sem_inc(s_used, 4)

                def body(m, bank, turn):
                    pe.wait_ge(s_taken, m + 1)
                    for i in range(pieces):
                        pe.wait_ge(s_lo, m * pieces + i + 1)
                        for k in range(width):
                            ins = products(nc, acc[:, bank, 0:t], part(w, slice(None), bank * pieces + i, slice(k * P, (k + 1) * P)),
                                           part(rhs, slice(None), i * width + k), start=(i == 0 and k == 0),
                                           stop=(i == pieces - 1 and k == width - 1))
                        ins.then_inc(s_used, 1)
                each_chunk(pe, 0, total, banks, body)

            @block.scalar
            def _(act):
                act.sem_inc(s_taken, banks)
                lead = banks // 2

                def hi(m, bank, turn):
                    for i in range(pieces):
                        slot = bank * pieces + i
                        act.wait_ge(s_loaded[slot], turn * 16 + 16)
                        act.wait_ge(s_used, m * pieces + i + 1)
                        nc.scalar.activation(w[0][:, slot, :], raw[:, slot, :], ACT.Copy).then_inc(s_hi, 1)

                def body(m, bank, turn):
                    hi(m + lead, (bank + lead) % banks, turn + (bank + lead) // banks)
                    take(m, bank, turn)

                def take(m, bank, turn):
                    act.wait_ge(s_used, m * pieces + 4 + pieces)
                    evacuate(m - first, acc[:, bank, 0:t]).then_inc(s_taken, 1)

                for m in range(lead):
                    hi(m, m, 0)
                first = 0
                for n, evacuate in segments:
                    ahead = min(n, total - lead - first)
                    each_chunk(act, first, ahead, banks, body)
                    for m in range(first + ahead, first + n):
                        take(m, m % banks, m // banks)
                    first += n


def copy_to(nc, dst, func=ACT.Copy, scale=1.0):
    def evacuate(index, psum):
        return nc.scalar.activation(dst[:, bass.ds(index, 1), :], psum.unsqueeze(1), func, scale=scale)
    return evacuate


def gate_to(nc, dst, gate):
    def evacuate(index, psum):
        for n in range(gate.shape[2]):
            half = slice(n * T, (n + 1) * T)
            ins = nc.scalar.activation(dst[:, bass.ds(index, 1), half], psum[:, half].unsqueeze(1), ACT.Copy,
                                       scale=gate[:, bass.ds(index, 1), n])
        return ins
    return evacuate


def token_major(nc, name, weights, n, xt, t, dst):
    with Stage(nc, name) as st:
        tiles = t // P
        groups = [(a, min(a + 512, n)) for a in range(0, n, 512)]
        raw = st.sb("raw", [P, 4, n])
        w = st.sb("hi", [P, 4, n], F32R), st.sb("lo", [P, 4, n], F32R)
        acc = st.ps("acc", [P, tiles * len(groups), 512])
        s_loaded = [st.sem(f"loaded{r}") for r in range(4)]
        s_hi, s_lo, s_used = st.sem("hi"), st.sem("lo"), st.sem("used")
        with nc.Block() as block:
            @block.sync
            def _(sp):
                for k in range(KD):
                    if k >= 4:
                        sp.wait_ge(s_lo, k - 3)
                    sp.dma_start(raw[:, k % 4, :], weights[k]).then_inc(s_loaded[k % 4], 16)

            @block.vector
            def _(dve):
                for k in range(KD):
                    dve.wait_ge(s_hi, k + 1)
                    nc.vector.tensor_tensor(w[1][:, k % 4, :], raw[:, k % 4, :], w[0][:, k % 4, :].bitcast(F32),
                                            ALU.subtract).then_inc(s_lo, 1)

            @block.tensor
            def _(pe):
                for k in range(KD):
                    pe.wait_ge(s_lo, k + 1)
                    for i in range(tiles):
                        for g, (a, b) in enumerate(groups):
                            ins = products(nc, acc[:, i * len(groups) + g, 0:b - a], part(xt, slice(None), k, slice(i * P, (i + 1) * P)),
                                           part(w, slice(None), k % 4, slice(a, b)), start=(k == 0), stop=(k == KD - 1))
                    ins.then_inc(s_used, 1)

            @block.scalar
            def _(act):
                for k in range(KD):
                    act.wait_ge(s_loaded[k % 4], 16 * (k // 4 + 1))
                    if k >= 4:
                        act.wait_ge(s_used, k - 3)
                    nc.scalar.activation(w[0][:, k % 4, :], raw[:, k % 4, :], ACT.Copy).then_inc(s_hi, 1)
                act.wait_ge(s_used, KD)
                for i in range(tiles):
                    for g, (a, b) in enumerate(groups):
                        nc.scalar.activation(dst[:, i, a:b], acc[:, i * len(groups) + g, 0:b - a], ACT.Copy)


def modulate(nc, name, h, pair, x, mods, shift, cols):
    with Stage(nc, name) as st:
        s_h, s_hi = st.sem("h"), st.sem("hi")
        n = len(cols)
        with nc.Block() as block:
            @block.vector
            def _(dve):
                for k in range(KD):
                    for i, c in enumerate(cols):
                        half = slice(i * T, (i + 1) * T)
                        nc.vector.tensor_scalar(h[:, k, half], x[:, k, half], mods[:, shift + KD + k, c:c + 1],
                                                mods[:, shift + k, c:c + 1], ALU.mult, ALU.add).then_inc(s_h, 1)
                for k in range(KD):
                    dve.wait_ge(s_hi, k + 1)
                    nc.vector.tensor_tensor(pair[1][:, k], h[:, k], pair[0][:, k].bitcast(F32), ALU.subtract)
                nc.vector.tensor_scalar(x[:], x[:], ALPHA, None, ALU.mult)

            @block.scalar
            def _(act):
                for k in range(KD):
                    act.wait_ge(s_h, (k + 1) * n)
                    nc.scalar.activation(pair[0][:, k], h[:, k], ACT.Copy).then_inc(s_hi, 1)


def layer_norm(nc, name, x, z, sq, t, gain, bias, mean_of_d, residual=True):
    with Stage(nc, name) as st:
        ps_mean, ps_var = st.ps("mean", [P, 512]), st.ps("var", [P, 512])
        rstd = st.sb("rstd", [P, t])
        s_mean, s_var, s_centred, s_squared = st.sem("mean"), st.sem("var"), st.sem("centred"), st.sem("squared")
        s_step, s_root, s_scaled, s_added = st.sem("step"), st.sem("root"), st.sem("scaled"), st.sem("added")
        with nc.Block() as block:
            @block.tensor
            def _(pe):
                for k in range(KD):
                    if residual:
                        pe.wait_ge(s_added, k + 1)
                    ins = nc.tensor.matmul(ps_mean[:, 0:t], mean_of_d, z[:, k, :], start=(k == 0), stop=(k == KD - 1))
                ins.then_inc(s_mean, 1)
                for k in range(KD):
                    pe.wait_ge(s_squared, k + 1)
                    ins = nc.tensor.matmul(ps_var[:, 0:t], mean_of_d, sq[:, k, :], start=(k == 0), stop=(k == KD - 1))
                ins.then_inc(s_var, 1)

            @block.vector
            def _(dve):
                step = Steps(dve, s_step)
                if residual:
                    for k in range(KD):
                        nc.vector.tensor_tensor(z[:, k, :], z[:, k, :], x[:, k, :], ALU.add).then_inc(s_added, 1)
                dve.wait_ge(s_mean, 1)
                for k in range(KD):
                    nc.vector.tensor_tensor(z[:, k, :], z[:, k, :], ps_mean[:, 0:t], ALU.subtract).then_inc(s_centred, 1)
                dve.wait_ge(s_var, 1)
                step.link(nc.vector.tensor_scalar(rstd[:], ps_var[:, 0:t], LN_EPS, None, ALU.add))
                step.link(nc.vector.reciprocal(rstd[:], rstd[:]))
                dve.wait_ge(s_root, 1)
                for k in range(KD):
                    nc.vector.tensor_tensor(z[:, k, :], z[:, k, :], rstd[:], ALU.mult).then_inc(s_scaled, 1)

            @block.scalar
            def _(act):
                for k in range(KD):
                    act.wait_ge(s_centred, k + 1)
                    nc.scalar.activation(sq[:, k, :], z[:, k, :], ACT.Square).then_inc(s_squared, 1)
                act.wait_ge(s_step, 2)
                nc.scalar.activation(rstd[:], rstd[:], ACT.Sqrt).then_inc(s_root, 1)
                for k in range(KD):
                    act.wait_ge(s_scaled, k + 1)
                    nc.scalar.activation(x[:, k, :], z[:, k, :], ACT.Identity, bias=bias[:, k:k + 1],
                                         scale=gain[:, k:k + 1])


def modulation(nc, name, c, weights, bias, mods, ident):
    n = c.shape[2]
    groups = 6 * D // 512
    half = KD // 2
    with Stage(nc, name) as st:
        act_c = st.sb("act_c", [P, KD, n])
        wt = st.sb("weights", [P, 4, half, 512])
        rows = st.sb("rows", [n, groups, 512])
        acc = st.ps("acc", [P, 4, 512])
        cols = st.ps("cols", [P, 6 * KD, n])
        s_loaded = [st.sem(f"loaded{r}") for r in range(4)]
        s_silu, s_used, s_row, s_cols, s_bias = (st.sem(k) for k in ("silu", "used", "row", "cols", "bias"))
        with nc.Block() as block:
            @block.sync
            def _(sp):
                def fetch(u, slot, turn):
                    if not isinstance(u, int) or u >= 4:
                        sp.wait_ge(s_used, u - 3)
                    sp.dma_start(wt[:, slot], weights[bass.ds(u, 1)].rearrange("a p k c -> p (a k) c")).then_inc(s_loaded[slot], 16)
                for u in range(4):
                    fetch(u, u, 0)
                each_chunk(sp, 4, 2 * groups - 4, 4, fetch)

            @block.tensor
            def _(pe):
                pe.wait_ge(s_silu, 1)

                def body(g, b, turn):
                    pe.wait_ge(s_row, g + 1)
                    for i in range(2):
                        slot = 2 * b + i
                        pe.wait_ge(s_loaded[slot], turn * 16 + 16)
                        for k in range(half):
                            ins = nc.tensor.matmul(acc[0:n, b, :], act_c[:, i * half + k, :], wt[:, slot, k, :],
                                                   start=(i == 0 and k == 0), stop=(i == 1 and k == half - 1))
                        ins.then_inc(s_used, 1)
                each_chunk(pe, 0, groups, 2, body)
                pe.wait_ge(s_row, groups + 2)
                for m in range(6 * KD):
                    ins = nc.tensor.transpose(cols[:, m, :], rows[:, m // 4, m % 4 * P:(m % 4 + 1) * P], ident[0:n, 0:n])
                ins.then_inc(s_cols, 1)

            @block.scalar
            def _(act):
                nc.scalar.activation(act_c[:], c, ACT.Silu).then_inc(s_silu, 1)
                act.sem_inc(s_row, 2)

                def body(g, b, turn):
                    act.wait_ge(s_used, g * 2 + 2)
                    nc.scalar.activation(rows[:, bass.ds(g, 1), :], acc[0:n, b:b + 1, :], ACT.Copy).then_inc(s_row, 1)
                each_chunk(act, 0, groups, 2, body)

            @block.vector
            def _(dve):
                dve.wait_ge(s_cols, 1)
                nc.vector.tensor_tensor(mods[:], cols[:], bcast(bias, n), ALU.add).then_inc(s_bias, 1)
                dve.wait_ge(s_bias, 1)
                for first in (KD, 4 * KD):
                    nc.vector.tensor_scalar(mods[:, first:first + KD, :], mods[:, first:first + KD, :], 1.0, None, ALU.add)


def conv_ffn(nc, name, pair, w_up, conv, w_down, z, gate):
    with Stage(nc, name) as st:
        hidden_pair = st.sb("hidden_hi", [P, KF, T], F32R), st.sb("hidden_lo", [P, KF, T], F32R)
        with Stage(nc, name + "_up") as up:
            hidden = up.sb("hidden", [P, KF, T])
            raw = up.sb("raw", [P, 4, KD * P])
            w = up.sb("hi", [P, 4, KD * P], F32R), up.sb("lo", [P, 4, KD * P], F32R)
            acc = up.ps("acc", [P, 4, 512])
            ubuf = up.sb("u", [P, 2, T + 2])
            cbuf, sbuf = up.sb("c", [P, 2, T]), up.sb("s", [P, 2, T])
            s_loaded = [up.sem(f"loaded{r}") for r in range(4)]
            s_hi, s_lo, s_summed, s_taken, s_zero = (up.sem(n) for n in ("hi", "lo", "summed", "taken", "zero"))
            s_u, s_tap, s_silu, s_hidden, s_hidden_hi = (up.sem(n) for n in ("u", "tap", "silu", "hidden", "hidden_hi"))
            with nc.Block() as block:
                @block.sync
                def _(sp):
                    def fetch(m, slot, turn):
                        if not isinstance(m, int) or m >= 4:
                            sp.wait_ge(s_lo, m - 3)
                        sp.dma_start(raw[:, slot, :], w_up[bass.ds(m, 1)].rearrange("a p c -> p (a c)")).then_inc(s_loaded[slot], 16)
                    for m in range(4):
                        fetch(m, m, 0)
                    each_chunk(sp, 4, 2 * KF - 4, 4, fetch)

                @block.tensor
                def _(pe):
                    pe.sem_inc(s_summed, 4)

                    def body(m, slot, turn):
                        pe.wait_ge(s_lo, m + 1)
                        pe.wait_ge(s_taken, m + 1)
                        for k in range(KD):
                            ins = products(nc, acc[:, slot, 0:T], part(w, slice(None), slot, slice(k * P, (k + 1) * P)),
                                           part(pair, slice(None), k), start=(k == 0), stop=(k == KD - 1))
                        ins.then_inc(s_summed, 1)
                    each_chunk(pe, 0, 2 * KF, 4, body)

                @block.scalar
                def _(act):
                    act.sem_inc(s_taken, 4)
                    act.wait_ge(s_zero, 1)

                    def hi(m, slot, turn):
                        act.wait_ge(s_loaded[slot], turn * 16 + 16)
                        act.wait_ge(s_summed, m + 1)
                        nc.scalar.activation(w[0][:, slot, :], raw[:, slot, :], ACT.Copy).then_inc(s_hi, 1)

                    def body(f, b, turn, more=True):
                        act.wait_ge(s_summed, f * 2 + 5)
                        act.wait_ge(s_tap, f * 3 + 3)
                        nc.scalar.activation(ubuf[:, b, 2:2 + T], acc[:, 2 * b, 0:T], ACT.Copy).then_inc(s_u, 1)
                        if more:
                            hi(f * 2 + 4, 2 * b, turn + 1)
                            hi(f * 2 + 5, 2 * b + 1, turn + 1)
                        act.wait_ge(s_u, f + 1)
                        act.sem_inc(s_taken, 1)
                        act.wait_ge(s_tap, f * 3 + 9)
                        nc.scalar.activation(sbuf[:, b, :], cbuf[:, b, :], ACT.Silu).then_inc(s_silu, 1)
                        act.wait_ge(s_hidden, f + 1)
                        act.sem_inc(s_taken, 1)
                        nc.scalar.activation(hidden_pair[0][:, bass.ds(f, 1), :], hidden[:, bass.ds(f, 1), :],
                                             ACT.Copy).then_inc(s_hidden_hi, 1)
                    for m in range(4):
                        hi(m, m, 0)
                    each_chunk(act, 0, KF - 2, 2, body)
                    for f in (KF - 2, KF - 1):
                        body(f, f % 2, f // 2, more=False)

                @block.vector
                def _(dve):
                    nc.vector.memset(ubuf[:], 0.0).then_inc(s_zero, 1)
                    dve.sem_inc(s_tap, 6)

                    def lo(m, slot):
                        dve.wait_ge(s_hi, m + 1)
                        nc.vector.tensor_tensor(w[1][:, slot, :], raw[:, slot, :], w[0][:, slot, :].bitcast(F32),
                                                ALU.subtract).then_inc(s_lo, 1)

                    def hidden_lo(f):
                        dve.wait_ge(s_hidden_hi, f + 1)
                        nc.vector.tensor_tensor(hidden_pair[1][:, bass.ds(f, 1), :], hidden[:, bass.ds(f, 1), :],
                                                hidden_pair[0][:, bass.ds(f, 1), :].bitcast(F32), ALU.subtract)

                    def body(f, b, turn, more=True):
                        dve.wait_ge(s_u, f + 1)
                        nc.vector.tensor_scalar(cbuf[:, b, :], ubuf[:, b, 0:T], conv[:, bass.ds(f, 1), 0],
                                                conv[:, bass.ds(f, 1), 3], ALU.mult, ALU.add).then_inc(s_tap, 1)
                        for j in (1, 2):
                            dve.wait_ge(s_tap, f * 3 + 6 + j)
                            nc.vector.scalar_tensor_tensor(cbuf[:, b, :], ubuf[:, b, j:j + T], conv[:, bass.ds(f, 1), j],
                                                           cbuf[:, b, :], ALU.mult, ALU.add).then_inc(s_tap, 1)
                        if more:
                            lo(f * 2 + 4, 2 * b)
                            lo(f * 2 + 5, 2 * b + 1)
                        if not isinstance(f, int) or f >= 1:
                            hidden_lo(f - 1)
                        dve.wait_ge(s_silu, f + 1)
                        dve.wait_ge(s_summed, f * 2 + 6)
                        nc.vector.tensor_tensor(hidden[:, bass.ds(f, 1), :], sbuf[:, b:b + 1, :],
                                                acc[:, 2 * b + 1:2 * b + 2, 0:T], ALU.mult).then_inc(s_hidden, 1)
                    for m in range(4):
                        lo(m, m)
                    body(0, 0, 0)
                    body(1, 1, 0)
                    with dve.Fori(1, KF // 2 - 1) as i:
                        for b in range(2):
                            body(i * 2 + b, b, i)
                    for f in (KF - 2, KF - 1):
                        body(f, f % 2, None, more=False)
                    hidden_lo(KF - 1)
        project(nc, name + "_down", w_down, KF, hidden_pair, T, [(KD, gate_to(nc, z, gate))])


def decayed_scores(nc, name, q, k, directions, masks, at, off, ctx=None):
    with Stage(nc, name) as st:
        nd, last = len(directions), LEVELS + 1 + (ctx is not None)
        qd, kd = st.sb("qd", [P, 2, H, T]), st.sb("kd", [P, 2, H, T])
        near, far, exp_near, exp_far = (st.sb(n, [P, H, T]) for n in ("near", "far", "exp_near", "exp_far"))
        zeros = st.sb("zeros", [P, T])
        acc = st.ps("acc", [P, 2, H * NT, P])
        ctx_acc = st.ps("ctx_acc", [P, 2, H, T]) if ctx else None
        s_init, s_ready, s_scored, s_kept, s_exp, s_grown = (
            st.sem(n) for n in ("init", "ready", "scored", "kept", "exp", "grown"))
        plan = [(0, 0)] + [(d, level) for d in range(nd) for level in range(1, last + 1)]
        grown = lambda d, level: 2 * (d * last + level)
        kept = lambda n: sum(level <= LEVELS + 1 for _, level in plan[:n + 1])

        def halves(ap, size):
            return ap.rearrange("p h (b c s) -> p (h b) c s", c=2, s=size)

        def sides(d):
            return (0, 1) if directions[d][1] else (1, 0)

        with nc.Block() as block:
            @block.vector
            def _(dve):
                init = Steps(dve, s_init)
                init.done(nc.vector.memset(at, 0.0))
                init.done(nc.vector.memset(zeros[:], 0.0))
                init.done(nc.vector.memset(qd[:, 1], 0.0))
                init.link(nc.vector.memset(kd[:, 1], 0.0))
                nc.vector.tensor_scalar(qd[:, 0], q, float(nd), None, ALU.mult).then_inc(s_ready, 1)
                nc.vector.tensor_copy(kd[:, 0], k).then_inc(s_ready, 1)

                def keep(n):
                    d, level = plan[n]
                    if level > LEVELS + 1:
                        return
                    dve.wait_ge(s_scored, n + 1)
                    if level == LEVELS + 1:
                        ins = nc.vector.tensor_copy(off[d], acc[:, n % 2, 0:H, :])
                    else:
                        if n >= 1:
                            dve.wait_ge(s_kept, kept(n - 1))
                        ins = nc.vector.copy_predicated(at, over(masks[d][:, level, :], H * NT), acc[:, n % 2])
                    ins.then_inc(s_kept, 1)

                for n, (d, level) in enumerate(plan):
                    if n == 0:
                        continue
                    g, backwards = directions[d]
                    tc, sc = sides(d)
                    if level == 1:
                        nc.vector.tensor_copy(near[:], g).then_inc(s_grown, 1)
                        nc.vector.memset(far[:], 0.0).then_inc(s_grown, 1)
                        dve.wait_ge(s_grown, grown(d, 1))
                    b, size = n % 2, 2 ** (level - 1)
                    dve.wait_ge(s_exp, 2 * n)
                    if n >= 2:
                        dve.wait_ge(s_scored, n - 1)
                        dve.wait_ge(s_ready, 2 * n)
                    if level <= LEVELS + 1:
                        nc.vector.tensor_tensor(halves(qd[:, b], size)[:, :, tc], halves(q, size)[:, :, tc],
                                                halves(exp_near[:], size)[:, :, tc], ALU.mult).then_inc(s_ready, 1)
                        nc.vector.tensor_tensor(halves(kd[:, b], size)[:, :, sc], halves(k, size)[:, :, sc],
                                                halves(exp_far[:], size)[:, :, sc], ALU.mult).then_inc(s_ready, 1)
                    else:
                        nc.vector.tensor_tensor(qd[:, b], q, exp_near[:], ALU.mult).then_inc(s_ready, 1)
                        nc.vector.tensor_tensor(kd[:, b], ctx[0], exp_far[:], ALU.mult).then_inc(s_ready, 1)
                    if level < last:
                        near_h, far_h = halves(near[:], size), halves(far[:], size)
                        edge = 0 if backwards else size - 1
                        blocks = H * T // (2 * size)
                        total = lambda c: near_h[:, :, c, edge:edge + 1].broadcast_to([P, blocks, size])
                        if level <= LEVELS:
                            nc.vector.tensor_tensor(far_h[:, :, sc], far_h[:, :, sc], total(tc),
                                                    ALU.add).then_inc(s_grown, 1)
                        else:
                            cg = ctx[1][d]
                            init.link(nc.vector.memset(far[:], 0.0))
                            for h in range(H):
                                out, src = ((far[:, h, 1:T], cg[:, h, 0:T - 1]) if backwards else
                                            (far[:, h, T - 2::-1], cg[:, h, T - 1:0:-1]))
                                ins = nc.vector.tensor_tensor_scan(out, zeros[:, 0:T - 1], src, 0.0, ALU.add, ALU.add)
                            ins.then_inc(s_grown, 1)
                        dve.wait_ge(s_grown, grown(d, level) + 1)
                        nc.vector.tensor_tensor(near_h[:, :, tc], near_h[:, :, tc], total(sc),
                                                ALU.add).then_inc(s_grown, 1)
                        dve.wait_ge(s_grown, grown(d, level + 1))
                    keep(n - 1)
                keep(len(plan) - 1)

            @block.scalar
            def _(act):
                for n, (d, level) in enumerate(plan):
                    if n == 0:
                        continue
                    tc, sc = sides(d)
                    act.wait_ge(s_grown, grown(d, level))
                    act.wait_ge(s_ready, 2 * n)
                    if level <= LEVELS + 1:
                        size = 2 ** (level - 1)
                        pairs = [(halves(a[:], size)[:, :, c], halves(b[:], size)[:, :, c])
                                 for a, b, c in ((exp_near, near, tc), (exp_far, far, sc))]
                    else:
                        pairs = [(exp_near[:], near[:]), (exp_far[:], far[:])]
                    for out, src in pairs:
                        nc.scalar.activation(out, src, ACT.Exp).then_inc(s_exp, 1)
                if ctx:
                    act.wait_ge(s_scored, len(plan))
                    for i in range(2):
                        nc.scalar.activation(ctx[2][:, i], ctx_acc[:, i], ACT.Copy)

            @block.tensor
            def _(pe):
                for n, (d, level) in enumerate(plan):
                    b = n % 2
                    pe.wait_ge(s_ready, 2 * n + 2)
                    if n >= 2:
                        pe.wait_ge(s_kept, kept(n - 2))
                    for h in range(H):
                        if level <= LEVELS:
                            for i in range(NT):
                                tile = slice(i * P, (i + 1) * P)
                                ins = nc.tensor.matmul(acc[:, b, h * NT + i, :], kd[:, b, h, tile], qd[:, b, h, tile],
                                                       start=True, stop=True)
                        elif level == LEVELS + 1:
                            tc, sc = sides(d)
                            ins = nc.tensor.matmul(acc[:, b, h, :], kd[:, b, h, sc * P:(sc + 1) * P],
                                                   qd[:, b, h, tc * P:(tc + 1) * P], start=True, stop=True)
                        else:
                            for i in range(2):
                                ins = nc.tensor.matmul(ctx_acc[:, i, h, :], kd[:, b, h, i * P:(i + 1) * P], qd[:, b, h, :],
                                                       start=(d == 0 and h % 2 == 0), stop=(d == nd - 1),
                                                       skip_group_check=True)
                    ins.then_inc(s_scored, 1)


def weighted_values(nc, name, v, width, at, off, out, ctx=None):
    with Stage(nc, name) as st:
        chunks = H * width // P
        acc = st.ps("acc", [P, chunks, T])
        s_summed = st.sem("summed")
        with nc.Block() as block:
            @block.tensor
            def _(pe):
                for c in range(chunks):
                    h, cols = c * P // width, slice(c * P, (c + 1) * P)
                    for i in range(NT):
                        tile = slice(i * P, (i + 1) * P)
                        terms = [(v[i], at[:, h * NT + i, :])]
                        if i == 1:
                            terms.append((v[0], off[0][:, h, :]))
                        elif len(off) > 1:
                            terms.append((v[1], off[1][:, h, :]))
                        if ctx:
                            terms += [(ctx[0][j], ctx[1][:, j, h, tile]) for j in range(2)]
                        for n, (value, score) in enumerate(terms):
                            ins = nc.tensor.matmul(acc[:, c, tile], value[:, cols], score,
                                                   start=(n == 0), stop=(n == len(terms) - 1))
                    ins.then_inc(s_summed, 1)

            @block.scalar
            def _(act):
                for c in range(chunks):
                    act.wait_ge(s_summed, c // 2 * 2 + 2)
                    nc.scalar.activation(out[:, c, :], acc[:, c, :], ACT.Copy)


def head_norm(nc, name, o, y, gate, weight, per_head, t, eps, mean_of_p):
    with Stage(nc, name) as st:
        chunks = o.shape[1]
        heads = chunks // per_head
        in_bank = 512 // t
        sq, rstd = st.sb("sq", [P, 2, t]), st.sb("rstd", [P, heads, t])
        acc = st.ps("acc", [P, heads, t])
        s_squared, s_mean, s_step, s_root, s_weighted = (st.sem(n) for n in ("squared", "mean", "step", "root", "weighted"))
        with nc.Block() as block:
            @block.scalar
            def _(act):
                for c in range(chunks):
                    if c >= 2:
                        act.wait_ge(s_mean, c - 1)
                    nc.scalar.activation(sq[:, c % 2, :], o[:, c, :], ACT.Square).then_inc(s_squared, 1)
                act.wait_ge(s_step, 2 * heads)
                nc.scalar.activation(rstd[:], rstd[:], ACT.Sqrt).then_inc(s_root, 1)

            @block.tensor
            def _(pe):
                for c in range(chunks):
                    pe.wait_ge(s_squared, c + 1)
                    nc.tensor.matmul(acc[:, c // per_head, :], mean_of_p, sq[:, c % 2, :], start=(c % per_head == 0),
                                     stop=(c % per_head == per_head - 1)).then_inc(s_mean, 1)

            @block.vector
            def _(dve):
                step = Steps(dve, s_step)
                for h in range(heads):
                    dve.wait_ge(s_mean, (h // in_bank + 1) * in_bank * per_head)
                    step.link(nc.vector.tensor_scalar(rstd[:, h, :], acc[:, h, :], 1.0 / per_head, eps, ALU.mult, ALU.add))
                    step.done(nc.vector.reciprocal(rstd[:, h, :], rstd[:, h, :]))
                for c in range(chunks):
                    nc.vector.scalar_tensor_tensor(y[:, c, :], o[:, c, :], weight(c), gate[:, c, :],
                                                   ALU.mult, ALU.mult).then_inc(s_weighted, 1)
                dve.wait_ge(s_root, 1)
                for c in range(chunks):
                    dve.wait_ge(s_weighted, c + 1)
                    nc.vector.tensor_tensor(y[:, c, :], y[:, c, :], rstd[:, c // per_head, :], ALU.mult)


def rope(nc, name, qk, perm_t, cos, sin):
    with Stage(nc, name) as st:
        chunks = qk.shape[1]
        acc = st.ps("acc", [P, chunks + 1, T])
        turned = st.sb("turned", [P, chunks, T])
        s_perm, s_turned, s_cos = st.sem("perm"), st.sem("turned"), st.sem("cos")
        with nc.Block() as block:
            @block.tensor
            def _(pe):
                for c in range(chunks):
                    nc.tensor.matmul(acc[:, c, :], perm_t, qk[:, c, :], start=True, stop=True).then_inc(s_perm, 1)

            @block.vector
            def _(dve):
                dve.wait_ge(s_perm, chunks)
                nc.vector.tensor_tensor(turned[:], acc[:, 0:chunks, :], over(sin, chunks), ALU.mult).then_inc(s_turned, 1)
                nc.vector.tensor_tensor(qk, qk, over(cos, chunks), ALU.mult).then_inc(s_cos, 1)
                dve.wait_ge(s_turned, 1)
                dve.wait_ge(s_cos, 1)
                nc.vector.tensor_tensor(qk, qk, turned[:], ALU.add)


def rope_tables(nc, name, positions, inv_freq, cos, sin):
    with Stage(nc, name) as st:
        pos, ang, turns, cosine = st.sb("pos", [P, T]), st.sb("ang", [P, T]), st.sb("turns", [P, T]), st.sb("cosine", [P, T])
        s_step = st.sem("step")
        with nc.Block() as block:
            @block.vector
            def _(dve):
                step = Steps(dve, s_step)
                step.link(nc.vector.tensor_copy(pos[:], positions))
                step.link(nc.vector.tensor_scalar(ang[:], pos[:], inv_freq, None, ALU.mult))
                step.link(nc.vector.tensor_scalar(turns[:], ang[:], float(0.5 / np.pi), ROUND, ALU.mult, ALU.add))
                step.link(nc.vector.tensor_scalar(turns[:], turns[:], ROUND, None, ALU.subtract))
                for part in (EVEN_PI_1, EVEN_PI_2, EVEN_PI_3):
                    step.link(nc.vector.scalar_tensor_tensor(ang[:], turns[:], -float(part), ang[:], ALU.mult, ALU.add))
                step.link(nc.vector.tensor_scalar(cosine[:], ang[:], float(np.pi / 2), None, ALU.add))
                step.link(nc.vector.tensor_scalar(turns[:], cosine[:], float(np.pi), float(-2 * np.pi), ALU.is_gt, ALU.mult))
                step.link(nc.vector.tensor_tensor(cosine[:], cosine[:], turns[:], ALU.add))
                for a in (ang, cosine):
                    step.link(nc.vector.tensor_scalar(a[:], a[:], 3.1415925, -3.1415925, ALU.min, ALU.max))

            @block.scalar
            def _(act):
                act.wait_ge(s_step, 12)
                nc.scalar.activation(sin, ang[:], ACT.Sin)
                nc.scalar.activation(cos, cosine[:], ACT.Sin)


def attention(nc, name, tiles, sinks, o, ident):
    with Stage(nc, name) as st:
        pair = 2
        scores = st.ps("scores", [P, 2, pair, 512])
        turned = st.ps("turned", [P, pair, 4, P])
        values, back = st.ps("values", [P, 512]), st.ps("back", [P, GQA, P])
        p, pt = st.sb("p", [P, 2, pair, 512]), st.sb("pt", [P, 2, pair, 4, P])
        m, minus_m = st.sb("m", [P, 2, pair]), st.sb("minus_m", [P, 2, pair])
        sink, denom = st.sb("sink", [P, 3, pair]), st.sb("denom", [P, 3, pair])
        o_tok = st.sb("o_tok", [P, 2, P])
        (s_scores, s_step, s_arg, s_exp, s_turned, s_pt, s_values, s_div, s_o, s_back, s_out) = (
            st.sem(n) for n in ("scores", "step", "arg", "exp", "turned", "pt", "values", "div", "o", "back", "out"))
        per_tile = A_HEADS // pair
        items = [(i, g, c) for i in range(len(tiles)) for g in range(2) for c in range(0, GQA, pair)]
        EXPS = pair + 1
        steps = range(-1, len(items) + 4)
        live = lambda n: 0 <= n < len(items)

        with nc.Block() as block:
            @block.tensor
            def _(pe):
                def score(n):
                    i, g, first = items[n]
                    q, ks, vs, mask, cols = tiles[i]
                    rows = slice(g * A_DIM, (g + 1) * A_DIM)
                    if n >= 2:
                        pe.wait_ge(s_exp, EXPS * (n - 1))
                    for c in range(pair):
                        at = 0
                        for kt in ks:
                            w = kt.shape[1]
                            ins = nc.tensor.matmul(scores[:, n % 2, c, at:at + w], q(first + c)[rows], kt[rows],
                                                   start=True, stop=True)
                            at += w
                    ins.then_inc(s_scores, 1)

                def turn(n):
                    vs = tiles[items[n][0]][2]
                    pe.wait_ge(s_exp, EXPS * (n + 1))
                    if n >= 1:
                        pe.wait_ge(s_pt, n)
                    for c in range(pair):
                        for j in range(len(vs)):
                            ins = nc.tensor.transpose(turned[:, c, j, :], p[:, n % 2, c, j * P:(j + 1) * P], ident)
                    ins.then_inc(s_turned, 1)

                def value(n):
                    i, g, first = items[n]
                    vs = tiles[i][2]
                    pe.wait_ge(s_pt, n + 1)
                    if n >= 1:
                        pe.wait_ge(s_o, n)
                    for c in range(pair):
                        for j, v in enumerate(vs):
                            ins = nc.tensor.matmul(values[:, c * A_DIM:(c + 1) * A_DIM], pt[:, n % 2, c, j, :], v[:, g, :],
                                                   start=(j == 0), stop=(j == len(vs) - 1))
                    ins.then_inc(s_values, 1)

                def features_first(n):
                    pe.wait_ge(s_o, n + 1)
                    if n % per_tile == 0 and n:
                        pe.wait_ge(s_out, n // per_tile)
                    nc.tensor.transpose(back[:, n % per_tile, :], o_tok[:, n % 2, :], ident).then_inc(s_back, 1)

                for n in steps:
                    for work, item in ((score, n + 1), (turn, n), (value, n - 1), (features_first, n - 2)):
                        if live(item):
                            work(item)

            @block.vector
            def _(dve):
                step = Steps(dve, s_step)

                def maximum(n):
                    i, g, first = items[n]
                    q, ks, vs, mask, cols = tiles[i]
                    w, b = len(vs) * P, n % 2
                    sk = sinks[:, g * GQA + first:g * GQA + first + pair]
                    dve.wait_ge(s_scores, n + 1)
                    if mask is not None:
                        if n >= 2:
                            dve.wait_ge(s_turned, n - 1)
                        step.link(nc.vector.scalar_tensor_tensor(p[:, b, :, 0:w], scores[:, b, :, 0:w], A_DIM ** -0.5,
                                                                 over(mask, pair), ALU.mult, ALU.add))
                    src = scores if mask is None else p
                    step.link(nc.vector.tensor_reduce(m[:, b], src[:, b, :, 0:w], AX.X, ALU.max))
                    step.link(nc.vector.scalar_tensor_tensor(m[:, b], m[:, b], A_DIM ** -0.5 if mask is None else 1.0, sk,
                                                             ALU.mult, ALU.max))
                    if n >= 2:
                        dve.wait_ge(s_exp, EXPS * (n - 1))
                    nc.vector.tensor_scalar(minus_m[:, b], m[:, b], -1.0, None, ALU.mult).then_inc(s_arg, 1)
                    nc.vector.tensor_tensor(sink[:, n % 3], sk, m[:, b], ALU.subtract).then_inc(s_arg, 1)

                def divide(n):
                    b = n % 3
                    dve.wait_ge(s_exp, EXPS * (n + 1))
                    nc.vector.tensor_tensor(denom[:, b], denom[:, b], sink[:, b], ALU.add).then_inc(s_div, 1)
                    dve.wait_ge(s_div, 2 * n + 1)
                    nc.vector.reciprocal(denom[:, b], denom[:, b]).then_inc(s_div, 1)
                    dve.wait_ge(s_div, 2 * n + 2)
                    dve.wait_ge(s_values, n + 1)
                    if n >= 2:
                        dve.wait_ge(s_back, n - 1)
                    nc.vector.tensor_tensor(o_tok[:, n % 2].rearrange("p (c e) -> p c e", c=pair),
                                            values[:, 0:pair * A_DIM].rearrange("p (c e) -> p c e", c=pair),
                                            bcast(denom[:, b], A_DIM), ALU.mult).then_inc(s_o, 1)

                for n in steps:
                    for work, item in ((maximum, n), (divide, n - 2)):
                        if live(item):
                            work(item)

            @block.scalar
            def _(act):
                def exponentials(n):
                    mask, w, b = tiles[items[n][0]][3], len(tiles[items[n][0]][2]) * P, n % 2
                    act.wait_ge(s_arg, 2 * n + 2)
                    if n >= 2:
                        act.wait_ge(s_turned, n - 1)
                    if n >= 3:
                        act.wait_ge(s_o, n - 2)
                    src, scale = (scores, A_DIM ** -0.5) if mask is None else (p, 1.0)
                    for c in range(pair):
                        nc.scalar.activation(p[:, b, c, 0:w], src[:, b, c, 0:w], ACT.Exp, bias=minus_m[:, b, c:c + 1],
                                             scale=scale, accum_out=denom[:, n % 3, c:c + 1]).then_inc(s_exp, 1)
                    nc.scalar.activation(sink[:, n % 3], sink[:, n % 3], ACT.Exp).then_inc(s_exp, 1)

                def copy(n):
                    vs = tiles[items[n][0]][2]
                    act.wait_ge(s_turned, n + 1)
                    if n >= 2:
                        act.wait_ge(s_values, n - 1)
                    nc.scalar.activation(pt[:, n % 2, :, 0:len(vs), :], turned[:, :, 0:len(vs), :], ACT.Copy).then_inc(s_pt, 1)

                def store_tile(n):
                    if n % per_tile == per_tile - 1:
                        act.wait_ge(s_back, n + 1)
                        nc.scalar.activation(o[:, :, tiles[items[n][0]][4]], back[:], ACT.Copy).then_inc(s_out, 1)

                for n in steps:
                    for work, item in ((exponentials, n), (copy, n - 1), (store_tile, n - 3)):
                        if live(item):
                            work(item)


def pool_mixer(nc, name, h, w_pool, scale, inv_count, z, gate, scaled):
    with Stage(nc, name) as st:
        pad = max(POOL_WINDOWS)
        a, b = st.sb("a", [P, KD, pad + T]), st.sb("b", [P, KD, pad + T])
        w = st.sb("w", [P, KD, 2, P])
        gs = st.sb("gs", [P, KD])
        acc = st.ps("acc", [P, KD, T])
        s_loaded, s_step, s_summed = st.sem("loaded"), st.sem("step"), st.sem("summed")
        with nc.Block() as block:
            @block.sync
            def _(sp):
                sp.dma_start(w[:], w_pool).then_inc(s_loaded, 16)

            @block.vector
            def _(dve):
                step = Steps(dve, s_step)
                step.done(nc.vector.memset(a[:, :, 0:pad], 0.0))
                step.done(nc.vector.memset(b[:, :, 0:pad], 0.0))
                step.done(nc.vector.tensor_tensor(gs[:], gate[:, :, 0], scale, ALU.mult))
                step.link(nc.vector.tensor_copy(a[:, :, pad:], h))
                src, dst, size = a, b, 1
                for g, window in enumerate(POOL_WINDOWS):
                    ks = slice(2 * g, KD)
                    step.link(nc.vector.tensor_tensor(dst[:, ks, pad:], src[:, ks, pad:],
                                                      src[:, ks, pad - size:pad + T - size], ALU.add))
                    size *= 2
                    own = slice(2 * g, 2 * g + 2)
                    step.link(nc.vector.tensor_tensor(src[:, own, pad:], dst[:, own, pad:], over(inv_count[:, g, :], 2), ALU.mult))
                    step.link(nc.vector.tensor_tensor(h[:, own, :], src[:, own, pad:], h[:, own, :], ALU.subtract))
                    src, dst = dst, src
                dve.wait_ge(s_summed, 1)
                for m in range(KD):
                    nc.vector.scalar_tensor_tensor(z[:, m, :], acc[:, m, :], gs[:, m:m + 1], scaled[:, m, :],
                                                   ALU.mult, ALU.add)

            @block.tensor
            def _(pe):
                pe.wait_ge(s_loaded, 16)
                pe.wait_ge(s_step, 4 + 3 * len(POOL_WINDOWS))
                for m in range(KD):
                    for j in range(2):
                        ins = nc.tensor.matmul(acc[:, m, :], w[:, m, j, :], h[:, m // 2 * 2 + j, :], start=(j == 0), stop=(j == 1))
                ins.then_inc(s_summed, 1)


def log_sigmoid_rows(nc, name, h, w_gates, gate_b, rows, u_cols, ident):
    with Stage(nc, name) as st:
        acc = st.ps("acc", [P, 4, 512])
        cols = st.ps("cols", [P, 2, 4, H])
        gates = [[st.sb(f"gate{d}{i}", [H, 2 * T]) for i in range(2)] for d in range(2)]
        tmp = [[st.sb(f"tmp{d}{i}", [H, 2 * T]) for i in range(2)] for d in range(2)]
        u = [st.sb(f"u{d}", [H, 2 * T]) for d in range(2)]
        zeros = st.sb("zeros", [H, 2 * T])
        s_summed, s_step, s_act, s_u, s_cols = (st.sem(n) for n in ("summed", "step", "act", "u", "cols"))
        with nc.Block() as block:
            @block.tensor
            def _(pe):
                for n in range(4):
                    for k in range(KD):
                        ins = nc.tensor.matmul(acc[0:H, n, :], w_gates[:, k, n * H:(n + 1) * H], h[:, k, :],
                                               start=(k == 0), stop=(k == KD - 1))
                ins.then_inc(s_summed, 1)
                pe.wait_ge(s_u, 2)
                for d in range(2):
                    for i in range(4):
                        ins = nc.tensor.transpose(cols[:, d, i, :], u[d][:, i * P:(i + 1) * P], ident[0:H, 0:H])
                ins.then_inc(s_cols, 1)

            @block.vector
            def _(dve):
                step = Steps(dve, s_step)
                step.done(nc.vector.memset(zeros[:], 0.0))
                dve.wait_ge(s_summed, 1)
                for d in range(2):
                    for i in range(2):
                        n = 2 * d + i
                        step.link(nc.vector.tensor_scalar(gates[d][i][:], acc[0:H, n, :], gate_b[:, n:n + 1], None, ALU.add))
                    step.link(nc.vector.scalar_tensor_tensor(tmp[d][0][:], gates[d][1][:], -1.0, gates[d][1][:], ALU.mult, ALU.min))
                for d in range(2):
                    li, lf, cum, big = gates[d][0], gates[d][1], tmp[d][0], rows[d][0]
                    dve.wait_ge(s_act, 2 * d + 2)
                    step.link(nc.vector.scalar_tensor_tensor(lf[:], lf[:], 0.0, tmp[d][1][:], ALU.min, ALU.subtract))

                    def scan(out, src, op):
                        start = 0.0
                        for a in (0, T):
                            if d == 0:
                                o, s, end = out[:, a:a + T], src[:, a:a + T], out[:, T - 1:T]
                            else:
                                o = out[:, a + T - 1:(a - 1 if a else None):-1]
                                s, end = src[:, a + T - 1:(a - 1 if a else None):-1], out[:, 0:1]
                            step.link(nc.vector.tensor_tensor_scan(o, zeros[:, 0:T], s, start, ALU.add, op))
                            start = end
                    scan(cum, lf, ALU.add)
                    nc.vector.tensor_tensor(u[d][:], li[:], cum[:], ALU.subtract).then_inc(s_u, 1)
                    dve.wait_ge(s_u, d + 1)
                    scan(big, u[d], ALU.max)
                    step.link(nc.vector.tensor_tensor(rows[d][1][:], cum[:], big[:], ALU.add))
                dve.wait_ge(s_cols, 1)
                for d in range(2):
                    nc.vector.tensor_copy(u_cols[:, :, d, :], cols[:, d])

            @block.scalar
            def _(act):
                for d in range(2):
                    act.wait_ge(s_step, 4 + 3 * d)
                    nc.scalar.activation(tmp[d][1][:], tmp[d][0][:], ACT.Exp).then_inc(s_act, 1)
                    act.wait_ge(s_act, 2 * d + 1)
                    nc.scalar.activation(tmp[d][1][:], tmp[d][1][:], ACT.Ln, bias=1.0).then_inc(s_act, 1)


def mlstm(nc, name, q, k, v, rows, u_cols, masks, select, ones, out):
    with Stage(nc, name) as st:
        qk = st.ps("qk", [P, 3, 512])
        row = st.ps("row", [P, 2, 512])
        num, den = st.ps("num", [P, 512]), st.ps("den", [P, 512])
        w_all, w_lat = st.sb("w_all", [P, 2, 2 * T]), st.sb("w_lat", [P, 2, T])
        floor, part = st.sb("floor", [P, 2 * T]), st.sb("part", [P, 2 * T])
        s_qk, s_row, s_arg, s_exp, s_w, s_num, s_div, s_out = (
            st.sem(n) for n in ("qk", "row", "arg", "exp", "w", "num", "div", "out"))
        items = [(h, d) for h in range(H) for d in range(2)]
        EXPS = 7
        with nc.Block() as block:
            @block.tensor
            def _(pe):
                for n, (h, d) in enumerate(items):
                    if n >= 1:
                        pe.wait_ge(s_exp, EXPS * n)
                        pe.wait_ge(s_arg, 2 * n)
                    for i in range(2):
                        ins = nc.tensor.matmul(row[:, i, :], select[:, h, :], rows[d][i][:], start=True, stop=True)
                    ins.then_inc(s_row, 1)
                    if d == 0:
                        if n >= 1:
                            pe.wait_ge(s_w, 2 * n)
                        for s in range(2):
                            nc.tensor.matmul(qk[:, s, :], k[:, h, s * P:(s + 1) * P], q[:, h, :], start=True, stop=True)
                        for s in range(2):
                            ins = nc.tensor.matmul(qk[:, 2, s * T:(s + 1) * T], k[:, h, (s + 2) * P:(s + 3) * P],
                                                   q[:, h, T:], start=True, stop=True)
                        ins.then_inc(s_qk, 1)
                    pe.wait_ge(s_w, 2 * n + 2)
                    if n >= 1:
                        pe.wait_ge(s_out, n)
                    for acc, value in ((num, None), (den, ones)):
                        for s in range(2):
                            lhs = v[:, s, h * P:(h + 1) * P] if value is None else value
                            nc.tensor.matmul(acc[:], lhs, w_all[:, s, :], start=(s == 0), stop=False, skip_group_check=True)
                        for s in range(2):
                            lhs = v[:, s + 2, h * P:(h + 1) * P] if value is None else value
                            ins = nc.tensor.matmul(acc[:, T:], lhs, w_lat[:, s, :], start=False, stop=(s == 1),
                                                   skip_group_check=True)
                    ins.then_inc(s_num, 1)

            @block.vector
            def _(dve):
                for n, (h, d) in enumerate(items):
                    dve.wait_ge(s_row, n + 1)
                    if n >= 1:
                        dve.wait_ge(s_num, n)
                    nc.vector.tensor_tensor(w_all[:, :, 0:T], masks[:, d], over(row[:, 0, 0:T], 2), ALU.subtract).then_inc(s_arg, 1)
                    nc.vector.tensor_tensor(w_lat[:], masks[:, d], over(row[:, 0, T:], 2), ALU.subtract).then_inc(s_arg, 1)
                    dve.wait_ge(s_exp, EXPS * (n + 1))
                    dve.wait_ge(s_qk, h + 1)
                    nc.vector.scalar_tensor_tensor(w_all[:], qk[:, 0:2, :], P ** -0.5, w_all[:], ALU.mult, ALU.mult).then_inc(s_w, 1)
                    nc.vector.scalar_tensor_tensor(w_lat[:], qk[:, 2, :].rearrange("p (s t) -> p s t", s=2), P ** -0.5,
                                                   w_lat[:], ALU.mult, ALU.mult).then_inc(s_w, 1)
                    dve.wait_ge(s_num, n + 1)
                    nc.vector.tensor_tensor(floor[:], den[:], floor[:], ALU.max).then_inc(s_div, 1)
                    dve.wait_ge(s_div, 3 * n + 1)
                    nc.vector.scalar_tensor_tensor(floor[:], den[:], -1.0, floor[:], ALU.mult, ALU.max).then_inc(s_div, 1)
                    dve.wait_ge(s_div, 3 * n + 2)
                    nc.vector.reciprocal(floor[:], floor[:]).then_inc(s_div, 1)
                    dve.wait_ge(s_div, 3 * n + 3)
                    if d == 0:
                        nc.vector.tensor_tensor(out[:, h, :], num[:], floor[:], ALU.mult).then_inc(s_out, 1)
                    else:
                        nc.vector.tensor_tensor(part[:], num[:], floor[:], ALU.mult).then_inc(s_out, 1)
                        dve.wait_ge(s_out, n + 1)
                        nc.vector.tensor_tensor(out[:, h, :], out[:, h, :], part[:], ALU.add)

            @block.scalar
            def _(act):
                for n, (h, d) in enumerate(items):
                    u = lambda s: u_cols[:, s, d, h:h + 1]
                    act.wait_ge(s_row, n + 1)
                    if n >= 1:
                        act.wait_ge(s_num, n)
                        act.wait_ge(s_out, n)
                    nc.scalar.activation(floor[:], row[:, 1, :], ACT.Exp, scale=-1.0).then_inc(s_exp, 1)
                    act.wait_ge(s_arg, 2 * n + 2)
                    for s in range(2):
                        nc.scalar.activation(w_all[:, s, T:], row[:, 0, T:], ACT.Exp, bias=u(s), scale=-1.0).then_inc(s_exp, 1)
                    for s in range(2):
                        nc.scalar.activation(w_all[:, s, 0:T], w_all[:, s, 0:T], ACT.Exp, bias=u(s)).then_inc(s_exp, 1)
                        nc.scalar.activation(w_lat[:, s, :], w_lat[:, s, :], ACT.Exp, bias=u(s + 2)).then_inc(s_exp, 1)


def gla_decays(nc, name, low, gate_up, gate_b, la):
    with Stage(nc, name) as st:
        acc = st.ps("acc", [P, H, 2 * T])
        z, e = st.sb("z", [P, H, 2 * T]), st.sb("e", [P, H, 2 * T])
        s_summed, s_z, s_abs, s_log, s_la = (st.sem(n) for n in ("summed", "z", "abs", "log", "la"))
        with nc.Block() as block:
            @block.tensor
            def _(pe):
                for d in range(2):
                    if d:
                        pe.wait_ge(s_z, d * H)
                    for h in range(H):
                        nc.tensor.matmul(acc[:, h, :], gate_up[:, d, h * P:(h + 1) * P], low[:, d, :],
                                         start=True, stop=True).then_inc(s_summed, 1)

            @block.vector
            def _(dve):
                for d in range(2):
                    if d:
                        dve.wait_ge(s_la, 2)
                    for h in range(H):
                        dve.wait_ge(s_summed, d * H + h + 1)
                        nc.vector.tensor_scalar(z[:, h, :], acc[:, h, :], gate_b[:, d, h:h + 1], None, ALU.add).then_inc(s_z, 1)
                    dve.wait_ge(s_z, (d + 1) * H)
                    nc.vector.scalar_tensor_tensor(e[:], z[:], -1.0, z[:], ALU.mult, ALU.min).then_inc(s_abs, 1)
                    dve.wait_ge(s_log, 2 * d + 2)
                    nc.vector.scalar_tensor_tensor(z[:], z[:], 0.0, e[:], ALU.min, ALU.subtract).then_inc(s_abs, 1)
                    dve.wait_ge(s_abs, 2 * d + 2)
                    for segment in range(2):
                        nc.vector.tensor_scalar(la[d][segment], z[:, :, segment * T:(segment + 1) * T], 1.0 / 16, None,
                                                ALU.mult).then_inc(s_la, 1)

            @block.scalar
            def _(act):
                for d in range(2):
                    act.wait_ge(s_abs, 2 * d + 1)
                    nc.scalar.activation(e[:], e[:], ACT.Exp).then_inc(s_log, 1)
                    act.wait_ge(s_log, 2 * d + 1)
                    nc.scalar.activation(e[:], e[:], ACT.Ln, bias=1.0).then_inc(s_log, 1)


def select_experts(nc, name, q, keys, tile, chosen, iota, ident):
    with Stage(nc, name) as st:
        n_half = 2 * PEER_H
        acc = st.ps("acc", [P, n_half, N_KEYS])
        turned = st.ps("turned", [P, 3, P])
        s, s2 = st.sb("s", [P, n_half, N_KEYS]), st.sb("s2", [P, n_half, N_KEYS])
        top, index = st.sb("top", [P, n_half, TOPK]), st.sb("index", [P, n_half, TOPK], U32)
        key_no = st.sb("key_no", [P, n_half, TOPK])
        cand, cand2 = (st.sb(n, [P, PEER_H, TOPK * TOPK]) for n in ("cand", "cand2"))
        best, pos = st.sb("best", [P, PEER_H, TOPK]), st.sb("pos", [P, PEER_H, TOPK], U32)
        part, part_f = st.sb("part", [P, 2, P], U32), st.sb("part_f", [P, 2, P])
        hit = st.sb("hit", [P, P, TOPK])
        pick = st.sb("pick", [P, 3, P])
        total = st.sb("total", [P, PEER_H])
        s_scores, s_copied, s_step, s_cmp, s_exp, s_turned = (st.sem(n) for n in ("scores", "copied", "step", "cmp", "exp", "turned"))
        cols = slice(tile * P, (tile + 1) * P)

        with nc.Block() as block:
            @block.tensor
            def _(pe):
                for m in range(n_half):
                    nc.tensor.matmul(acc[:, m, :], q[:, m, cols], keys[:, m, :], start=True, stop=True).then_inc(s_scores, 1)
                pe.wait_ge(s_cmp, 1)
                for i in range(3):
                    ins = nc.tensor.transpose(turned[:, i, :], pick[:, i, :], ident)
                ins.then_inc(s_turned, 1)

            @block.scalar
            def _(act):
                for m in range(0, n_half, 4):
                    act.wait_ge(s_scores, m + 4)
                    nc.scalar.activation(s[:, m:m + 4, :], acc[:, m:m + 4, :], ACT.Copy).then_inc(s_copied, 1)
                act.wait_ge(s_exp, 1)
                nc.scalar.activation(best[:], best[:], ACT.Exp).then_inc(s_exp, 1)
                act.wait_ge(s_turned, 1)
                for i in range(3):
                    nc.scalar.activation(chosen[i][:, cols], turned[:, i, :], ACT.Copy)

            @block.vector
            def _(dve):
                step = Steps(dve, s_step)

                def best16(values, rest, groups, out, where, ready):
                    for m in range(groups):
                        ready(m)
                        step.done(nc.vector.max(out[:, m, 0:8], values[:, m, :]))
                    step.wait()
                    for m in range(groups):
                        step.done(nc.vector.max_index(where[:, m, 0:8], out[:, m, 0:8], values[:, m, :]))
                        step.done(nc.vector.match_replace(rest[:, m, :], out[:, m, 0:8], values[:, m, :], float(-3.4e38)))
                    step.wait()
                    for m in range(groups):
                        step.done(nc.vector.max(out[:, m, 8:16], rest[:, m, :]))
                    step.wait()
                    for m in range(groups):
                        step.done(nc.vector.max_index(where[:, m, 8:16], out[:, m, 8:16], rest[:, m, :]))
                    step.wait()

                best16(s, s2, n_half, top, index, lambda m: dve.wait_ge(s_copied, m // 4 + 1))
                step.done(nc.vector.tensor_copy(key_no[:], index[:]))
                pair = top[:].rearrange("p (h c) r -> p h c r", c=2)
                first = pair[:, :, 0, :].unsqueeze(3).broadcast_to([P, PEER_H, TOPK, TOPK])
                second = pair[:, :, 1, :].unsqueeze(2).broadcast_to([P, PEER_H, TOPK, TOPK])
                step.link(nc.vector.tensor_tensor(cand[:].rearrange("p h (a b) -> p h a b", a=TOPK), first, second, ALU.add))
                best16(cand, cand2, PEER_H, best, pos, lambda m: None)
                flat = pos[:].rearrange("p h r -> p (h r)")
                step.done(nc.vector.tensor_scalar(part[:, 0, :], flat, 4, None, ALU.logical_shift_right))
                step.link(nc.vector.tensor_scalar(part[:, 1, :], flat, TOPK - 1, None, ALU.bitwise_and))
                step.link(nc.vector.tensor_copy(part_f[:], part[:]))
                step.link(nc.vector.tensor_copy(total[:], best[:, :, 0]))
                nc.vector.tensor_tensor(best[:], best[:], bcast(total[:], TOPK), ALU.subtract).then_inc(s_exp, 1)
                numbers = key_no[:].rearrange("p (h c) r -> p h c r", c=2)
                for c in range(2):
                    step.link(nc.vector.tensor_tensor(hit[:], bcast(part_f[:, c, :], TOPK), over(iota[:, 0:TOPK], P), ALU.is_equal))
                    hit4 = hit[:].rearrange("p (h r) a -> p h r a", h=PEER_H)
                    step.link(nc.vector.tensor_tensor(hit4, hit4, numbers[:, :, c, :].unsqueeze(2).broadcast_to(
                        [P, PEER_H, TOPK, TOPK]), ALU.mult))
                    step.link(nc.vector.tensor_reduce(pick[:, c, :], hit[:], AX.X, ALU.add))
                dve.wait_ge(s_exp, 2)
                step.link(nc.vector.tensor_reduce(total[:], best[:], AX.X, ALU.add))
                step.link(nc.vector.reciprocal(total[:], total[:]))
                nc.vector.tensor_tensor(pick[:, 2, :].rearrange("p (h r) -> p h r", h=PEER_H), best[:],
                                        bcast(total[:], TOPK), ALU.mult).then_inc(s_cmp, 1)


def spread_weights(nc, name, chosen, iota, gmat):
    with Stage(nc, name) as st:
        n_tok = 8
        rows = st.sb("rows", [P, 2, n_tok, N_KEYS])
        cols = st.sb("cols", [P, 2, n_tok, N_KEYS])
        acc = st.ps("acc", [P, 2, n_tok, N_KEYS])
        s_hit, s_rows, s_cols, s_summed, s_taken = (st.sem(n) for n in ("hit", "rows", "cols", "summed", "taken"))
        steps = T // n_tok
        which = lambda i, t: chosen[i][:, bass.ds(t, n_tok)].unsqueeze(2).broadcast_to([P, n_tok, N_KEYS])
        with nc.Block() as block:
            @block.vector
            def _(dve):
                dve.sem_inc(s_summed, 2)
                with dve.Fori(0, steps // 2) as i:
                    for b in range(2):
                        n = i * 2 + b
                        dve.wait_ge(s_summed, n + 1)
                        nc.vector.tensor_tensor(rows[:, b], over(iota, n_tok), which(0, n * n_tok), ALU.is_equal).then_inc(s_hit, 1)
                        nc.vector.tensor_tensor(cols[:, b], over(iota, n_tok), which(1, n * n_tok), ALU.is_equal).then_inc(s_cols, 1)

            @block.gpsimd
            def _(pool):
                with pool.Fori(0, steps // 2) as i:
                    for b in range(2):
                        n = i * 2 + b
                        pool.wait_ge(s_hit, n + 1)
                        nc.gpsimd.tensor_tensor(rows[:, b], rows[:, b], which(2, n * n_tok), ALU.mult).then_inc(s_rows, 1)

            @block.tensor
            def _(pe):
                with pe.Fori(0, steps // 2) as i:
                    for b in range(2):
                        n = i * 2 + b
                        pe.wait_ge(s_rows, n + 1)
                        pe.wait_ge(s_cols, n + 1)
                        pe.wait_ge(s_taken, n + 1)
                        for t in range(n_tok):
                            ins = nc.tensor.matmul(acc[:, b, t, :], rows[:, b, t, :], cols[:, b, t, :], start=True, stop=True)
                        ins.then_inc(s_summed, 1)

            @block.scalar
            def _(act):
                act.sem_inc(s_taken, 2)
                with act.Fori(0, steps // 2) as i:
                    for b in range(2):
                        n = i * 2 + b
                        act.wait_ge(s_summed, n + 3)
                        nc.scalar.activation(gmat[:, bass.ds(n * n_tok, n_tok), :], acc[:, b], ACT.Copy).then_inc(s_taken, 1)


def dense_experts(nc, name, pair, w_u, w_v, gmat, x, gate):
    with Stage(nc, name) as st:
        half = KD // 2
        cols = half * P
        raw_u, raw_v = st.sb("raw_u", [P, 4, cols]), st.sb("raw_v", [P, 4, cols])
        u = st.sb("u_hi", [P, 2, cols], F32R), st.sb("u_lo", [P, 2, cols], F32R)
        v = st.sb("v_hi", [P, 2, cols], F32R), st.sb("v_lo", [P, 2, cols], F32R)
        e = st.sb("e", [P, T])
        ew = st.sb("e_hi", [P, 2, T], F32R), st.sb("e_lo", [P, 2, T], F32R)
        score = st.ps("score", [P, 2, 512])
        acc = st.ps("acc", [P, KD, T])
        s_u, s_v = [st.sem(f"u{r}") for r in range(4)], [st.sem(f"v{r}") for r in range(4)]
        (s_u_hi, s_u_lo, s_u_used, s_v_hi, s_v_lo, s_v_used, s_gelu, s_e, s_e_hi, s_e_lo) = (
            st.sem(n) for n in ("u_hi", "u_lo", "u_used", "v_hi", "v_lo", "v_used", "gelu", "e", "e_hi", "e_lo"))
        RAW, HALF, OUT, BANK, BUF = 4, 2, 4, 2, 1

        with nc.Block() as block:
            @block.sync
            def _(sp):
                def fetch_u(j, slot):
                    for i in range(2):
                        sp.wait_ge(s_u_lo, j * 2 + i + 1)
                        sp.dma_start(raw_u[:, slot * 2 + i, :], w_u[bass.ds(j, 1), :, i * cols:(i + 1) * cols].rearrange(
                            "a p c -> p (a c)")).then_inc(s_u[slot * 2 + i], 16)

                def fetch_v(j, slot):
                    for i in range(2):
                        sp.wait_ge(s_v_lo, j * 2 + i + 1)
                        sp.dma_start(raw_v[:, slot * 2 + i, :], w_v[:, bass.ds(j, 1), i * cols:(i + 1) * cols].rearrange(
                            "p a c -> p (a c)")).then_inc(s_v[slot * 2 + i], 16)

                def body(j, slot, turn):
                    fetch_u(j + 1, 1 - slot)
                    fetch_v(j, slot)
                fetch_u(0, 0)
                each_chunk(sp, 0, N_KEYS - 1, 2, body)
                fetch_v(N_KEYS - 1, 1)

            @block.tensor
            def _(pe):
                pe.sem_inc(s_u_used, HALF)
                pe.sem_inc(s_v_used, OUT)

                def scores(j, slot):
                    pe.wait_ge(s_gelu, j + 1)
                    for i in range(2):
                        pe.wait_ge(s_u_lo, j * 2 + i + 1 + RAW)
                        for k in range(half):
                            ins = products(nc, score[:, slot, 0:T], part(u, slice(None), i, slice(k * P, (k + 1) * P)),
                                           part(pair, slice(None), i * half + k), start=(i == 0 and k == 0),
                                           stop=(i == 1 and k == half - 1))
                        ins.then_inc(s_u_used, 1)

                def outputs(j, slot, start=False, stop=False):
                    pe.wait_ge(s_e_lo, j + 1 + BUF)
                    for i in range(2):
                        pe.wait_ge(s_v_lo, j * 2 + i + 1 + RAW)
                        for k in range(half):
                            m = i * half + k
                            ins = products(nc, acc[:, m, :], part(v, slice(None), i, slice(k * P, (k + 1) * P)),
                                           part(ew, slice(None), slot), start=start and m % 2 == 0, stop=stop)
                        ins.then_inc(s_v_used, 1)

                scores(0, 0)
                scores(1, 1)
                outputs(0, 0, start=True)
                with pe.Fori(1, N_KEYS // 2) as i:
                    scores(i * 2, 0)
                    outputs(i * 2 - 1, 1)
                    scores(i * 2 + 1, 1)
                    outputs(i * 2, 0)
                outputs(N_KEYS - 1, 1, stop=True)

            @block.scalar
            def _(act):
                act.sem_inc(s_gelu, BANK)

                def hi(s_loaded, s_used, ahead, s_done, dst, raw, j, slot, turn):
                    for i in range(2):
                        act.wait_ge(s_loaded[slot * 2 + i], turn * 16 + 16)
                        act.wait_ge(s_used, j * 2 + i - 1 + ahead)
                        nc.scalar.activation(dst[0][:, i, :], raw[:, slot * 2 + i, :], ACT.Copy).then_inc(s_done, 1)

                def hi_u(j, slot, turn):
                    hi(s_u, s_u_used, HALF, s_u_hi, u, raw_u, j, slot, turn)

                def gelu_and_v(j, slot, turn):
                    act.wait_ge(s_u_used, j * 2 + 2 + HALF)
                    act.wait_ge(s_e_lo, j + BUF)
                    nc.scalar.activation(e[:], score[:, slot, 0:T], ACT.Gelu).then_inc(s_gelu, 1)
                    hi(s_v, s_v_used, OUT, s_v_hi, v, raw_v, j, slot, turn)

                def body(j, slot, turn):
                    gelu_and_v(j, slot % 2, turn * 2 + slot // 2)
                    hi_u(j + 2, slot % 2, turn * 2 + slot // 2 + 1)
                hi_u(0, 0, 0)
                hi_u(1, 1, 0)
                each_chunk(act, 0, N_KEYS - 2, 4, body)
                for j in range(N_KEYS - 2, N_KEYS):
                    gelu_and_v(j, j % 2, j // 2)

            @block.vector
            def _(dve):
                dve.sem_inc(s_u_lo, RAW)
                dve.sem_inc(s_v_lo, RAW)
                dve.sem_inc(s_e_lo, BUF)

                def lo(s_hi, s_done, dst, raw, j, slot):
                    for i in range(2):
                        dve.wait_ge(s_hi, j * 2 + i + 1)
                        nc.vector.tensor_tensor(dst[1][:, i, :], raw[:, slot * 2 + i, :],
                                                dst[0][:, i, :].bitcast(F32), ALU.subtract).then_inc(s_done, 1)

                def body(j, slot, turn):
                    if not isinstance(j, int) or j < N_KEYS - 1:
                        lo(s_u_hi, s_u_lo, u, raw_u, j + 1, 1 - slot)
                    dve.wait_ge(s_gelu, j + 1 + BANK)
                    nc.vector.tensor_tensor(e[:].unsqueeze(2), e[:].unsqueeze(2), gmat[:, :, bass.ds(j, 1)],
                                            ALU.mult).then_inc(s_e, 1)
                    dve.wait_ge(s_e, j + 1)
                    dve.wait_ge(s_v_used, j * 2 - 2 + OUT)
                    nc.vector.tensor_copy(ew[0][:, slot, :], e[:]).then_inc(s_e_hi, 1)
                    dve.wait_ge(s_e_hi, j + 1)
                    nc.vector.tensor_tensor(ew[1][:, slot, :], e[:], ew[0][:, slot, :].bitcast(F32), ALU.subtract).then_inc(s_e_lo, 1)
                    lo(s_v_hi, s_v_lo, v, raw_v, j, slot)
                lo(s_u_hi, s_u_lo, u, raw_u, 0, 0)
                each_chunk(dve, 0, N_KEYS - 1, 2, body)
                body(N_KEYS - 1, 1, None)
                dve.wait_ge(s_v_used, 2 * N_KEYS + OUT)
                for m in range(KD):
                    nc.vector.scalar_tensor_tensor(x[:, m, :], acc[:, m, :], gate[:, m, :], x[:, m, :], ALU.mult, ALU.add)


def peer(nc, name, x, mods, col, w_q, keys_dram, w_u, w_v, iota, ident):
    with Stage(nc, name) as st:
        pair = st.sb("hi", [P, KD, T], F32R), st.sb("lo", [P, KD, T], F32R)
        with Stage(nc, name + "_in") as tmp:
            modulate(nc, name + "_h", tmp.sb("h", [P, KD, T]), pair, x, mods, 3 * KD, (col,))
        chosen = [st.sb(f"chosen{i}", [P, T]) for i in range(3)]
        with Stage(nc, name + "_pick") as sel:
            q, keys = sel.sb("q", [P, 2 * PEER_H, T]), sel.sb("keys", [P, 2 * PEER_H, N_KEYS])
            load(nc, name + "_keys", [(keys[:], keys_dram)])
            project(nc, name + "_q", w_q, KD, pair, T, [(2 * PEER_H, copy_to(nc, q))])
            for tile in range(NT):
                select_experts(nc, f"{name}_select{tile}", q, keys, tile, chosen, iota, ident)
        gmat = st.sb("gmat", [P, T, N_KEYS])
        spread_weights(nc, name + "_spread", chosen, iota, gmat)
        dense_experts(nc, name + "_dense", pair, w_u, w_v, gmat, x, mods[:, 5 * KD:, col:col + 1])


VECTORS = [("c", KD), ("ada_b", 2 * 6 * KD), ("ln_g", 4 * KD), ("ln_b", 4 * KD), ("lb_raw", H), ("norm_g", 1),
           ("pool_scale", KD), ("conv", 2 * KF * 4), ("sinks", A_HEADS), ("c_2", KD * 2), ("b_mod_2", 2 * 6 * KD),
           ("ln_w_2", 4 * KD), ("ln_b_2", 4 * KD), ("ab_norm_w_2", H), ("sinks_2", A_HEADS), ("gla_gate_b_2", 2 * H),
           ("gla_norm_w_2", KD)]
CONSTANTS = [("ones", P), ("mean_of_p", P), ("mean_of_d", P), ("ident", P), ("iota", P)]
Q_ORDER = [h for c in range(GQA) for h in (c, GQA + c)]


def offsets(fields):
    at, out = 0, {}
    for name, n in fields:
        out[name] = (at, at + n)
        at += n
    return out, at


def first_block(nc, d, x, vec, con):
    with Stage(nc, "first") as blk:
        mods = blk.sb("mods", [P, 6 * KD, 1])
        h, z = blk.sb("h", [P, KD, T]), blk.sb("z", [P, KD, T])
        pair = blk.sb("h_hi", [P, KD, T], F32R), blk.sb("h_lo", [P, KD, T], F32R)
        c = vec("c").unsqueeze(2)
        ln = lambda layer, i: (vec("ln_g")[:, (2 * layer + i) * KD:(2 * layer + i + 1) * KD],
                               vec("ln_b")[:, (2 * layer + i) * KD:(2 * layer + i + 1) * KD])
        conv = lambda layer: vec("conv").rearrange("p (l f j) -> p l f j", l=2, j=4)[:, layer]
        ada_b = lambda layer: vec("ada_b")[:, layer * 6 * KD:(layer + 1) * 6 * KD]

        modulation(nc, "mod0", c, d["ada_w"][0], ada_b(0), mods, con("ident"))
        modulate(nc, "h00", h, pair, x, mods, 0, (0,))
        even_mixer(nc, d, pair, z, mods, vec, con)
        layer_norm(nc, "ln00", x, z, h, T, *ln(0, 0), con("mean_of_d"))
        modulate(nc, "h01", h, pair, x, mods, 3 * KD, (0,))
        conv_ffn(nc, "ffn0", pair, d["w_up"][0], conv(0), d["w_down"][0], z, mods[:, 5 * KD:, :])
        layer_norm(nc, "ln01", x, z, h, T, *ln(0, 1), con("mean_of_d"))

        modulation(nc, "mod1", c, d["ada_w"][1], ada_b(1), mods, con("ident"))
        modulate(nc, "h10", h, pair, x, mods, 0, (0,))
        with Stage(nc, "poolmix") as st:
            inv_count = st.sb("inv_count", [P, len(POOL_WINDOWS), T])
            load(nc, "load_pool", [(inv_count[:], d["inv_count"])])
            pool_mixer(nc, "pool", h, d["pool_w"], vec("pool_scale"), inv_count, z, mods[:, 2 * KD:3 * KD, :], x)
        layer_norm(nc, "ln10", x, z, h, T, *ln(1, 0), con("mean_of_d"), residual=False)
        modulate(nc, "h11", h, pair, x, mods, 3 * KD, (0,))
        conv_ffn(nc, "ffn1", pair, d["w_up"][1], conv(1), d["w_down"][1], z, mods[:, 5 * KD:, :])
        layer_norm(nc, "ln11", x, z, h, T, *ln(1, 1), con("mean_of_d"))


def hgrn_gates(nc, name, f, k, g, lb_raw):
    with Stage(nc, name) as st:
        share, lb, rest = st.sb("share", [P, H]), st.sb("lb", [P, H]), st.sb("rest", [P, H])
        s_step, s_sig, s_exp, s_clamped = st.sem("step"), st.sem("sig"), st.sem("exp"), st.sem("clamped")
        with nc.Block() as block:
            @block.scalar
            def _(act):
                nc.scalar.activation(k, f, ACT.Sigmoid, scale=-1.0).then_inc(s_sig, 1)
                act.wait_ge(s_sig, 1)
                nc.scalar.activation(f, f, ACT.Sigmoid).then_inc(s_sig, 1)
                act.wait_ge(s_step, 1)
                nc.scalar.activation(share[:], share[:], ACT.Exp).then_inc(s_exp, 1)
                act.wait_ge(s_clamped, 1)
                nc.scalar.activation(g, f, ACT.Ln)

            @block.vector
            def _(dve):
                step = Steps(dve, s_step)
                step.done(nc.vector.tensor_tensor(share[:], lb_raw, lb_raw, ALU.subtract))
                dve.wait_ge(s_exp, 1)
                step.link(nc.vector.reciprocal(lb[:], share[:]))
                step.link(nc.vector.tensor_tensor(share[:], share[:], lb[:], ALU.mult))
                step.link(nc.vector.tensor_tensor(lb[:], share[:], share[:], ALU.subtract))
                step.link(nc.vector.tensor_scalar(rest[:], lb[:], -1.0, 1.0, ALU.mult, ALU.add))
                dve.wait_ge(s_sig, 2)
                for h in range(H):
                    step.done(nc.vector.tensor_scalar(k[:, h, :], k[:, h, :], rest[:, h:h + 1], None, ALU.mult))
                    step.done(nc.vector.tensor_scalar(f[:, h, :], f[:, h, :], rest[:, h:h + 1], lb[:, h:h + 1], ALU.mult, ALU.add))
                step.wait()
                nc.vector.tensor_scalar(f, f, LN_MIN, None, ALU.max).then_inc(s_clamped, 1)


def even_mixer(nc, d, h, z, mods, vec, con):
    with Stage(nc, "mixer") as mix:
        cat = mix.sb("cat", [P, KD, T])
        qk = mix.sb("qk", [P, GQA + 1, T])
        v = mix.sb("v", [P, NT, 2 * P + 3 * P])
        with Stage(nc, "hgrn") as st:
            q, f, gate, k, g = (st.sb(n, [P, H, T]) for n in ("q", "f", "gate", "k", "g"))
            o = st.sb("o", [P, H, T])
            at, off = st.sb("at", [P, H * NT, P]), st.sb("off", [P, H, P])
            masks = st.sb("masks", [P, LEVELS + 1, P], I32)

            project(nc, "ab_in", d["ab_w_in"], KD, h, T, [(H, copy_to(nc, q)), (H, copy_to(nc, f)),
                                                          (H, copy_to(nc, gate, ACT.Silu)), (GQA + 1, copy_to(nc, qk))])
            token_major(nc, "ab_v", d["ab_w_v"], 5 * P, h, T, v)
            load(nc, "load_levels", [(masks[:], d["levels"][0])])
            hgrn_gates(nc, "gates", f[:], k[:], g[:], vec("lb_raw"))
            decayed_scores(nc, "hgrn_scores", q[:], k[:], [(g[:], False)], [masks], at[:], [off[:]])
            weighted_values(nc, "hgrn_values", [v[:, i, 0:4 * P] for i in range(NT)], P, at, [off], o)
            head_norm(nc, "hgrn_norm", o, cat[:, 0:H, :], gate, lambda c: vec("norm_g"), 1, T, RMS_EPS, con("mean_of_p"))
        with Stage(nc, "swa") as st:
            positions, cos, sin = st.sb("positions", [P, T], I32), st.sb("cos", [P, T]), st.sb("sin", [P, T])
            perm, inv_freq, mask = st.sb("perm", [P, P]), st.sb("inv_freq", [P, 1]), st.sb("mask", [P, 2 * P])
            load(nc, "load_swa", [(positions[:], d["positions"]), (perm[:], d["perm"]), (inv_freq[:], d["inv_freq"]),
                                  (mask[:], d["swa_mask"])])
            rope_tables(nc, "tables", positions[:], inv_freq[:], cos[:], sin[:])
            rope(nc, "rope", qk[:], perm[:], cos[:], sin[:])
            values = [v[:, i, 4 * P:5 * P].rearrange("p (g e) -> p g e", g=2) for i in range(NT)]
            attention(nc, "swa_attention",
                      [(lambda c: qk[:, c, 0:P], [qk[:, GQA, 0:P]], values[0:1], mask[:, P:2 * P], slice(0, P)),
                       (lambda c: qk[:, c, P:2 * P], [qk[:, GQA, :]], values, mask[:], slice(P, 2 * P))],
                      vec("sinks"), cat[:, H:, :], con("ident"))
        cat_pair = mix.sb("cat_hi", [P, KD, T], F32R), mix.sb("cat_lo", [P, KD, T], F32R)
        split(nc, "cat_split", cat, cat_pair)
        project(nc, "ab_out", d["ab_w_out"], KD, cat_pair, T, [(KD, gate_to(nc, z, mods[:, 2 * KD:3 * KD, :]))])


def second_block(nc, d, x, out, vec, con):
    with Stage(nc, "second") as blk:
        mods = blk.sb("mods2", [P, 6 * KD, 2])
        lat = slice(T, 2 * T)
        c = vec("c_2").rearrange("p (k n) -> p k n", n=2)
        ln = lambda layer, i: (vec("ln_w_2")[:, (2 * layer + i) * KD:(2 * layer + i + 1) * KD],
                               vec("ln_b_2")[:, (2 * layer + i) * KD:(2 * layer + i + 1) * KD])
        bias = lambda layer: vec("b_mod_2")[:, layer * 6 * KD:(layer + 1) * 6 * KD]
        streams = x[:, :, 0:T], x[:, :, lat]

        def peer_layer(layer, stream):
            peer(nc, f"peer{layer}{stream}", streams[stream], mods, stream, d["peer_wq"][layer], d["peer_keys"][layer],
                 d["peer_u"][layer], d["peer_v"][layer], con("iota"), con("ident"))

        for layer, mixer in enumerate((mixer_ab, mixer_c)):
            modulation(nc, f"mod2{layer}", c, d["w_mod"][layer], bias(layer), mods, con("ident"))
            with Stage(nc, f"mix{layer}") as st:
                h = st.sb("h", [P, KD, 2 * T])
                pair = st.sb("h_hi", [P, KD, 2 * T], F32R), st.sb("h_lo", [P, KD, 2 * T], F32R)
                modulate(nc, f"h2{layer}", h, pair, x, mods, 0, (0, 1))
                mixer(nc, d, h, pair, mods, vec, con)
                if layer == 0:
                    with Stage(nc, "norm20") as norm:
                        layer_norm(nc, "ln20", x, h, norm.sb("sq", [P, KD, 2 * T]), 2 * T, *ln(0, 0), con("mean_of_d"))
                else:
                    with Stage(nc, "norm30") as norm:
                        layer_norm(nc, "ln30", streams[1], h[:, :, lat], norm.sb("sq", [P, KD, T]), T, *ln(1, 0), con("mean_of_d"))
            if layer == 0:
                peer_layer(0, 0)
            peer_layer(layer, 1)
            which = x if layer == 0 else streams[1]
            t = which.shape[2]
            with Stage(nc, f"norm{layer}1") as norm:
                layer_norm(nc, f"ln{layer + 2}1", which, which, norm.sb("sq", [P, KD, t]), t, *ln(layer, 1), con("mean_of_d"),
                           residual=False)
        store(nc, "store", out, streams[1])


def store(nc, name, out, src):
    with Stage(nc, name) as st:
        s_stored = st.sem("stored")
        with nc.Block() as block:
            @block.sync
            def _(sp):
                sp.dma_start(out, src).then_inc(s_stored, 16)
                sp.wait_ge(s_stored, 16)


def mixer_ab(nc, d, h, pair, mods, vec, con):
    lat = slice(T, 2 * T)
    with Stage(nc, "mixab") as mix:
        cat = mix.sb("cat", [P, KD, 2 * T])
        qk = mix.sb("qk", [P, GQA + 1, 2 * T])
        v = mix.sb("v", [P, 2 * NT, 5 * P])
        with Stage(nc, "mlstm") as st:
            q, k, gate, o = (st.sb(n, [P, H, 2 * T]) for n in ("q", "k", "gate", "o"))
            rows = [[st.sb(f"row{a}{b}", [H, 2 * T]) for b in range(2)] for a in range(2)]
            u_cols = st.sb("u_cols", [P, 4, 2, H])
            w_gates, gate_b = st.sb("w_gates", [P, KD, 4 * H]), st.sb("gate_b", [H, 4])
            masks, select = st.sb("masks", [P, 2, NT, T]), st.sb("select", [H, H, P])

            project(nc, "ab2_in", d["ab_w_in_2"], KD, pair, 2 * T,
                    [(H, copy_to(nc, q)), (H, copy_to(nc, k)), (H, copy_to(nc, gate, ACT.Sigmoid)), (GQA + 1, copy_to(nc, qk))])
            token_major(nc, "ab2_v", d["ab_w_v_2"], 5 * P, pair, 2 * T, v)
            load(nc, "load_gates", [(w_gates[:], d["ab_w_gates_2"]), (gate_b[:], d["ab_gate_b_2"]),
                                    (masks[:], d["causal"]), (select[:], d["select"])])
            log_sigmoid_rows(nc, "gate_rows", h, w_gates, gate_b, rows, u_cols, con("ident"))
            mlstm(nc, "mlstm_scan", q, k, v, rows, u_cols, masks, select, con("ones"), o)
            head_norm(nc, "mlstm_norm", o, cat[:, 0:H, :], gate, lambda c: vec("ab_norm_w_2")[:, c:c + 1], 1, 2 * T,
                      LN_EPS, con("mean_of_p"))
        with Stage(nc, "window") as st:
            perm, tables, mask = st.sb("perm", [P, P]), st.sb("tables", [P, 2, T]), st.sb("mask", [P, NT, 2 * T])
            load(nc, "load_window", [(perm[:], d["perm_2"]), (tables[:], d["axial"]), (mask[:], d["window"])])
            rope(nc, "rope2", qk[:, :, lat], perm[:], tables[:, 0, :], tables[:, 1, :])
            values = [v[:, i, 4 * P:5 * P].rearrange("p (g e) -> p g e", g=2) for i in range(2 * NT)]
            tiles = [(lambda c, a=i * P: qk[:, c, a:a + P], [qk[:, GQA, 0:T]] + [qk[:, GQA, lat]] * (i >= NT),
                      values if i >= NT else values[0:NT], mask[:, i - NT, :] if i >= NT else None, slice(i * P, (i + 1) * P))
                     for i in range(2 * NT)]
            attention(nc, "window_attention", tiles, vec("sinks_2"), cat[:, H:, :], con("ident"))
        cat_pair = mix.sb("cat_hi", [P, KD, 2 * T], F32R), mix.sb("cat_lo", [P, KD, 2 * T], F32R)
        split(nc, "cat2_split", cat, cat_pair)
        project(nc, "ab2_out", d["ab_w_out_2"], KD, cat_pair, 2 * T, [(KD, gate_to(nc, h, mods[:, 2 * KD:3 * KD, :]))])


def mixer_c(nc, d, h, pair, mods, vec, con):
    lat = slice(T, 2 * T)
    with Stage(nc, "mixc") as mix:
        gate = mix.sb("gate", [P, KD, T])
        o = mix.sb("o", [P, KD, T])
        with Stage(nc, "gla") as st:
            q = st.sb("q", [P, H, T])
            k = [st.sb(f"k{i}", [P, H, T]) for i in range(2)]
            v = st.sb("v", [P, 2 * NT, KD * P])
            la = [[st.sb(f"la{a}{b}", [P, H, T]) for b in range(2)] for a in range(2)]

            def k_to(index, psum):
                nc.scalar.activation(k[0][:, bass.ds(index, 1), :], psum[:, 0:T].unsqueeze(1), ACT.Copy)
                return nc.scalar.activation(k[1][:, bass.ds(index, 1), :], psum[:, lat].unsqueeze(1), ACT.Copy)
            project(nc, "gla_k", d["gla_w_k_2"], KD, pair, 2 * T, [(H, k_to)])
            project(nc, "gla_qg", d["gla_w_qg_2"], KD, part(pair, slice(None), slice(None), lat), T,
                    [(H, copy_to(nc, q, scale=P ** -0.5)), (KD, copy_to(nc, gate, ACT.Silu))])
            token_major(nc, "gla_v", d["gla_w_v_2"], KD * P, pair, 2 * T, v)
            with Stage(nc, "decays") as dec:
                w_low, low = dec.sb("w_low", [P, KD, 32]), dec.sb("low", [16, 2, 2 * T])
                gate_up = dec.sb("gate_up", [16, 2, H * P])
                acc = dec.ps("acc", [P, 2, 2 * T])
                s_low, s_copied = dec.sem("low"), dec.sem("copied")
                load(nc, "load_low", [(w_low[:], d["gla_w_low_2"]), (gate_up[:], d["gla_gate_up_2"])])
                with nc.Block() as block:
                    @block.tensor
                    def _(pe):
                        for n in range(2):
                            for kc in range(KD):
                                ins = nc.tensor.matmul(acc[0:16, n, :], w_low[:, kc, n * 16:(n + 1) * 16], h[:, kc, :],
                                                       start=(kc == 0), stop=(kc == KD - 1))
                        ins.then_inc(s_low, 1)

                    @block.scalar
                    def _(act):
                        act.wait_ge(s_low, 1)
                        nc.scalar.activation(low[:], acc[0:16], ACT.Copy).then_inc(s_copied, 1)
                gla_decays(nc, "gla_decays", low, gate_up, vec("gla_gate_b_2").rearrange("p (d h) -> p d h", d=2),
                           [[a[:] for a in row] for row in la])
            with Stage(nc, "scores") as sc:
                at, offs = sc.sb("at", [P, H * NT, P]), [sc.sb(f"off{i}", [P, H, P]) for i in range(2)]
                ctx_at = sc.sb("ctx_at", [P, 2, H, T])
                masks = [sc.sb(f"masks{i}", [P, LEVELS + 1, P], I32) for i in range(2)]
                load(nc, "load_levels2", [(masks[0][:], d["levels"][0]), (masks[1][:], d["levels"][1])])
                decayed_scores(nc, "gla_scores", q[:], k[1][:], [(la[0][1][:], False), (la[1][1][:], True)], masks, at[:],
                               [a[:] for a in offs], (k[0][:], [la[0][0], la[1][0]], ctx_at))
                weighted_values(nc, "gla_values", [v[:, NT + i, :] for i in range(NT)], 2 * P, at, offs, o,
                                ([v[:, i, :] for i in range(NT)], ctx_at))
        y = mix.sb("y", [P, KD, T])
        head_norm(nc, "gla_norm", o, y, gate, lambda c: vec("gla_norm_w_2")[:, c:c + 1], 2, T, LN_EPS, con("mean_of_p"))
        y_pair = mix.sb("y_hi", [P, KD, T], F32R), mix.sb("y_lo", [P, KD, T], F32R)
        split(nc, "y_split", y, y_pair)
        project(nc, "gla_out", d["gla_w_out_2"], KD, y_pair, T, [(KD, gate_to(nc, h[:, :, lat], mods[:, 2 * KD:3 * KD, 1:2]))])


def program(nc, d, out):
    vec_at, n_vec = offsets(VECTORS)
    con_at, n_con = offsets(CONSTANTS)
    with Stage(nc, "all") as st:
        vectors, constants = st.sb("vectors", [P, n_vec]), st.sb("constants", [P, n_con])
        x = st.sb("x", [P, KD, 2 * T])
        vec = lambda name: vectors[:, vec_at[name][0]:vec_at[name][1]]
        con = lambda name: constants[:, con_at[name][0]:con_at[name][1]]
        load(nc, "load_all", [(vectors[:], d["vectors"]), (constants[:], d["constants"]), (x[:, :, 0:T], d["ctx"]), (x[:, :, T:], d["x"])])
        first_block(nc, d, x[:, :, T:], vec, con)
        second_block(nc, d, x, out, vec, con)


def columns(v):
    return np.ascontiguousarray(np.reshape(v, (-1, P)).T)


def chunked(w):
    kc, mo = w.shape[0] // P, w.shape[1] // P
    return np.ascontiguousarray(w.reshape(kc, P, mo, P).transpose(2, 1, 0, 3).reshape(mo, P, kc * P))


def streamed(w):
    half = w.shape[0] // P // 2
    return w.reshape(2, half, P, -1, 512).transpose(3, 0, 2, 1, 4).reshape(-1, P, half, 512)


def feature_major(x):
    return np.ascontiguousarray(x.reshape(x.shape[0], -1, P).transpose(2, 1, 0))


def constants_of_shapes():
    f = np.float32
    i = np.arange(P)
    con = np.concatenate([np.ones((P, P)), np.full((P, P), 1 / P), np.full((P, P), 1 / D), np.eye(P),
                          np.broadcast_to(i, (P, P))], 1).astype(f)
    s, t = i[:, None], i[None, :]
    levels = np.zeros((2, P, LEVELS + 1, P), np.int32)
    levels[:, :, 0, :] = s == t
    for level in range(1, LEVELS + 1):
        half = 2 ** (level - 1)
        same = s // (2 * half) == t // (2 * half)
        levels[0, :, level, :] = same & (s // half % 2 == 0) & (t // half % 2 == 1)
        levels[1, :, level, :] = levels[0, :, level, :].T
    masked = lambda keep: np.where(keep, 0.0, MASKED).astype(f)
    rel = s + P - np.arange(2 * P)[None, :]
    swa_mask = masked((rel >= 0) & (rel < P))
    tt = np.arange(T)
    causal = np.stack([masked((tt[:, None] <= tt[None, :])), masked(tt[:, None] >= tt[None, :])])
    causal = causal.reshape(2, NT, P, T).transpose(2, 0, 1, 3)
    window = np.zeros((NT, P, 2 * T), f)
    window[:, :, T:] = masked(np.abs(tt[:, None] - tt[None, :]) <= P).reshape(NT, P, T)
    select = np.zeros((H, H, P), f)
    select[np.arange(H), np.arange(H), :] = 1
    inv_count = np.stack([1.0 / np.minimum(tt + 1, w) for w in POOL_WINDOWS]).astype(f)
    dim = i % A_DIM
    rope_dim = A_DIM // 4
    inv = f(500000.0) ** (-np.arange(0, rope_dim, 2, dtype=f) / f(rope_dim))
    inv_freq = np.where(dim < rope_dim, inv[dim % (rope_dim // 2)], 0.0).astype(f)[:, None]
    perm = np.zeros((P, P), f)
    for r in range(P):
        if dim[r] < rope_dim // 2:
            perm[r, r + rope_dim // 2] = -1
        elif dim[r] < rope_dim:
            perm[r, r - rope_dim // 2] = 1
    n_freq = A_DIM // 4
    inv2 = f(10000.0) ** (-np.arange(n_freq, dtype=f) / f(n_freq))
    ang = np.concatenate([(tt // 64).astype(f)[:, None] * inv2, (tt % 64).astype(f)[:, None] * inv2], -1).astype(f)
    axial = np.stack([np.cos(ang).T[dim // 2], np.sin(ang).T[dim // 2]], 1).astype(f)
    perm_2 = np.zeros((P, P), f)
    perm_2[i[0::2], i[1::2]] = -1
    perm_2[i[1::2], i[0::2]] = 1
    return {"constants": con, "levels": levels, "swa_mask": swa_mask, "causal": causal,
            "window": window.transpose(1, 0, 2), "select": select,
            "inv_count": np.broadcast_to(inv_count, (P,) + inv_count.shape), "inv_freq": inv_freq,
            "perm": perm.T, "axial": axial, "perm_2": perm_2.T}


def lay_out(a):
    w = {}
    w["x"], w["ctx"] = feature_major(a["x"][0]), feature_major(a["ctx_2"][0])
    w["positions"] = np.broadcast_to(a["positions"], (P, T))
    w["ada_w"] = np.stack([streamed(m) for m in a["ada_w"]])
    w["w_mod"] = np.stack([streamed(m) for m in a["w_mod_2"]])
    heads = lambda m: m.reshape(m.shape[0], A_HEADS, A_DIM)[:, Q_ORDER].reshape(m.shape[0], -1)
    cut = lambda m, widths: np.split(m, np.cumsum(widths)[:-1], axis=1)
    aq, af, ai, ag, bq, bk, bv = cut(a["ab_w_in"][0], [512, 512, 512, 512, 512, 128, 128])
    w["ab_w_in"] = chunked(np.concatenate([aq, af, ag, heads(bq), bk], 1))
    w["ab_w_v"] = np.concatenate([ai, bv], 1).reshape(KD, P, -1)
    w["ab_w_out"] = chunked(a["ab_w_out"][0])
    w["pool_w"] = a["pool_w"][0].reshape(4, 2, P, 2, P).transpose(2, 0, 3, 1, 4).reshape(P, KD, 2, P)
    up = a["ffn_w_up"].reshape(2, D, 2, KF, P).transpose(0, 1, 3, 2, 4).reshape(2, D, -1)
    w["w_up"] = np.stack([chunked(m) for m in up])
    w["w_down"] = np.stack([chunked(m) for m in a["ffn_w_down"]])
    mq, mk, mv, mo, mg, q2, k2, v2 = cut(a["ab_w_in_2"][0], [512, 512, 512, 512, 16, 512, 128, 128])
    w["ab_w_in_2"] = chunked(np.concatenate([mq, mk, mo, heads(q2), k2], 1))
    w["ab_w_v_2"] = np.concatenate([mv, v2], 1).reshape(KD, P, -1)
    w["ab_w_gates_2"] = mg.reshape(KD, P, 16).transpose(1, 0, 2)
    w["ab_gate_b_2"] = a["ab_gate_b_2"][0].reshape(4, H).T
    w["ab_w_out_2"] = chunked(a["ab_w_out_2"][0])
    gq, gk, gv, gg, glow = cut(a["gla_w_in_2"][0], [512, 512, 1024, 1024, 32])
    w["gla_w_k_2"], w["gla_w_qg_2"] = chunked(gk), chunked(np.concatenate([gq, gg], 1))
    w["gla_w_v_2"] = gv.reshape(KD, P, -1)
    w["gla_w_low_2"] = glow.reshape(KD, P, 32).transpose(1, 0, 2)
    w["gla_gate_up_2"] = a["gla_gate_up_2"][0].transpose(1, 0, 2)
    w["gla_w_out_2"] = chunked(a["gla_w_out_2"][0])
    w["peer_wq"] = np.stack([chunked(m) for m in a["peer_wq_2"]])
    w["peer_keys"] = a["peer_keys_2"].reshape(2, 2 * PEER_H, N_KEYS, P).transpose(0, 3, 1, 2)
    w["peer_u"] = a["peer_u_2"].reshape(2, N_KEYS, N_KEYS, KD, P).transpose(0, 2, 4, 3, 1).reshape(2, N_KEYS, P, D)
    w["peer_v"] = a["peer_v_2"].reshape(2, N_KEYS, N_KEYS, D)
    spread = lambda v: np.broadcast_to(np.reshape(v, (1, -1)), (P, np.size(v)))
    conv = np.concatenate([a["ffn_conv_w"], a["ffn_conv_b"][:, None, :]], 1)
    vectors = {
        "c": columns(a["c"]), "ada_b": columns(a["ada_b"]), "ln_g": columns(a["ln_g"]), "ln_b": columns(a["ln_b"]),
        "lb_raw": columns(a["hgrn_lb_raw"]), "norm_g": columns(a["hgrn_norm_g"]), "pool_scale": columns(a["pool_scale"]),
        "conv": conv.reshape(2, 4, KF, P).transpose(3, 0, 2, 1).reshape(P, -1), "sinks": spread(a["attn_sinks"]),
        "c_2": np.stack([columns(a["c_ctx_2"]), columns(a["c_2"])], 2).reshape(P, -1), "b_mod_2": columns(a["b_mod_2"]),
        "ln_w_2": columns(a["ln_w_2"]), "ln_b_2": columns(a["ln_b_2"]), "ab_norm_w_2": columns(a["ab_norm_w_2"]),
        "sinks_2": spread(a["ab_sink_2"]), "gla_gate_b_2": columns(a["gla_gate_b_2"]),
        "gla_norm_w_2": columns(a["gla_norm_w_2"])}
    w["vectors"] = np.concatenate([vectors[name] for name, _ in VECTORS], 1)
    w.update(constants_of_shapes())
    return {name: np.ascontiguousarray(v) for name, v in w.items()}


def kernel(**inputs):
    import concourse.bacc as bacc
    from concourse.bass_utils import run_bass_kernel_spmd

    arrays = lay_out({name: np.asarray(v) for name, v in inputs.items()})
    nc = bacc.Bacc("TRN2", target_bir_lowering=False, num_devices=1)
    d = {name: nc.dram_tensor(f"in_{name}", v.shape, mybir.dt.from_np(v.dtype), kind="ExternalInput").ap()
         for name, v in arrays.items()}
    out = nc.dram_tensor("out", (P, KD, T), F32, kind="ExternalOutput").ap()
    program(nc, d, out)
    run = run_bass_kernel_spmd(nc, [{f"in_{name}": v for name, v in arrays.items()}], core_ids=[0])
    y = np.asarray(run.results[0]["out"])
    return np.ascontiguousarray(y.transpose(2, 1, 0).reshape(1, T, D))
```

```python
from contextlib import ExitStack

import numpy as np

import concourse.bass as bass
from concourse import mybir
from concourse.alu_op_type import AluOpType as ALU

ACT = mybir.ActivationFunctionType
AX = mybir.AxisListType
F32 = mybir.dt.float32
I32 = mybir.dt.int32
U32 = mybir.dt.uint32
BF16 = mybir.dt.bfloat16
F32R = mybir.dt.float32r

P = 128
D = 1024
KD = D // P
T = 256
NT = T // P
H = 4
D_FF = 2816
KF = D_FF // P
LEVELS = 7
A_HEADS, A_DIM, GQA = 8, 64, 4
N_KEYS, PEER_H, TOPK = 128, 8, 16
POOL_WINDOWS = (2, 4, 8, 16)
ALPHA = float((2.0 * 2) ** 0.25)
LN_EPS, RMS_EPS = 1e-5, 1e-6
LN_MIN = 2.0 ** -64
MASKED = -1e30
EVEN_PI_1, EVEN_PI_2 = 6.28125, 0.001934051513671875
EVEN_PI_3 = 2 * np.pi - EVEN_PI_1 - EVEN_PI_2
ROUND = 12582912.0


class Stage:

    def __init__(self, nc, name):
        self.nc, self.name, self.ctx, self.sems = nc, name, ExitStack(), []

    def __enter__(self):
        return self

    def __exit__(self, *_):
        self.nc.clear_and_free_semaphores(self.sems)
        self.nc.all_engine_barrier()
        self.ctx.close()

    def sb(self, name, shape, dt=F32):
        return self.ctx.enter_context(self.nc.sbuf_tensor(f"{self.name}_{name}", shape, dt))[:]

    def ps(self, name, shape):
        return self.ctx.enter_context(self.nc.psum_tensor(f"{self.name}_{name}", shape, F32))[:]

    def sem(self, name):
        s = self.nc.alloc_semaphore(f"{self.name}_{name}")
        self.sems.append(s)
        return s


class Steps:

    def __init__(self, eng, sem):
        self.eng, self.sem, self.n = eng, sem, 0

    def done(self, ins):
        ins.then_inc(self.sem, 1)
        self.n = self.n + 1

    def wait(self):
        self.eng.wait_ge(self.sem, self.n)

    def link(self, ins):
        self.done(ins)
        self.wait()


def each_chunk(eng, first, count, ring, body):
    turns = count // ring
    if turns >= 2:
        with eng.Fori(0, turns) as i:
            for r in range(ring):
                body(first + r + i * ring, (first + r) % ring, (first + r) // ring + i)
    else:
        turns = 0
    for m in range(first + turns * ring, first + count):
        body(m, m % ring, m // ring)


def bcast(ap, n):
    return ap.unsqueeze(2).broadcast_to([ap.shape[0], ap.shape[1], n])


def over(ap, n):
    return ap.unsqueeze(1).broadcast_to([ap.shape[0], n, ap.shape[1]])


def load(nc, name, pairs):
    with Stage(nc, name) as st:
        s_loaded = st.sem("loaded")
        with nc.Block() as block:
            @block.sync
            def _(sp):
                for dst, src in pairs:
                    sp.dma_start(dst, src).then_inc(s_loaded, 16)
                sp.wait_ge(s_loaded, 16 * len(pairs))


def products(nc, out, lhs, rhs, start, stop):
    for n, (a, b) in enumerate(((lhs[0], rhs[0]), (lhs[0], rhs[1]), (lhs[1], rhs[0]))):
        ins = nc.tensor.matmul(out, a, b, start=start and n == 0, stop=stop and n == 2, skip_group_check=True)
    return ins


def part(pair, *index):
    return tuple(a[index] for a in pair)


def split(nc, name, src, pair, ahead):
    with Stage(nc, name) as st:
        s_hi = st.sem("hi")
        chunks = src.shape[1]
        with nc.Block() as block:
            @block.sync
            def _(sp):
                ahead.start(sp)

            @block.scalar
            def _(act):
                for k in range(chunks):
                    nc.scalar.activation(pair[0][:, k], src[:, k], ACT.Copy).then_inc(s_hi, 1)

            @block.vector
            def _(dve):
                for k in range(chunks):
                    dve.wait_ge(s_hi, k + 1)
                    nc.vector.tensor_tensor(pair[1][:, k], src[:, k], pair[0][:, k].bitcast(F32), ALU.subtract)


class Ahead:

    def __init__(self, nc, st, name, weights, kc=KD, raw=None):
        self.weights = weights
        self.pieces = 1 if kc <= KD else 2
        self.width = kc // self.pieces * P
        self.raw = st.sb(name + "_raw", [P, 4, self.width]) if raw is None else raw
        self.s_loaded = [st.sem(f"{name}_loaded{r}") for r in range(4)]

    def fetch(self, sp, m, bank, s_lo):
        for i in range(self.pieces):
            slot = bank * self.pieces + i
            if s_lo is not None:
                sp.wait_ge(s_lo, m * self.pieces + i - 3)
            src = self.weights[bass.ds(m, 1), :, i * self.width:(i + 1) * self.width].rearrange("a p c -> p (a c)")
            sp.dma_start(self.raw[:, slot, :], src).then_inc(self.s_loaded[slot], 16)

    def start(self, sp):
        for m in range(4 // self.pieces):
            self.fetch(sp, m, m, None)


def project(nc, name, weights, kc, rhs, t, segments, loads=()):
    with Stage(nc, name) as st:
        total = sum(n for n, _ in segments)
        pieces = 1 if kc <= KD else 2
        banks, width = 4 // pieces, kc // pieces
        started = isinstance(weights, Ahead)
        ahead = weights if started else Ahead(nc, st, "own", weights, kc)
        raw = ahead.raw
        w = st.sb("hi", [P, 4, width * P], F32R), st.sb("lo", [P, 4, width * P], F32R)
        acc = st.ps("acc", [P, banks, 512])
        s_loaded = ahead.s_loaded
        s_hi, s_lo, s_used, s_taken, s_extra = (st.sem(n) for n in ("hi", "lo", "used", "taken", "extra"))

        with nc.Block() as block:
            @block.sync
            def _(sp):
                if not started:
                    ahead.start(sp)
                if total > banks:
                    each_chunk(sp, banks, total - banks, banks, lambda m, bank, turn: ahead.fetch(sp, m, bank, s_lo))
                for dst, src in loads:
                    sp.dma_start(dst, src).then_inc(s_extra, 16)
                if loads:
                    sp.wait_ge(s_extra, 16 * len(loads))

            @block.vector
            def _(dve):
                def body(m, bank, turn):
                    for i in range(pieces):
                        slot = bank * pieces + i
                        dve.wait_ge(s_hi, m * pieces + i + 1)
                        nc.vector.tensor_tensor(w[1][:, slot, :], raw[:, slot, :], w[0][:, slot, :].bitcast(F32),
                                                ALU.subtract).then_inc(s_lo, 1)
                each_chunk(dve, 0, total, banks, body)

            @block.tensor
            def _(pe):
                pe.sem_inc(s_used, 4)

                def body(m, bank, turn):
                    pe.wait_ge(s_taken, m + 1)
                    for i in range(pieces):
                        pe.wait_ge(s_lo, m * pieces + i + 1)
                        for k in range(width):
                            ins = products(nc, acc[:, bank, 0:t], part(w, slice(None), bank * pieces + i, slice(k * P, (k + 1) * P)),
                                           part(rhs, slice(None), i * width + k), start=(i == 0 and k == 0),
                                           stop=(i == pieces - 1 and k == width - 1))
                        ins.then_inc(s_used, 1)
                each_chunk(pe, 0, total, banks, body)

            @block.scalar
            def _(act):
                act.sem_inc(s_taken, banks)
                lead = banks // 2

                def hi(m, bank, turn):
                    for i in range(pieces):
                        slot = bank * pieces + i
                        act.wait_ge(s_loaded[slot], turn * 16 + 16)
                        act.wait_ge(s_used, m * pieces + i + 1)
                        nc.scalar.activation(w[0][:, slot, :], raw[:, slot, :], ACT.Copy).then_inc(s_hi, 1)

                def body(m, bank, turn):
                    hi(m + lead, (bank + lead) % banks, turn + (bank + lead) // banks)
                    take(m, bank, turn)

                def take(m, bank, turn):
                    act.wait_ge(s_used, m * pieces + 4 + pieces)
                    evacuate(m - first, acc[:, bank, 0:t]).then_inc(s_taken, 1)

                for m in range(lead):
                    hi(m, m, 0)
                first = 0
                for n, evacuate in segments:
                    ahead = min(n, total - lead - first)
                    each_chunk(act, first, ahead, banks, body)
                    for m in range(first + ahead, first + n):
                        take(m, m % banks, m // banks)
                    first += n


def copy_to(nc, dst, func=ACT.Copy, scale=1.0):
    def evacuate(index, psum):
        return nc.scalar.activation(dst[:, bass.ds(index, 1), :], psum.unsqueeze(1), func, scale=scale)
    return evacuate


def gate_to(nc, dst, gate):
    def evacuate(index, psum):
        for n in range(gate.shape[2]):
            half = slice(n * T, (n + 1) * T)
            ins = nc.scalar.activation(dst[:, bass.ds(index, 1), half], psum[:, half].unsqueeze(1), ACT.Copy,
                                       scale=gate[:, bass.ds(index, 1), n])
        return ins
    return evacuate


def token_major(nc, name, weights, n, xt, t, dst):
    with Stage(nc, name) as st:
        tiles = t // P
        width = n // -(-n // 512)
        groups = [(a, a + width) for a in range(0, n, width)]
        raw = st.sb("raw", [P, 4, n])
        w = st.sb("hi", [P, 4, n], F32R), st.sb("lo", [P, 4, n], F32R)
        acc = st.ps("acc", [P, tiles * len(groups), 512])
        s_loaded = [st.sem(f"loaded{r}") for r in range(4)]
        s_hi, s_lo, s_used = st.sem("hi"), st.sem("lo"), st.sem("used")
        with nc.Block() as block:
            @block.sync
            def _(sp):
                for k in range(KD):
                    if k >= 4:
                        sp.wait_ge(s_lo, k - 3)
                    sp.dma_start(raw[:, k % 4, :], weights[k]).then_inc(s_loaded[k % 4], 16)

            @block.vector
            def _(dve):
                for k in range(KD):
                    dve.wait_ge(s_hi, k + 1)
                    nc.vector.tensor_tensor(w[1][:, k % 4, :], raw[:, k % 4, :], w[0][:, k % 4, :].bitcast(F32),
                                            ALU.subtract).then_inc(s_lo, 1)

            @block.tensor
            def _(pe):
                for k in range(KD):
                    pe.wait_ge(s_lo, k + 1)
                    for i in range(tiles):
                        for g, (a, b) in enumerate(groups):
                            ins = products(nc, acc[:, i * len(groups) + g, 0:b - a], part(xt, slice(None), k, slice(i * P, (i + 1) * P)),
                                           part(w, slice(None), k % 4, slice(a, b)), start=(k == 0), stop=(k == KD - 1))
                    ins.then_inc(s_used, 1)

            @block.scalar
            def _(act):
                for k in range(KD):
                    act.wait_ge(s_loaded[k % 4], 16 * (k // 4 + 1))
                    if k >= 4:
                        act.wait_ge(s_used, k - 3)
                    nc.scalar.activation(w[0][:, k % 4, :], raw[:, k % 4, :], ACT.Copy).then_inc(s_hi, 1)
                act.wait_ge(s_used, KD)
                for i in range(tiles):
                    for g, (a, b) in enumerate(groups):
                        nc.scalar.activation(dst[:, i, a:b], acc[:, i * len(groups) + g, 0:b - a], ACT.Copy)


def modulate(nc, name, h, pair, x, mods, shift, cols, ahead=None):
    with Stage(nc, name) as st:
        s_h, s_hi = st.sem("h"), st.sem("hi")
        n = len(cols)
        with nc.Block() as block:
            if ahead:
                @block.sync
                def _(sp):
                    ahead.start(sp)

            @block.vector
            def _(dve):
                for k in range(KD):
                    for i, c in enumerate(cols):
                        half = slice(i * T, (i + 1) * T)
                        nc.vector.tensor_scalar(h[:, k, half], x[:, k, half], mods[:, shift + KD + k, c:c + 1],
                                                mods[:, shift + k, c:c + 1], ALU.mult, ALU.add).then_inc(s_h, 1)
                for k in range(KD):
                    dve.wait_ge(s_hi, k + 1)
                    nc.vector.tensor_tensor(pair[1][:, k], h[:, k], pair[0][:, k].bitcast(F32), ALU.subtract)
                nc.vector.tensor_scalar(x[:], x[:], ALPHA, None, ALU.mult)

            @block.scalar
            def _(act):
                for k in range(KD):
                    act.wait_ge(s_h, (k + 1) * n)
                    nc.scalar.activation(pair[0][:, k], h[:, k], ACT.Copy).then_inc(s_hi, 1)


def layer_norm(nc, name, x, z, sq, t, gain, bias, mean_of_d, residual=True):
    with Stage(nc, name) as st:
        ps_mean, ps_var = st.ps("mean", [P, 512]), st.ps("var", [P, 512])
        rstd = st.sb("rstd", [P, t])
        s_mean, s_var, s_centred, s_squared = st.sem("mean"), st.sem("var"), st.sem("centred"), st.sem("squared")
        s_step, s_root, s_scaled, s_added = st.sem("step"), st.sem("root"), st.sem("scaled"), st.sem("added")
        with nc.Block() as block:
            @block.tensor
            def _(pe):
                for k in range(KD):
                    if residual:
                        pe.wait_ge(s_added, k + 1)
                    ins = nc.tensor.matmul(ps_mean[:, 0:t], mean_of_d, z[:, k, :], start=(k == 0), stop=(k == KD - 1))
                ins.then_inc(s_mean, 1)
                for k in range(KD):
                    pe.wait_ge(s_squared, k + 1)
                    ins = nc.tensor.matmul(ps_var[:, 0:t], mean_of_d, sq[:, k, :], start=(k == 0), stop=(k == KD - 1))
                ins.then_inc(s_var, 1)

            @block.vector
            def _(dve):
                step = Steps(dve, s_step)
                if residual:
                    for k in range(KD):
                        nc.vector.tensor_tensor(z[:, k, :], z[:, k, :], x[:, k, :], ALU.add).then_inc(s_added, 1)
                dve.wait_ge(s_mean, 1)
                for k in range(KD):
                    nc.vector.tensor_tensor(z[:, k, :], z[:, k, :], ps_mean[:, 0:t], ALU.subtract).then_inc(s_centred, 1)
                dve.wait_ge(s_var, 1)
                step.link(nc.vector.tensor_scalar(rstd[:], ps_var[:, 0:t], LN_EPS, None, ALU.add))
                step.link(nc.vector.reciprocal(rstd[:], rstd[:]))
                dve.wait_ge(s_root, 1)
                for k in range(KD):
                    nc.vector.tensor_tensor(z[:, k, :], z[:, k, :], rstd[:], ALU.mult).then_inc(s_scaled, 1)

            @block.scalar
            def _(act):
                for k in range(KD):
                    act.wait_ge(s_centred, k + 1)
                    nc.scalar.activation(sq[:, k, :], z[:, k, :], ACT.Square).then_inc(s_squared, 1)
                act.wait_ge(s_step, 2)
                nc.scalar.activation(rstd[:], rstd[:], ACT.Sqrt).then_inc(s_root, 1)
                for k in range(KD):
                    act.wait_ge(s_scaled, k + 1)
                    nc.scalar.activation(x[:, k, :], z[:, k, :], ACT.Identity, bias=bias[:, k:k + 1],
                                         scale=gain[:, k:k + 1])


def modulation(nc, name, c, weights, bias, mods, ident):
    n = c.shape[2]
    groups = 6 * D // 512
    half = KD // 2
    with Stage(nc, name) as st:
        act_c = st.sb("act_c", [P, KD, n])
        wt = st.sb("weights", [P, 4, half, 512])
        rows = st.sb("rows", [n, groups, 512])
        acc = st.ps("acc", [P, 4, 512])
        cols = st.ps("cols", [P, 6 * KD, n])
        s_loaded = [st.sem(f"loaded{r}") for r in range(4)]
        s_silu, s_used, s_row, s_cols, s_bias = (st.sem(k) for k in ("silu", "used", "row", "cols", "bias"))
        with nc.Block() as block:
            @block.sync
            def _(sp):
                def fetch(u, slot, turn):
                    if not isinstance(u, int) or u >= 4:
                        sp.wait_ge(s_used, u - 3)
                    sp.dma_start(wt[:, slot], weights[bass.ds(u, 1)].rearrange("a p k c -> p (a k) c")).then_inc(s_loaded[slot], 16)
                for u in range(4):
                    fetch(u, u, 0)
                each_chunk(sp, 4, 2 * groups - 4, 4, fetch)

            @block.tensor
            def _(pe):
                pe.wait_ge(s_silu, 1)

                def body(g, b, turn):
                    pe.wait_ge(s_row, g + 1)
                    for i in range(2):
                        slot = 2 * b + i
                        pe.wait_ge(s_loaded[slot], turn * 16 + 16)
                        for k in range(half):
                            ins = nc.tensor.matmul(acc[0:n, b, :], act_c[:, i * half + k, :], wt[:, slot, k, :],
                                                   start=(i == 0 and k == 0), stop=(i == 1 and k == half - 1))
                        ins.then_inc(s_used, 1)
                each_chunk(pe, 0, groups, 2, body)
                pe.wait_ge(s_row, groups + 2)
                for m in range(6 * KD):
                    ins = nc.tensor.transpose(cols[:, m, :], rows[:, m // 4, m % 4 * P:(m % 4 + 1) * P], ident[0:n, 0:n])
                ins.then_inc(s_cols, 1)

            @block.scalar
            def _(act):
                nc.scalar.activation(act_c[:], c, ACT.Silu).then_inc(s_silu, 1)
                act.sem_inc(s_row, 2)

                def body(g, b, turn):
                    act.wait_ge(s_used, g * 2 + 2)
                    nc.scalar.activation(rows[:, bass.ds(g, 1), :], acc[0:n, b:b + 1, :], ACT.Copy).then_inc(s_row, 1)
                each_chunk(act, 0, groups, 2, body)

            @block.vector
            def _(dve):
                dve.wait_ge(s_cols, 1)
                nc.vector.tensor_tensor(mods[:], cols[:], bcast(bias, n), ALU.add).then_inc(s_bias, 1)
                dve.wait_ge(s_bias, 1)
                for first in (KD, 4 * KD):
                    nc.vector.tensor_scalar(mods[:, first:first + KD, :], mods[:, first:first + KD, :], 1.0, None, ALU.add)


class Conditioning:
    GROUPS = 3

    def __init__(self, nc, st, name, c, weights, bias, mods, ident):
        self.nc, self.weights, self.bias, self.mods, self.ident, self.n = nc, weights, bias, mods, ident, c.shape[2]
        self.c, self.silu = c, st.sb(name + "_silu", [P, KD, self.n])
        self.raw = st.sb(name + "_raw", [P, 3, KD // 2, 512])
        self.rows = st.sb(name + "_rows", [self.n, self.GROUPS, 512])
        self.acc, self.cols = st.ps(name + "_acc", [P, 2, 512]), st.ps(name + "_cols", [P, 4 * self.GROUPS, self.n])
        self.s_loaded = [st.sem(f"{name}_loaded{r}") for r in range(3)]
        self.s_silu, self.s_used, self.s_row, self.s_cols, self.s_added = (
            st.sem(f"{name}_{k}") for k in ("silu", "used", "row", "cols", "added"))

    def sync(self, sp, start):
        for u in range(2 * self.GROUPS):
            if u >= 3:
                sp.wait_ge(self.s_used, u - 2)
            sp.dma_start(self.raw[:, u % 3], self.weights[start * 2 + u]).then_inc(self.s_loaded[u % 3], 16)

    def scalar(self, act):
        self.nc.scalar.activation(self.silu[:], self.c, ACT.Silu).then_inc(self.s_silu, 1)
        for g in range(self.GROUPS):
            act.wait_ge(self.s_used, 2 * g + 2)
            self.nc.scalar.activation(self.rows[:, g, :], self.acc[0:self.n, g % 2, :], ACT.Copy).then_inc(self.s_row, 1)

    def tensor(self, pe):
        nc, n = self.nc, self.n
        pe.wait_ge(self.s_silu, 1)
        for g in range(self.GROUPS):
            if g >= 2:
                pe.wait_ge(self.s_row, g - 1)
            for i in range(2):
                u = 2 * g + i
                pe.wait_ge(self.s_loaded[u % 3], (u // 3 + 1) * 16)
                for k in range(KD // 2):
                    ins = nc.tensor.matmul(self.acc[0:n, g % 2, :], self.silu[:, i * KD // 2 + k, :], self.raw[:, u % 3, k, :],
                                           start=(i == 0 and k == 0), stop=(i == 1 and k == KD // 2 - 1))
                ins.then_inc(self.s_used, 1)
        pe.wait_ge(self.s_row, self.GROUPS)
        for m in range(4 * self.GROUPS):
            ins = nc.tensor.transpose(self.cols[:, m, :], self.rows[:, m // 4, m % 4 * P:(m % 4 + 1) * P], self.ident[0:n, 0:n])
        ins.then_inc(self.s_cols, 1)

    def vector(self, dve, start):
        nc, first, last = self.nc, 4 * start, 4 * (start + self.GROUPS)
        dve.wait_ge(self.s_cols, 1)
        nc.vector.tensor_tensor(self.mods[:, first:last, :], self.cols[:], bcast(self.bias[:, first:last], self.n),
                                ALU.add).then_inc(self.s_added, 1)
        dve.wait_ge(self.s_added, 1)
        for scale in (KD, 4 * KD):
            a, b = max(scale, first), min(scale + KD, last)
            if a < b:
                nc.vector.tensor_scalar(self.mods[:, a:b, :], self.mods[:, a:b, :], 1.0, None, ALU.add)


def conv_ffn(nc, name, pair, up_ahead, conv, w_down, z, gate):
    with Stage(nc, name) as st:
        hidden_pair = st.sb("hidden_hi", [P, KF, T], F32R), st.sb("hidden_lo", [P, KF, T], F32R)
        down_ahead = Ahead(nc, st, "down", w_down, KF)
        with Stage(nc, name + "_up") as up:
            hidden = up.sb("hidden", [P, KF, T])
            raw, s_loaded = up_ahead.raw, up_ahead.s_loaded
            w = up.sb("hi", [P, 4, KD * P], F32R), up.sb("lo", [P, 4, KD * P], F32R)
            acc = up.ps("acc", [P, 4, 512])
            ubuf = up.sb("u", [P, 2, T + 2])
            cbuf, sbuf = up.sb("c", [P, 2, T]), up.sb("s", [P, 2, T])
            s_hi, s_lo, s_summed, s_taken, s_zero = (up.sem(n) for n in ("hi", "lo", "summed", "taken", "zero"))
            s_u, s_tap, s_silu, s_hidden, s_hidden_hi = (up.sem(n) for n in ("u", "tap", "silu", "hidden", "hidden_hi"))
            with nc.Block() as block:
                @block.sync
                def _(sp):
                    each_chunk(sp, 4, 2 * KF - 4, 4, lambda m, slot, turn: up_ahead.fetch(sp, m, slot, s_lo))
                    down_ahead.start(sp)

                @block.tensor
                def _(pe):
                    pe.sem_inc(s_summed, 4)

                    def body(m, slot, turn):
                        pe.wait_ge(s_lo, m + 1)
                        pe.wait_ge(s_taken, m + 1)
                        for k in range(KD):
                            ins = products(nc, acc[:, slot, 0:T], part(w, slice(None), slot, slice(k * P, (k + 1) * P)),
                                           part(pair, slice(None), k), start=(k == 0), stop=(k == KD - 1))
                        ins.then_inc(s_summed, 1)
                    each_chunk(pe, 0, 2 * KF, 4, body)

                @block.scalar
                def _(act):
                    act.sem_inc(s_taken, 4)
                    act.wait_ge(s_zero, 1)

                    def hi(m, slot, turn):
                        act.wait_ge(s_loaded[slot], turn * 16 + 16)
                        act.wait_ge(s_summed, m + 1)
                        nc.scalar.activation(w[0][:, slot, :], raw[:, slot, :], ACT.Copy).then_inc(s_hi, 1)

                    def taps(f, b, turn, more=True):
                        act.wait_ge(s_summed, f * 2 + 5)
                        act.wait_ge(s_tap, f * 3 + 3)
                        nc.scalar.activation(ubuf[:, b, 2:2 + T], acc[:, 2 * b, 0:T], ACT.Copy).then_inc(s_u, 1)
                        if more:
                            hi(f * 2 + 4, 2 * b, turn + 1)
                            hi(f * 2 + 5, 2 * b + 1, turn + 1)
                        act.wait_ge(s_u, f + 1)
                        act.sem_inc(s_taken, 1)

                    def finish(f, b):
                        act.wait_ge(s_tap, f * 3 + 9)
                        nc.scalar.activation(sbuf[:, b, :], cbuf[:, b, :], ACT.Silu).then_inc(s_silu, 1)
                        act.wait_ge(s_hidden, f + 1)
                        act.sem_inc(s_taken, 1)
                        nc.scalar.activation(hidden_pair[0][:, bass.ds(f, 1), :], hidden[:, bass.ds(f, 1), :],
                                             ACT.Copy).then_inc(s_hidden_hi, 1)

                    def body(f, slot, turn):
                        finish(f, slot % 2)
                        taps(f + 1, (slot + 1) % 2, turn * 2 + (slot + 1) // 2)

                    for m in range(4):
                        hi(m, m, 0)
                    taps(0, 0, 0)
                    each_chunk(act, 0, KF - 3, 4, body)
                    for f in range(KF - 3, KF):
                        finish(f, f % 2)
                        if f + 1 < KF:
                            taps(f + 1, (f + 1) % 2, None, more=False)

                @block.vector
                def _(dve):
                    nc.vector.memset(ubuf[:], 0.0).then_inc(s_zero, 1)
                    dve.sem_inc(s_tap, 6)

                    def lo(m, slot):
                        dve.wait_ge(s_hi, m + 1)
                        nc.vector.tensor_tensor(w[1][:, slot, :], raw[:, slot, :], w[0][:, slot, :].bitcast(F32),
                                                ALU.subtract).then_inc(s_lo, 1)

                    def hidden_lo(f):
                        dve.wait_ge(s_hidden_hi, f + 1)
                        nc.vector.tensor_tensor(hidden_pair[1][:, bass.ds(f, 1), :], hidden[:, bass.ds(f, 1), :],
                                                hidden_pair[0][:, bass.ds(f, 1), :].bitcast(F32), ALU.subtract)

                    def body(f, b, turn, more=True):
                        dve.wait_ge(s_u, f + 1)
                        nc.vector.tensor_scalar(cbuf[:, b, :], ubuf[:, b, 0:T], conv[:, bass.ds(f, 1), 0],
                                                conv[:, bass.ds(f, 1), 3], ALU.mult, ALU.add).then_inc(s_tap, 1)
                        for j in (1, 2):
                            dve.wait_ge(s_tap, f * 3 + 6 + j)
                            nc.vector.scalar_tensor_tensor(cbuf[:, b, :], ubuf[:, b, j:j + T], conv[:, bass.ds(f, 1), j],
                                                           cbuf[:, b, :], ALU.mult, ALU.add).then_inc(s_tap, 1)
                        if more:
                            lo(f * 2 + 4, 2 * b)
                            lo(f * 2 + 5, 2 * b + 1)
                        if not isinstance(f, int) or f >= 1:
                            hidden_lo(f - 1)
                        dve.wait_ge(s_silu, f + 1)
                        dve.wait_ge(s_summed, f * 2 + 6)
                        nc.vector.tensor_tensor(hidden[:, bass.ds(f, 1), :], sbuf[:, b:b + 1, :],
                                                acc[:, 2 * b + 1:2 * b + 2, 0:T], ALU.mult).then_inc(s_hidden, 1)
                    for m in range(4):
                        lo(m, m)
                    body(0, 0, 0)
                    body(1, 1, 0)
                    with dve.Fori(1, KF // 2 - 1) as i:
                        for b in range(2):
                            body(i * 2 + b, b, i)
                    for f in (KF - 2, KF - 1):
                        body(f, f % 2, None, more=False)
                    hidden_lo(KF - 1)
        project(nc, name + "_down", down_ahead, KF, hidden_pair, T, [(KD, gate_to(nc, z, gate))])


def decayed_scores(nc, name, q, k, directions, masks, at, off, ctx=None):
    with Stage(nc, name) as st:
        nd, last = len(directions), LEVELS + 1 + (ctx is not None)
        qd, kd = st.sb("qd", [P, 2, H, T]), st.sb("kd", [P, 2, H, T])
        near, far, exp_near, exp_far = (st.sb(n, [P, H, T]) for n in ("near", "far", "exp_near", "exp_far"))
        zeros = st.sb("zeros", [P, T])
        acc = st.ps("acc", [P, 2, H * NT, P])
        ctx_acc = st.ps("ctx_acc", [P, 2, H, T]) if ctx else None
        s_init, s_ready, s_scored, s_kept, s_exp, s_grown = (
            st.sem(n) for n in ("init", "ready", "scored", "kept", "exp", "grown"))
        plan = [(0, 0)] + [(d, level) for d in range(nd) for level in range(1, last + 1)]
        grown = lambda d, level: 2 * (d * last + level)
        kept = lambda n: sum(level <= LEVELS + 1 for _, level in plan[:n + 1])

        def halves(ap, size):
            return ap.rearrange("p h (b c s) -> p (h b) c s", c=2, s=size)

        def sides(d):
            return (0, 1) if directions[d][1] else (1, 0)

        with nc.Block() as block:
            @block.vector
            def _(dve):
                init = Steps(dve, s_init)
                init.done(nc.vector.memset(at, 0.0))
                init.done(nc.vector.memset(zeros[:], 0.0))
                init.done(nc.vector.memset(qd[:, 1], 0.0))
                init.link(nc.vector.memset(kd[:, 1], 0.0))
                nc.vector.tensor_scalar(qd[:, 0], q, float(nd), None, ALU.mult).then_inc(s_ready, 1)
                nc.vector.tensor_copy(kd[:, 0], k).then_inc(s_ready, 1)

                def keep(n):
                    d, level = plan[n]
                    if level > LEVELS + 1:
                        return
                    dve.wait_ge(s_scored, n + 1)
                    if level == LEVELS + 1:
                        ins = nc.vector.tensor_copy(off[d], acc[:, n % 2, 0:H, :])
                    else:
                        if n >= 1:
                            dve.wait_ge(s_kept, kept(n - 1))
                        ins = nc.vector.copy_predicated(at, over(masks[d][:, level, :], H * NT), acc[:, n % 2])
                    ins.then_inc(s_kept, 1)

                for n, (d, level) in enumerate(plan):
                    if n == 0:
                        continue
                    g, backwards = directions[d]
                    tc, sc = sides(d)
                    if level == 1:
                        nc.vector.tensor_copy(near[:], g).then_inc(s_grown, 1)
                        nc.vector.memset(far[:], 0.0).then_inc(s_grown, 1)
                        dve.wait_ge(s_grown, grown(d, 1))
                    b, size = n % 2, 2 ** (level - 1)
                    dve.wait_ge(s_exp, 2 * n)
                    if n >= 2:
                        dve.wait_ge(s_scored, n - 1)
                        dve.wait_ge(s_ready, 2 * n)
                    if level <= LEVELS + 1:
                        nc.vector.tensor_tensor(halves(qd[:, b], size)[:, :, tc], halves(q, size)[:, :, tc],
                                                halves(exp_near[:], size)[:, :, tc], ALU.mult).then_inc(s_ready, 1)
                        nc.vector.tensor_tensor(halves(kd[:, b], size)[:, :, sc], halves(k, size)[:, :, sc],
                                                halves(exp_far[:], size)[:, :, sc], ALU.mult).then_inc(s_ready, 1)
                    else:
                        nc.vector.tensor_tensor(qd[:, b], q, exp_near[:], ALU.mult).then_inc(s_ready, 1)
                        nc.vector.tensor_tensor(kd[:, b], ctx[0], exp_far[:], ALU.mult).then_inc(s_ready, 1)
                    if level < last:
                        near_h, far_h = halves(near[:], size), halves(far[:], size)
                        edge = 0 if backwards else size - 1
                        blocks = H * T // (2 * size)
                        total = lambda c: near_h[:, :, c, edge:edge + 1].broadcast_to([P, blocks, size])
                        if level <= LEVELS:
                            nc.vector.tensor_tensor(far_h[:, :, sc], far_h[:, :, sc], total(tc),
                                                    ALU.add).then_inc(s_grown, 1)
                        else:
                            cg = ctx[1][d]
                            init.link(nc.vector.memset(far[:], 0.0))
                            for h in range(H):
                                out, src = ((far[:, h, 1:T], cg[:, h, 0:T - 1]) if backwards else
                                            (far[:, h, T - 2::-1], cg[:, h, T - 1:0:-1]))
                                ins = nc.vector.tensor_tensor_scan(out, zeros[:, 0:T - 1], src, 0.0, ALU.add, ALU.add)
                            ins.then_inc(s_grown, 1)
                        dve.wait_ge(s_grown, grown(d, level) + 1)
                        nc.vector.tensor_tensor(near_h[:, :, tc], near_h[:, :, tc], total(sc),
                                                ALU.add).then_inc(s_grown, 1)
                        dve.wait_ge(s_grown, grown(d, level + 1))
                    keep(n - 1)
                keep(len(plan) - 1)

            @block.scalar
            def _(act):
                for n, (d, level) in enumerate(plan):
                    if n == 0:
                        continue
                    tc, sc = sides(d)
                    act.wait_ge(s_grown, grown(d, level))
                    act.wait_ge(s_ready, 2 * n)
                    if level <= LEVELS + 1:
                        size = 2 ** (level - 1)
                        pairs = [(halves(a[:], size)[:, :, c], halves(b[:], size)[:, :, c])
                                 for a, b, c in ((exp_near, near, tc), (exp_far, far, sc))]
                    else:
                        pairs = [(exp_near[:], near[:]), (exp_far[:], far[:])]
                    for out, src in pairs:
                        nc.scalar.activation(out, src, ACT.Exp).then_inc(s_exp, 1)
                if ctx:
                    act.wait_ge(s_scored, len(plan))
                    for i in range(2):
                        nc.scalar.activation(ctx[2][:, i], ctx_acc[:, i], ACT.Copy)

            @block.tensor
            def _(pe):
                for n, (d, level) in enumerate(plan):
                    b = n % 2
                    pe.wait_ge(s_ready, 2 * n + 2)
                    if n >= 2:
                        pe.wait_ge(s_kept, kept(n - 2))
                    for h in range(H):
                        if level <= LEVELS:
                            for i in range(NT):
                                tile = slice(i * P, (i + 1) * P)
                                ins = nc.tensor.matmul(acc[:, b, h * NT + i, :], kd[:, b, h, tile], qd[:, b, h, tile],
                                                       start=True, stop=True)
                        elif level == LEVELS + 1:
                            tc, sc = sides(d)
                            ins = nc.tensor.matmul(acc[:, b, h, :], kd[:, b, h, sc * P:(sc + 1) * P],
                                                   qd[:, b, h, tc * P:(tc + 1) * P], start=True, stop=True)
                        else:
                            for i in range(2):
                                ins = nc.tensor.matmul(ctx_acc[:, i, h, :], kd[:, b, h, i * P:(i + 1) * P], qd[:, b, h, :],
                                                       start=(d == 0 and h % 2 == 0), stop=(d == nd - 1),
                                                       skip_group_check=True)
                    ins.then_inc(s_scored, 1)


def weighted_values(nc, name, v, width, at, off, out, ctx=None):
    with Stage(nc, name) as st:
        chunks = H * width // P
        acc = st.ps("acc", [P, chunks, T])
        s_summed = st.sem("summed")
        with nc.Block() as block:
            @block.tensor
            def _(pe):
                for c in range(chunks):
                    h, cols = c * P // width, slice(c * P, (c + 1) * P)
                    for i in range(NT):
                        tile = slice(i * P, (i + 1) * P)
                        terms = [(v[i], at[:, h * NT + i, :])]
                        if i == 1:
                            terms.append((v[0], off[0][:, h, :]))
                        elif len(off) > 1:
                            terms.append((v[1], off[1][:, h, :]))
                        if ctx:
                            terms += [(ctx[0][j], ctx[1][:, j, h, tile]) for j in range(2)]
                        for n, (value, score) in enumerate(terms):
                            ins = nc.tensor.matmul(acc[:, c, tile], value[:, cols], score,
                                                   start=(n == 0), stop=(n == len(terms) - 1))
                    ins.then_inc(s_summed, 1)

            @block.scalar
            def _(act):
                for c in range(chunks):
                    act.wait_ge(s_summed, c // 2 * 2 + 2)
                    nc.scalar.activation(out[:, c, :], acc[:, c, :], ACT.Copy)


def head_norm(nc, name, o, y, gate, weight, per_head, t, eps, mean_of_p):
    with Stage(nc, name) as st:
        chunks = o.shape[1]
        heads = chunks // per_head
        in_bank = 512 // t
        sq, rstd = st.sb("sq", [P, 2, t]), st.sb("rstd", [P, heads, t])
        acc = st.ps("acc", [P, heads, t])
        s_squared, s_mean, s_step, s_root, s_weighted = (st.sem(n) for n in ("squared", "mean", "step", "root", "weighted"))
        with nc.Block() as block:
            @block.scalar
            def _(act):
                for c in range(chunks):
                    if c >= 2:
                        act.wait_ge(s_mean, c - 1)
                    nc.scalar.activation(sq[:, c % 2, :], o[:, c, :], ACT.Square).then_inc(s_squared, 1)
                act.wait_ge(s_step, 2 * heads)
                nc.scalar.activation(rstd[:], rstd[:], ACT.Sqrt).then_inc(s_root, 1)

            @block.tensor
            def _(pe):
                for c in range(chunks):
                    pe.wait_ge(s_squared, c + 1)
                    nc.tensor.matmul(acc[:, c // per_head, :], mean_of_p, sq[:, c % 2, :], start=(c % per_head == 0),
                                     stop=(c % per_head == per_head - 1)).then_inc(s_mean, 1)

            @block.vector
            def _(dve):
                step = Steps(dve, s_step)
                for h in range(heads):
                    dve.wait_ge(s_mean, (h // in_bank + 1) * in_bank * per_head)
                    step.link(nc.vector.tensor_scalar(rstd[:, h, :], acc[:, h, :], 1.0 / per_head, eps, ALU.mult, ALU.add))
                    step.done(nc.vector.reciprocal(rstd[:, h, :], rstd[:, h, :]))
                for c in range(chunks):
                    nc.vector.scalar_tensor_tensor(y[:, c, :], o[:, c, :], weight(c), gate[:, c, :],
                                                   ALU.mult, ALU.mult).then_inc(s_weighted, 1)
                dve.wait_ge(s_root, 1)
                for c in range(chunks):
                    dve.wait_ge(s_weighted, c + 1)
                    nc.vector.tensor_tensor(y[:, c, :], y[:, c, :], rstd[:, c // per_head, :], ALU.mult)


def rope(nc, name, qk, perm_t, cos, sin):
    with Stage(nc, name) as st:
        chunks = qk.shape[1]
        acc = st.ps("acc", [P, chunks + 1, T])
        turned = st.sb("turned", [P, chunks, T])
        s_perm, s_turned, s_cos = st.sem("perm"), st.sem("turned"), st.sem("cos")
        with nc.Block() as block:
            @block.tensor
            def _(pe):
                for c in range(chunks):
                    nc.tensor.matmul(acc[:, c, :], perm_t, qk[:, c, :], start=True, stop=True).then_inc(s_perm, 1)

            @block.vector
            def _(dve):
                dve.wait_ge(s_perm, chunks)
                nc.vector.tensor_tensor(turned[:], acc[:, 0:chunks, :], over(sin, chunks), ALU.mult).then_inc(s_turned, 1)
                nc.vector.tensor_tensor(qk, qk, over(cos, chunks), ALU.mult).then_inc(s_cos, 1)
                dve.wait_ge(s_turned, 1)
                dve.wait_ge(s_cos, 1)
                nc.vector.tensor_tensor(qk, qk, turned[:], ALU.add)


def rope_tables(nc, name, positions, inv_freq, cos, sin):
    with Stage(nc, name) as st:
        pos, ang, turns, cosine = st.sb("pos", [P, T]), st.sb("ang", [P, T]), st.sb("turns", [P, T]), st.sb("cosine", [P, T])
        s_step = st.sem("step")
        with nc.Block() as block:
            @block.vector
            def _(dve):
                step = Steps(dve, s_step)
                step.link(nc.vector.tensor_copy(pos[:], positions))
                step.link(nc.vector.tensor_scalar(ang[:], pos[:], inv_freq, None, ALU.mult))
                step.link(nc.vector.tensor_scalar(turns[:], ang[:], float(0.5 / np.pi), ROUND, ALU.mult, ALU.add))
                step.link(nc.vector.tensor_scalar(turns[:], turns[:], ROUND, None, ALU.subtract))
                for part in (EVEN_PI_1, EVEN_PI_2, EVEN_PI_3):
                    step.link(nc.vector.scalar_tensor_tensor(ang[:], turns[:], -float(part), ang[:], ALU.mult, ALU.add))
                step.link(nc.vector.tensor_scalar(cosine[:], ang[:], float(np.pi / 2), None, ALU.add))
                step.link(nc.vector.tensor_scalar(turns[:], cosine[:], float(np.pi), float(-2 * np.pi), ALU.is_gt, ALU.mult))
                step.link(nc.vector.tensor_tensor(cosine[:], cosine[:], turns[:], ALU.add))
                for a in (ang, cosine):
                    step.link(nc.vector.tensor_scalar(a[:], a[:], 3.1415925, -3.1415925, ALU.min, ALU.max))

            @block.scalar
            def _(act):
                act.wait_ge(s_step, 12)
                nc.scalar.activation(sin, ang[:], ACT.Sin)
                nc.scalar.activation(cos, cosine[:], ACT.Sin)


def attention(nc, name, tiles, sinks, o, ident):
    with Stage(nc, name) as st:
        pair = 2
        scores = st.ps("scores", [P, 2, pair, 512])
        turned = st.ps("turned", [P, pair, 4, P])
        values, back = st.ps("values", [P, 512]), st.ps("back", [P, GQA, P])
        p, pt = st.sb("p", [P, 2, pair, 512]), st.sb("pt", [P, 2, pair, 4, P])
        m, minus_m = st.sb("m", [P, 2, pair]), st.sb("minus_m", [P, 2, pair])
        sink, denom = st.sb("sink", [P, 3, pair]), st.sb("denom", [P, 3, pair])
        o_tok = st.sb("o_tok", [P, 2, P])
        (s_scores, s_step, s_arg, s_exp, s_turned, s_pt, s_values, s_div, s_o, s_back, s_out) = (
            st.sem(n) for n in ("scores", "step", "arg", "exp", "turned", "pt", "values", "div", "o", "back", "out"))
        per_tile = A_HEADS // pair
        items = [(i, g, c) for i in range(len(tiles)) for g in range(2) for c in range(0, GQA, pair)]
        EXPS = pair + 1
        steps = range(-1, len(items) + 4)
        live = lambda n: 0 <= n < len(items)

        with nc.Block() as block:
            @block.tensor
            def _(pe):
                def score(n):
                    i, g, first = items[n]
                    q, ks, vs, mask, cols = tiles[i]
                    rows = slice(g * A_DIM, (g + 1) * A_DIM)
                    if n >= 2:
                        pe.wait_ge(s_exp, EXPS * (n - 1))
                    for c in range(pair):
                        at = 0
                        for kt in ks:
                            w = kt.shape[1]
                            ins = nc.tensor.matmul(scores[:, n % 2, c, at:at + w], q(first + c)[rows], kt[rows],
                                                   start=True, stop=True)
                            at += w
                    ins.then_inc(s_scores, 1)

                def turn(n):
                    vs = tiles[items[n][0]][2]
                    pe.wait_ge(s_exp, EXPS * (n + 1))
                    if n >= 1:
                        pe.wait_ge(s_pt, n)
                    for c in range(pair):
                        for j in range(len(vs)):
                            ins = nc.tensor.transpose(turned[:, c, j, :], p[:, n % 2, c, j * P:(j + 1) * P], ident)
                    ins.then_inc(s_turned, 1)

                def value(n):
                    i, g, first = items[n]
                    vs = tiles[i][2]
                    pe.wait_ge(s_pt, n + 1)
                    if n >= 1:
                        pe.wait_ge(s_o, n)
                    for c in range(pair):
                        for j, v in enumerate(vs):
                            ins = nc.tensor.matmul(values[:, c * A_DIM:(c + 1) * A_DIM], pt[:, n % 2, c, j, :], v[:, g, :],
                                                   start=(j == 0), stop=(j == len(vs) - 1))
                    ins.then_inc(s_values, 1)

                def features_first(n):
                    pe.wait_ge(s_o, n + 1)
                    if n % per_tile == 0 and n:
                        pe.wait_ge(s_out, n // per_tile)
                    nc.tensor.transpose(back[:, n % per_tile, :], o_tok[:, n % 2, :], ident).then_inc(s_back, 1)

                for n in steps:
                    for work, item in ((score, n + 1), (turn, n), (value, n - 1), (features_first, n - 2)):
                        if live(item):
                            work(item)

            @block.vector
            def _(dve):
                step = Steps(dve, s_step)

                def maximum(n):
                    i, g, first = items[n]
                    q, ks, vs, mask, cols = tiles[i]
                    w, b = len(vs) * P, n % 2
                    sk = sinks[:, g * GQA + first:g * GQA + first + pair]
                    dve.wait_ge(s_scores, n + 1)
                    if mask is not None:
                        if n >= 2:
                            dve.wait_ge(s_turned, n - 1)
                        step.link(nc.vector.scalar_tensor_tensor(p[:, b, :, 0:w], scores[:, b, :, 0:w], A_DIM ** -0.5,
                                                                 over(mask, pair), ALU.mult, ALU.add))
                    src = scores if mask is None else p
                    step.link(nc.vector.tensor_reduce(m[:, b], src[:, b, :, 0:w], AX.X, ALU.max))
                    step.link(nc.vector.scalar_tensor_tensor(m[:, b], m[:, b], A_DIM ** -0.5 if mask is None else 1.0, sk,
                                                             ALU.mult, ALU.max))
                    if n >= 2:
                        dve.wait_ge(s_exp, EXPS * (n - 1))
                    nc.vector.tensor_scalar(minus_m[:, b], m[:, b], -1.0, None, ALU.mult).then_inc(s_arg, 1)
                    nc.vector.tensor_tensor(sink[:, n % 3], sk, m[:, b], ALU.subtract).then_inc(s_arg, 1)

                def divide(n):
                    b = n % 3
                    dve.wait_ge(s_exp, EXPS * (n + 1))
                    nc.vector.tensor_tensor(denom[:, b], denom[:, b], sink[:, b], ALU.add).then_inc(s_div, 1)
                    dve.wait_ge(s_div, 2 * n + 1)
                    nc.vector.reciprocal(denom[:, b], denom[:, b]).then_inc(s_div, 1)
                    dve.wait_ge(s_div, 2 * n + 2)
                    dve.wait_ge(s_values, n + 1)
                    if n >= 2:
                        dve.wait_ge(s_back, n - 1)
                    nc.vector.tensor_tensor(o_tok[:, n % 2].rearrange("p (c e) -> p c e", c=pair),
                                            values[:, 0:pair * A_DIM].rearrange("p (c e) -> p c e", c=pair),
                                            bcast(denom[:, b], A_DIM), ALU.mult).then_inc(s_o, 1)

                for n in steps:
                    for work, item in ((maximum, n), (divide, n - 2)):
                        if live(item):
                            work(item)

            @block.scalar
            def _(act):
                def exponentials(n):
                    mask, w, b = tiles[items[n][0]][3], len(tiles[items[n][0]][2]) * P, n % 2
                    act.wait_ge(s_arg, 2 * n + 2)
                    if n >= 2:
                        act.wait_ge(s_turned, n - 1)
                    if n >= 3:
                        act.wait_ge(s_o, n - 2)
                    src, scale = (scores, A_DIM ** -0.5) if mask is None else (p, 1.0)
                    for c in range(pair):
                        nc.scalar.activation(p[:, b, c, 0:w], src[:, b, c, 0:w], ACT.Exp, bias=minus_m[:, b, c:c + 1],
                                             scale=scale, accum_out=denom[:, n % 3, c:c + 1]).then_inc(s_exp, 1)
                    nc.scalar.activation(sink[:, n % 3], sink[:, n % 3], ACT.Exp).then_inc(s_exp, 1)

                def copy(n):
                    vs = tiles[items[n][0]][2]
                    act.wait_ge(s_turned, n + 1)
                    if n >= 2:
                        act.wait_ge(s_values, n - 1)
                    nc.scalar.activation(pt[:, n % 2, :, 0:len(vs), :], turned[:, :, 0:len(vs), :], ACT.Copy).then_inc(s_pt, 1)

                def store_tile(n):
                    if n % per_tile == per_tile - 1:
                        act.wait_ge(s_back, n + 1)
                        nc.scalar.activation(o[:, :, tiles[items[n][0]][4]], back[:], ACT.Copy).then_inc(s_out, 1)

                for n in steps:
                    for work, item in ((exponentials, n), (copy, n - 1), (store_tile, n - 3)):
                        if live(item):
                            work(item)


def pool_mixer(nc, name, h, w_pool, scale, inv_count_dram, z, gate, scaled):
    with Stage(nc, name) as st:
        pad = max(POOL_WINDOWS)
        a, b = st.sb("a", [P, KD, pad + T]), st.sb("b", [P, KD, pad + T])
        w = st.sb("w", [P, KD, 2, P])
        inv_count = st.sb("inv_count", [P, len(POOL_WINDOWS), T])
        gs = st.sb("gs", [P, KD])
        acc = st.ps("acc", [P, KD, T])
        s_counts, s_loaded, s_step, s_summed = st.sem("counts"), st.sem("loaded"), st.sem("step"), st.sem("summed")
        with nc.Block() as block:
            @block.sync
            def _(sp):
                sp.dma_start(inv_count[:], inv_count_dram).then_inc(s_counts, 16)
                sp.dma_start(w[:], w_pool).then_inc(s_loaded, 16)

            @block.vector
            def _(dve):
                step = Steps(dve, s_step)
                step.done(nc.vector.memset(a[:, :, 0:pad], 0.0))
                step.done(nc.vector.memset(b[:, :, 0:pad], 0.0))
                step.done(nc.vector.tensor_tensor(gs[:], gate[:, :, 0], scale, ALU.mult))
                step.link(nc.vector.tensor_copy(a[:, :, pad:], h))
                dve.wait_ge(s_counts, 16)
                src, dst, size = a, b, 1
                for g, window in enumerate(POOL_WINDOWS):
                    ks = slice(2 * g, KD)
                    step.link(nc.vector.tensor_tensor(dst[:, ks, pad:], src[:, ks, pad:],
                                                      src[:, ks, pad - size:pad + T - size], ALU.add))
                    size *= 2
                    own = slice(2 * g, 2 * g + 2)
                    step.link(nc.vector.tensor_tensor(src[:, own, pad:], dst[:, own, pad:], over(inv_count[:, g, :], 2), ALU.mult))
                    step.link(nc.vector.tensor_tensor(h[:, own, :], src[:, own, pad:], h[:, own, :], ALU.subtract))
                    src, dst = dst, src
                dve.wait_ge(s_summed, 1)
                for m in range(KD):
                    nc.vector.scalar_tensor_tensor(z[:, m, :], acc[:, m, :], gs[:, m:m + 1], scaled[:, m, :],
                                                   ALU.mult, ALU.add)

            @block.tensor
            def _(pe):
                pe.wait_ge(s_loaded, 16)
                pe.wait_ge(s_step, 4 + 3 * len(POOL_WINDOWS))
                for m in range(KD):
                    for j in range(2):
                        ins = nc.tensor.matmul(acc[:, m, :], w[:, m, j, :], h[:, m // 2 * 2 + j, :], start=(j == 0), stop=(j == 1))
                ins.then_inc(s_summed, 1)


def log_sigmoid_rows(nc, name, h, w_gates, gate_b, rows, u_cols, ident):
    with Stage(nc, name) as st:
        acc = st.ps("acc", [P, 512])
        cols = st.ps("cols", [P, 2, 4, H])
        w_wide = st.sb("w_wide", [P, KD, 4, 32])
        gates = [[st.sb(f"gate{d}{i}", [H, 2 * T]) for i in range(2)] for d in range(2)]
        tmp = [[st.sb(f"tmp{d}{i}", [H, 2 * T]) for i in range(2)] for d in range(2)]
        u = [st.sb(f"u{d}", [H, 2 * T]) for d in range(2)]
        zeros = st.sb("zeros", [H, 2 * T])
        s_wide, s_summed, s_step, s_act, s_u, s_cols = (st.sem(n) for n in ("wide", "summed", "step", "act", "u", "cols"))
        with nc.Block() as block:
            @block.tensor
            def _(pe):
                pe.wait_ge(s_wide, 2)
                for k in range(KD):
                    ins = nc.tensor.matmul(acc[:], w_wide[:, k].rearrange("p n c -> p (n c)"), h[:, k, :],
                                           start=(k == 0), stop=(k == KD - 1))
                ins.then_inc(s_summed, 1)
                pe.wait_ge(s_u, 2)
                for d in range(2):
                    for i in range(4):
                        ins = nc.tensor.transpose(cols[:, d, i, :], u[d][:, i * P:(i + 1) * P], ident[0:H, 0:H])
                ins.then_inc(s_cols, 1)

            @block.vector
            def _(dve):
                step = Steps(dve, s_step)
                nc.vector.memset(w_wide[:], 0.0).then_inc(s_wide, 1)
                dve.wait_ge(s_wide, 1)
                nc.vector.tensor_copy(w_wide[:, :, :, 0:H], w_gates[:].rearrange("p k (n c) -> p k n c", n=4)).then_inc(s_wide, 1)
                step.done(nc.vector.memset(zeros[:], 0.0))
                dve.wait_ge(s_summed, 1)
                for d in range(2):
                    for i in range(2):
                        n = 2 * d + i
                        step.link(nc.vector.tensor_scalar(gates[d][i][:], acc[32 * n:32 * n + H, :], gate_b[:, n:n + 1], None, ALU.add))
                    step.link(nc.vector.scalar_tensor_tensor(tmp[d][0][:], gates[d][1][:], -1.0, gates[d][1][:], ALU.mult, ALU.min))
                for d in range(2):
                    li, lf, cum, big = gates[d][0], gates[d][1], tmp[d][0], rows[d][0]
                    dve.wait_ge(s_act, 2 * d + 2)
                    step.link(nc.vector.scalar_tensor_tensor(lf[:], lf[:], 0.0, tmp[d][1][:], ALU.min, ALU.subtract))

                    def scan(out, src, op):
                        start = 0.0
                        for a in (0, T):
                            if d == 0:
                                o, s, end = out[:, a:a + T], src[:, a:a + T], out[:, T - 1:T]
                            else:
                                o = out[:, a + T - 1:(a - 1 if a else None):-1]
                                s, end = src[:, a + T - 1:(a - 1 if a else None):-1], out[:, 0:1]
                            step.link(nc.vector.tensor_tensor_scan(o, zeros[:, 0:T], s, start, ALU.add, op))
                            start = end
                    scan(cum, lf, ALU.add)
                    nc.vector.tensor_tensor(u[d][:], li[:], cum[:], ALU.subtract).then_inc(s_u, 1)
                    dve.wait_ge(s_u, d + 1)
                    scan(big, u[d], ALU.max)
                    step.link(nc.vector.tensor_tensor(rows[d][1][:], cum[:], big[:], ALU.add))
                dve.wait_ge(s_cols, 1)
                for d in range(2):
                    nc.vector.tensor_copy(u_cols[:, :, d, :], cols[:, d])

            @block.scalar
            def _(act):
                for d in range(2):
                    act.wait_ge(s_step, 4 + 3 * d)
                    nc.scalar.activation(tmp[d][1][:], tmp[d][0][:], ACT.Exp).then_inc(s_act, 1)
                    act.wait_ge(s_act, 2 * d + 1)
                    nc.scalar.activation(tmp[d][1][:], tmp[d][1][:], ACT.Ln, bias=1.0).then_inc(s_act, 1)


def mlstm(nc, name, q, k, v, rows, u_cols, masks, select, ones, out):
    with Stage(nc, name) as st:
        qk = st.ps("qk", [P, 3, 512])
        row = st.ps("row", [P, 2, 512])
        num, den = st.ps("num", [P, 512]), st.ps("den", [P, 512])
        qk_sb = st.sb("qk_sb", [P, 3, 512])
        w_all, w_lat = st.sb("w_all", [P, 2, 2, 2 * T]), st.sb("w_lat", [P, 2, 2, T])
        big = st.sb("big", [P, 2, 2 * T])
        floor, part = st.sb("floor", [P, 2, 2 * T]), st.sb("part", [P, 2 * T])
        s_qk, s_qk_out, s_row, s_big, s_arg, s_exp, s_floor, s_w, s_num, s_den, s_div, s_out = (
            st.sem(n) for n in ("qk", "qk_out", "row", "big", "arg", "exp", "floor", "w", "num", "den", "div", "out"))
        items = [(h, d) for h in range(H) for d in range(2)]
        EXPS = 6
        live = lambda n: 0 <= n < len(items)
        steps = range(-1, len(items) + 1)
        with nc.Block() as block:
            @block.tensor
            def _(pe):
                def prepare(n):
                    h, d = items[n]
                    if n >= 1:
                        pe.wait_ge(s_big, n)
                        pe.wait_ge(s_floor, n)
                    for i in range(2):
                        ins = nc.tensor.matmul(row[:, i, :], select[:, h, :], rows[d][i][:], start=True, stop=True)
                    ins.then_inc(s_row, 1)
                    if d == 0:
                        if h:
                            pe.wait_ge(s_qk_out, h)
                        for s in range(2):
                            nc.tensor.matmul(qk[:, s, :], k[:, h, s * P:(s + 1) * P], q[:, h, :], start=True, stop=True)
                        for s in range(2):
                            ins = nc.tensor.matmul(qk[:, 2, s * T:(s + 1) * T], k[:, h, (s + 2) * P:(s + 3) * P],
                                                   q[:, h, T:], start=True, stop=True)
                        ins.then_inc(s_qk, 1)

                def weigh(n):
                    h, b = items[n][0], n % 2
                    pe.wait_ge(s_w, 2 * n + 2)
                    for acc, value, taken in ((den, ones, s_den), (num, None, s_out)):
                        if n >= 1:
                            pe.wait_ge(taken, n)
                        for s in range(2):
                            lhs = v[:, s, h * P:(h + 1) * P] if value is None else value
                            nc.tensor.matmul(acc[:], lhs, w_all[:, b, s, :], start=(s == 0), stop=False, skip_group_check=True)
                        for s in range(2):
                            lhs = v[:, s + 2, h * P:(h + 1) * P] if value is None else value
                            ins = nc.tensor.matmul(acc[:, T:], lhs, w_lat[:, b, s, :], start=False, stop=(s == 1),
                                                   skip_group_check=True)
                        ins.then_inc(s_num, 1)

                for n in steps:
                    for work, item in ((prepare, n + 1), (weigh, n)):
                        if live(item):
                            work(item)

            @block.vector
            def _(dve):
                def arguments(n):
                    d, b = items[n][1], n % 2
                    dve.wait_ge(s_big, n + 1)
                    if n >= 2:
                        dve.wait_ge(s_num, 2 * n - 2)
                    nc.vector.tensor_tensor(w_all[:, b, :, 0:T], masks[:, d], over(big[:, b, 0:T], 2), ALU.subtract).then_inc(s_arg, 1)
                    nc.vector.tensor_tensor(w_lat[:, b], masks[:, d], over(big[:, b, T:], 2), ALU.subtract).then_inc(s_arg, 1)

                def weights(n):
                    h, b = items[n][0], n % 2
                    dve.wait_ge(s_exp, EXPS * (n + 1))
                    dve.wait_ge(s_qk_out, h + 1)
                    nc.vector.tensor_tensor(w_all[:, b], qk_sb[:, 0:2, :], w_all[:, b], ALU.mult).then_inc(s_w, 1)
                    nc.vector.tensor_tensor(w_lat[:, b], qk_sb[:, 2, :].rearrange("p (s t) -> p s t", s=2),
                                            w_lat[:, b], ALU.mult).then_inc(s_w, 1)

                def divide(n):
                    (h, d), b = items[n], n % 2
                    dve.wait_ge(s_num, 2 * n + 1)
                    dve.wait_ge(s_floor, n + 1)
                    nc.vector.tensor_tensor(floor[:, b], den[:], floor[:, b], ALU.max).then_inc(s_div, 1)
                    dve.wait_ge(s_div, 3 * n + 1)
                    nc.vector.scalar_tensor_tensor(floor[:, b], den[:], -1.0, floor[:, b], ALU.mult, ALU.max).then_inc(s_div, 1)
                    dve.wait_ge(s_div, 3 * n + 2)
                    dve.sem_inc(s_den, 1)
                    nc.vector.reciprocal(floor[:, b], floor[:, b]).then_inc(s_div, 1)
                    dve.wait_ge(s_div, 3 * n + 3)
                    dve.wait_ge(s_num, 2 * n + 2)
                    if d == 0:
                        nc.vector.tensor_tensor(out[:, h, :], num[:], floor[:, b], ALU.mult).then_inc(s_out, 1)
                    else:
                        nc.vector.tensor_tensor(part[:], num[:], floor[:, b], ALU.mult).then_inc(s_out, 1)
                        dve.wait_ge(s_out, n + 1)
                        nc.vector.tensor_tensor(out[:, h, :], out[:, h, :], part[:], ALU.add)

                for n in steps:
                    for work, item in ((weights, n), (divide, n - 1), (arguments, n + 1)):
                        if live(item):
                            work(item)

            @block.scalar
            def _(act):
                def copies(n):
                    (h, d), b = items[n], n % 2
                    act.wait_ge(s_row, n + 1)
                    if n >= 2:
                        act.wait_ge(s_arg, 2 * n - 2)
                        act.wait_ge(s_exp, EXPS * (n - 1))
                        act.wait_ge(s_out, n - 1)
                    nc.scalar.activation(big[:, b], row[:, 0, :], ACT.Copy).then_inc(s_big, 1)
                    nc.scalar.activation(floor[:, b], row[:, 1, :], ACT.Exp, scale=-1.0).then_inc(s_floor, 1)
                    if d == 0:
                        act.wait_ge(s_qk, h + 1)
                        if h:
                            act.wait_ge(s_w, 2 * n)
                        nc.scalar.activation(qk_sb[:], qk[:], ACT.Copy, scale=P ** -0.5).then_inc(s_qk_out, 1)

                def exponentials(n):
                    d, b = items[n][1], n % 2
                    h = items[n][0]
                    u = lambda s: u_cols[:, s, d, h:h + 1]
                    act.wait_ge(s_big, n + 1)
                    if n >= 2:
                        act.wait_ge(s_num, 2 * n - 2)
                    for s in range(2):
                        nc.scalar.activation(w_all[:, b, s, T:], big[:, b, T:], ACT.Exp, bias=u(s), scale=-1.0).then_inc(s_exp, 1)
                    act.wait_ge(s_arg, 2 * n + 2)
                    for s in range(2):
                        nc.scalar.activation(w_all[:, b, s, 0:T], w_all[:, b, s, 0:T], ACT.Exp, bias=u(s)).then_inc(s_exp, 1)
                        nc.scalar.activation(w_lat[:, b, s, :], w_lat[:, b, s, :], ACT.Exp, bias=u(s + 2)).then_inc(s_exp, 1)

                for n in steps:
                    for work, item in ((copies, n + 1), (exponentials, n + 1)):
                        if live(item):
                            work(item)


def gla_decays(nc, name, low, gate_up, gate_b, la):
    with Stage(nc, name) as st:
        acc = st.ps("acc", [P, H, 2 * T])
        z, e = st.sb("z", [P, H, 2 * T]), st.sb("e", [P, H, 2 * T])
        s_summed, s_z, s_abs, s_log, s_la = (st.sem(n) for n in ("summed", "z", "abs", "log", "la"))
        with nc.Block() as block:
            @block.tensor
            def _(pe):
                for d in range(2):
                    if d:
                        pe.wait_ge(s_z, d * H)
                    for h in range(H):
                        nc.tensor.matmul(acc[:, h, :], gate_up[:, d, h * P:(h + 1) * P], low[:, d, :],
                                         start=True, stop=True).then_inc(s_summed, 1)

            @block.vector
            def _(dve):
                for d in range(2):
                    if d:
                        dve.wait_ge(s_la, 2)
                    for h in range(H):
                        dve.wait_ge(s_summed, d * H + h + 1)
                        nc.vector.tensor_scalar(z[:, h, :], acc[:, h, :], gate_b[:, d, h:h + 1], None, ALU.add).then_inc(s_z, 1)
                    dve.wait_ge(s_z, (d + 1) * H)
                    nc.vector.scalar_tensor_tensor(e[:], z[:], -1.0, z[:], ALU.mult, ALU.min).then_inc(s_abs, 1)
                    dve.wait_ge(s_log, 2 * d + 2)
                    nc.vector.scalar_tensor_tensor(z[:], z[:], 0.0, e[:], ALU.min, ALU.subtract).then_inc(s_abs, 1)
                    dve.wait_ge(s_abs, 2 * d + 2)
                    for segment in range(2):
                        nc.vector.tensor_scalar(la[d][segment], z[:, :, segment * T:(segment + 1) * T], 1.0 / 16, None,
                                                ALU.mult).then_inc(s_la, 1)

            @block.scalar
            def _(act):
                for d in range(2):
                    act.wait_ge(s_abs, 2 * d + 1)
                    nc.scalar.activation(e[:], e[:], ACT.Exp).then_inc(s_log, 1)
                    act.wait_ge(s_log, 2 * d + 1)
                    nc.scalar.activation(e[:], e[:], ACT.Ln, bias=1.0).then_inc(s_log, 1)


def best16(nc, step, groups):
    for values, rest, out, where in groups:
        step.done(nc.vector.max(out[:, 0:8], values))
    step.wait()
    for values, rest, out, where in groups:
        step.done(nc.vector.max_index(where[:, 0:8], out[:, 0:8], values))
        step.done(nc.vector.match_replace(rest, out[:, 0:8], values, float(-3.4e38)))
    step.wait()
    for values, rest, out, where in groups:
        step.done(nc.vector.max(out[:, 8:16], rest))
    step.wait()
    for values, rest, out, where in groups:
        step.done(nc.vector.max_index(where[:, 8:16], out[:, 8:16], rest))
    step.wait()


def best_keys(nc, name, ahead, pair, keys_dram, top, index):
    with Stage(nc, name) as st:
        total = 2 * PEER_H
        keys = st.sb("keys", [P, total, N_KEYS])
        raw, s_loaded = ahead.raw, ahead.s_loaded
        w = st.sb("hi", [P, 4, KD * P], F32R), st.sb("lo", [P, 4, KD * P], F32R)
        q = st.sb("q", [P, 4, T])
        s, rest = st.sb("s", [P, 4, NT, N_KEYS]), st.sb("rest", [P, 2, NT, N_KEYS])
        acc, scores = st.ps("acc", [P, 4, 512]), st.ps("scores", [P, 2, 512])
        s_keys, s_hi, s_lo, s_used, s_taken, s_scores, s_copied, s_step, s_best = (
            st.sem(n) for n in ("keys", "hi", "lo", "used", "taken", "scores", "copied", "step", "best"))
        SLOTS, BANKS = 4, 2

        with nc.Block() as block:
            @block.sync
            def _(sp):
                sp.dma_start(keys[:], keys_dram).then_inc(s_keys, 16)
                each_chunk(sp, 4, total - 4, 4, lambda m, slot, turn: ahead.fetch(sp, m, slot, s_lo))

            @block.tensor
            def _(pe):
                pe.sem_inc(s_used, SLOTS)

                def query(m, slot):
                    pe.wait_ge(s_lo, m + 1)
                    pe.wait_ge(s_taken, m + 1)
                    for k in range(KD):
                        ins = products(nc, acc[:, slot, 0:T], part(w, slice(None), slot, slice(k * P, (k + 1) * P)),
                                       part(pair, slice(None), k), start=(k == 0), stop=(k == KD - 1))
                    ins.then_inc(s_used, 1)

                def score(m, slot):
                    pe.wait_ge(s_taken, m + 1 + SLOTS)
                    pe.wait_ge(s_copied, m + 1)
                    for tile in range(NT):
                        ins = nc.tensor.matmul(scores[:, slot % 2, tile * N_KEYS:(tile + 1) * N_KEYS], q[:, slot, tile * P:(tile + 1) * P],
                                               keys[:, bass.ds(m, 1), :].rearrange("p a c -> p (a c)"), start=True, stop=True)
                    ins.then_inc(s_scores, 1)

                def body(m, slot, turn):
                    query(m, slot)
                    score(m - 1, (slot - 1) % 4)
                query(0, 0)
                pe.wait_ge(s_keys, 16)
                each_chunk(pe, 1, total - 1, 4, body)
                score(total - 1, (total - 1) % 4)

            @block.scalar
            def _(act):
                act.sem_inc(s_taken, SLOTS)
                act.sem_inc(s_copied, BANKS)

                def hi(m, slot, turn):
                    act.wait_ge(s_loaded[slot], turn * 16 + 16)
                    act.wait_ge(s_used, m + 1)
                    nc.scalar.activation(w[0][:, slot, :], raw[:, slot, :], ACT.Copy).then_inc(s_hi, 1)

                def take(m, slot):
                    act.wait_ge(s_used, m + 1 + SLOTS)
                    act.wait_ge(s_scores, m + 1)
                    nc.scalar.activation(q[:, slot, :], acc[:, slot, 0:T], ACT.Copy).then_inc(s_taken, 1)

                def copy(m, slot):
                    act.wait_ge(s_scores, m + 1 + SLOTS)
                    act.wait_ge(s_best, m + 1)
                    nc.scalar.activation(s[:, slot].rearrange("p i k -> p (i k)"), scores[:, slot % 2, 0:NT * N_KEYS],
                                         ACT.Copy).then_inc(s_copied, 1)

                def body(m, slot, turn):
                    hi(m + 2, (slot + 2) % 4, turn + (slot + 2) // 4)
                    take(m, slot)
                    copy(m - 1, (slot - 1) % 4)
                for m in range(3):
                    hi(m, m, 0)
                take(0, 0)
                each_chunk(act, 1, total - 3, 4, body)
                for m in (total - 2, total - 1):
                    take(m, m % 4)
                    copy(m - 1, (m - 1) % 4)
                copy(total - 1, (total - 1) % 4)

            @block.vector
            def _(dve):
                step = Steps(dve, s_step)
                dve.sem_inc(s_scores, SLOTS)
                dve.sem_inc(s_best, SLOTS)
                for m in range(total):
                    dve.wait_ge(s_copied, m + 1 + BANKS)
                    best16(nc, step, [(s[:, m % 4, tile, :], rest[:, m % 2, tile, :], top[:, tile, m, :], index[:, tile, m, :])
                                      for tile in range(NT)])
                    dve.sem_inc(s_best, 1)

            @block.gpsimd
            def _(pool):
                for m in range(total):
                    pool.wait_ge(s_hi, m + 1)
                    nc.gpsimd.tensor_tensor(w[1][:, m % 4, :], raw[:, m % 4, :], w[0][:, m % 4, :].bitcast(F32),
                                            ALU.subtract).then_inc(s_lo, 1)


def select_experts(nc, name, top, index, tile, chosen, iota, ident, upcoming=None):
    with Stage(nc, name) as st:
        n_half = 2 * PEER_H
        turned = st.ps("turned", [P, 3, P])
        key_no, ranks = st.sb("key_no", [P, n_half, TOPK], BF16), st.sb("ranks", [P, TOPK], BF16)
        cand, cand2 = (st.sb(n, [P, PEER_H, TOPK * TOPK]) for n in ("cand", "cand2"))
        best, pos = st.sb("best", [P, PEER_H, TOPK]), st.sb("pos", [P, PEER_H, TOPK], U32)
        part, part_f = st.sb("part", [P, 2, P], U32), st.sb("part_f", [P, 2, P], BF16)
        hit = st.sb("hit", [P, P, TOPK], BF16)
        pick = st.sb("pick", [P, 3, P])
        total = st.sb("total", [P, PEER_H])
        s_step, s_cmp, s_exp, s_turned = (st.sem(n) for n in ("step", "cmp", "exp", "turned"))
        cols = slice(tile * P, (tile + 1) * P)
        beside = None
        if upcoming:
            beside, start = Conditioning(nc, st, "next", *upcoming[:4], ident), upcoming[4]

        with nc.Block() as block:
            if beside:
                @block.sync
                def _(sp):
                    beside.sync(sp, start)

            @block.tensor
            def _(pe):
                if beside:
                    beside.tensor(pe)
                pe.wait_ge(s_cmp, 1)
                for i in range(3):
                    ins = nc.tensor.transpose(turned[:, i, :], pick[:, i, :], ident)
                ins.then_inc(s_turned, 1)

            @block.scalar
            def _(act):
                if beside:
                    beside.scalar(act)
                act.wait_ge(s_exp, 1)
                nc.scalar.activation(best[:], best[:], ACT.Exp).then_inc(s_exp, 1)
                act.wait_ge(s_turned, 1)
                for i in range(3):
                    nc.scalar.activation(chosen[i][:, cols], turned[:, i, :], ACT.Copy)

            @block.vector
            def _(dve):
                step = Steps(dve, s_step)

                step.done(nc.vector.tensor_copy(key_no[:], index))
                step.done(nc.vector.tensor_copy(ranks[:], iota[:, 0:TOPK]))
                pair = top.rearrange("p (h c) r -> p h c r", c=2)
                first = pair[:, :, 0, :].unsqueeze(3).broadcast_to([P, PEER_H, TOPK, TOPK])
                second = pair[:, :, 1, :].unsqueeze(2).broadcast_to([P, PEER_H, TOPK, TOPK])
                step.link(nc.vector.tensor_tensor(cand[:].rearrange("p h (a b) -> p h a b", a=TOPK), first, second, ALU.add))
                best16(nc, step, [(cand[:, h, :], cand2[:, h, :], best[:, h, :], pos[:, h, :]) for h in range(PEER_H)])
                flat = pos[:].rearrange("p h r -> p (h r)")
                step.done(nc.vector.tensor_scalar(part[:, 0, :], flat, 4, None, ALU.logical_shift_right))
                step.link(nc.vector.tensor_scalar(part[:, 1, :], flat, TOPK - 1, None, ALU.bitwise_and))
                step.link(nc.vector.tensor_copy(part_f[:], part[:]))
                step.link(nc.vector.tensor_copy(total[:], best[:, :, 0]))
                nc.vector.tensor_tensor(best[:], best[:], bcast(total[:], TOPK), ALU.subtract).then_inc(s_exp, 1)
                numbers = key_no[:].rearrange("p (h c) r -> p h c r", c=2)
                for c in range(2):
                    step.link(nc.vector.tensor_tensor(hit[:], bcast(part_f[:, c, :], TOPK), over(ranks[:], P), ALU.is_equal))
                    hit4 = hit[:].rearrange("p (h r) a -> p h r a", h=PEER_H)
                    step.link(nc.vector.tensor_tensor(hit4, hit4, numbers[:, :, c, :].unsqueeze(2).broadcast_to(
                        [P, PEER_H, TOPK, TOPK]), ALU.mult))
                    step.link(nc.vector.tensor_reduce(pick[:, c, :], hit[:], AX.X, ALU.add))
                dve.wait_ge(s_exp, 2)
                step.link(nc.vector.tensor_reduce(total[:], best[:], AX.X, ALU.add))
                step.link(nc.vector.reciprocal(total[:], total[:]))
                nc.vector.tensor_tensor(pick[:, 2, :].rearrange("p (h r) -> p h r", h=PEER_H), best[:],
                                        bcast(total[:], TOPK), ALU.mult).then_inc(s_cmp, 1)
                if beside:
                    beside.vector(dve, start)


def spread_weights(nc, name, chosen, iota, gmat):
    with Stage(nc, name) as st:
        n_tok = 8
        ring = 4
        rows = st.sb("rows", [P, ring, n_tok, N_KEYS])
        cols = st.sb("cols", [P, ring, n_tok, N_KEYS])
        acc = st.ps("acc", [P, ring, n_tok, N_KEYS])
        s_hit, s_rows, s_cols, s_summed, s_taken = (st.sem(n) for n in ("hit", "rows", "cols", "summed", "taken"))
        steps = T // n_tok
        which = lambda i, t: chosen[i][:, bass.ds(t, n_tok)].unsqueeze(2).broadcast_to([P, n_tok, N_KEYS])
        with nc.Block() as block:
            @block.vector
            def _(dve):
                dve.sem_inc(s_summed, ring)
                with dve.Fori(0, steps // ring) as i:
                    for b in range(ring):
                        n = i * ring + b
                        dve.wait_ge(s_summed, n + 1)
                        nc.vector.tensor_tensor(rows[:, b], over(iota, n_tok), which(0, n * n_tok), ALU.is_equal).then_inc(s_hit, 1)
                        nc.vector.tensor_tensor(cols[:, b], over(iota, n_tok), which(1, n * n_tok), ALU.is_equal).then_inc(s_cols, 1)

            @block.gpsimd
            def _(pool):
                with pool.Fori(0, steps // ring) as i:
                    for b in range(ring):
                        n = i * ring + b
                        pool.wait_ge(s_hit, n + 1)
                        nc.gpsimd.tensor_tensor(rows[:, b], rows[:, b], which(2, n * n_tok), ALU.mult).then_inc(s_rows, 1)

            @block.tensor
            def _(pe):
                with pe.Fori(0, steps // ring) as i:
                    for b in range(ring):
                        n = i * ring + b
                        pe.wait_ge(s_rows, n + 1)
                        pe.wait_ge(s_cols, n + 1)
                        pe.wait_ge(s_taken, n + 1)
                        for t in range(n_tok):
                            ins = nc.tensor.matmul(acc[:, b, t, :], rows[:, b, t, :], cols[:, b, t, :], start=True, stop=True)
                        ins.then_inc(s_summed, 1)

            @block.scalar
            def _(act):
                act.sem_inc(s_taken, ring)
                with act.Fori(0, steps // ring) as i:
                    for b in range(ring):
                        n = i * ring + b
                        act.wait_ge(s_summed, n + 1 + ring)
                        nc.scalar.activation(gmat[:, bass.ds(n * n_tok, n_tok), :], acc[:, b], ACT.Copy).then_inc(s_taken, 1)


def dense_experts(nc, name, pair, w_u, w_v, gmat, x, gate):
    with Stage(nc, name) as st:
        half = KD // 2
        cols = half * P
        raw_u, raw_v = st.sb("raw_u", [P, 4, cols]), st.sb("raw_v", [P, 4, cols])
        u = st.sb("u_hi", [P, 2, cols], F32R), st.sb("u_lo", [P, 2, cols], F32R)
        v = st.sb("v_hi", [P, 2, cols], F32R), st.sb("v_lo", [P, 2, cols], F32R)
        e = st.sb("e", [P, T])
        ew = st.sb("e_hi", [P, 2, T], F32R), st.sb("e_lo", [P, 2, T], F32R)
        score = st.ps("score", [P, 2, 512])
        acc = st.ps("acc", [P, KD, T])
        s_u, s_v = [st.sem(f"u{r}") for r in range(4)], [st.sem(f"v{r}") for r in range(4)]
        (s_u_hi, s_u_lo, s_u_used, s_v_hi, s_v_lo, s_v_used, s_gelu, s_e, s_e_hi, s_e_lo) = (
            st.sem(n) for n in ("u_hi", "u_lo", "u_used", "v_hi", "v_lo", "v_used", "gelu", "e", "e_hi", "e_lo"))
        RAW, HALF, OUT, BANK, BUF = 4, 2, 4, 2, 1

        with nc.Block() as block:
            @block.sync
            def _(sp):
                def fetch_u(j, slot):
                    for i in range(2):
                        sp.wait_ge(s_u_lo, j * 2 + i + 1)
                        sp.dma_start(raw_u[:, slot * 2 + i, :], w_u[bass.ds(j, 1), :, i * cols:(i + 1) * cols].rearrange(
                            "a p c -> p (a c)")).then_inc(s_u[slot * 2 + i], 16)

                def fetch_v(j, slot):
                    for i in range(2):
                        sp.wait_ge(s_v_lo, j * 2 + i + 1)
                        sp.dma_start(raw_v[:, slot * 2 + i, :], w_v[:, bass.ds(j, 1), i * cols:(i + 1) * cols].rearrange(
                            "p a c -> p (a c)")).then_inc(s_v[slot * 2 + i], 16)

                def body(j, slot, turn):
                    fetch_u(j + 1, 1 - slot)
                    fetch_v(j, slot)
                fetch_u(0, 0)
                each_chunk(sp, 0, N_KEYS - 1, 2, body)
                fetch_v(N_KEYS - 1, 1)

            @block.tensor
            def _(pe):
                pe.sem_inc(s_u_used, HALF)
                pe.sem_inc(s_v_used, OUT)

                def scores(j, slot):
                    pe.wait_ge(s_gelu, j + 1)
                    for i in range(2):
                        pe.wait_ge(s_u_lo, j * 2 + i + 1 + RAW)
                        for k in range(half):
                            ins = products(nc, score[:, slot, 0:T], part(u, slice(None), i, slice(k * P, (k + 1) * P)),
                                           part(pair, slice(None), i * half + k), start=(i == 0 and k == 0),
                                           stop=(i == 1 and k == half - 1))
                        ins.then_inc(s_u_used, 1)

                def outputs(j, slot, start=False, stop=False):
                    pe.wait_ge(s_e_lo, j + 1 + BUF)
                    for i in range(2):
                        pe.wait_ge(s_v_lo, j * 2 + i + 1 + RAW)
                        for k in range(half):
                            m = i * half + k
                            ins = products(nc, acc[:, m, :], part(v, slice(None), i, slice(k * P, (k + 1) * P)),
                                           part(ew, slice(None), slot), start=start and m % 2 == 0, stop=stop)
                        ins.then_inc(s_v_used, 1)

                scores(0, 0)
                scores(1, 1)
                outputs(0, 0, start=True)
                with pe.Fori(1, N_KEYS // 2) as i:
                    scores(i * 2, 0)
                    outputs(i * 2 - 1, 1)
                    scores(i * 2 + 1, 1)
                    outputs(i * 2, 0)
                outputs(N_KEYS - 1, 1, stop=True)

            @block.scalar
            def _(act):
                act.sem_inc(s_gelu, BANK)

                def hi(s_loaded, s_used, ahead, s_done, dst, raw, j, slot, turn):
                    for i in range(2):
                        act.wait_ge(s_loaded[slot * 2 + i], turn * 16 + 16)
                        act.wait_ge(s_used, j * 2 + i - 1 + ahead)
                        nc.scalar.activation(dst[0][:, i, :], raw[:, slot * 2 + i, :], ACT.Copy).then_inc(s_done, 1)

                def hi_u(j, slot, turn):
                    hi(s_u, s_u_used, HALF, s_u_hi, u, raw_u, j, slot, turn)

                def gelu_and_v(j, slot, turn):
                    act.wait_ge(s_u_used, j * 2 + 2 + HALF)
                    act.wait_ge(s_e_lo, j + BUF)
                    nc.scalar.activation(e[:], score[:, slot, 0:T], ACT.Gelu).then_inc(s_gelu, 1)
                    hi(s_v, s_v_used, OUT, s_v_hi, v, raw_v, j, slot, turn)

                def body(j, slot, turn):
                    gelu_and_v(j, slot % 2, turn * 2 + slot // 2)
                    hi_u(j + 2, slot % 2, turn * 2 + slot // 2 + 1)
                hi_u(0, 0, 0)
                hi_u(1, 1, 0)
                each_chunk(act, 0, N_KEYS - 2, 4, body)
                for j in range(N_KEYS - 2, N_KEYS):
                    gelu_and_v(j, j % 2, j // 2)

            @block.vector
            def _(dve):
                dve.sem_inc(s_u_lo, RAW)
                dve.sem_inc(s_v_lo, RAW)
                dve.sem_inc(s_e_lo, BUF)

                def lo(s_hi, s_done, dst, raw, j, slot):
                    for i in range(2):
                        dve.wait_ge(s_hi, j * 2 + i + 1)
                        nc.vector.tensor_tensor(dst[1][:, i, :], raw[:, slot * 2 + i, :],
                                                dst[0][:, i, :].bitcast(F32), ALU.subtract).then_inc(s_done, 1)

                def body(j, slot, turn):
                    if not isinstance(j, int) or j < N_KEYS - 1:
                        lo(s_u_hi, s_u_lo, u, raw_u, j + 1, 1 - slot)
                    dve.wait_ge(s_gelu, j + 1 + BANK)
                    nc.vector.tensor_tensor(e[:].unsqueeze(2), e[:].unsqueeze(2), gmat[:, :, bass.ds(j, 1)],
                                            ALU.mult).then_inc(s_e, 1)
                    dve.wait_ge(s_e, j + 1)
                    dve.wait_ge(s_v_used, j * 2 - 2 + OUT)
                    nc.vector.tensor_copy(ew[0][:, slot, :], e[:]).then_inc(s_e_hi, 1)
                    dve.wait_ge(s_e_hi, j + 1)
                    nc.vector.tensor_tensor(ew[1][:, slot, :], e[:], ew[0][:, slot, :].bitcast(F32), ALU.subtract).then_inc(s_e_lo, 1)
                    lo(s_v_hi, s_v_lo, v, raw_v, j, slot)
                lo(s_u_hi, s_u_lo, u, raw_u, 0, 0)
                each_chunk(dve, 0, N_KEYS - 1, 2, body)
                body(N_KEYS - 1, 1, None)
                dve.wait_ge(s_v_used, 2 * N_KEYS + OUT)
                for m in range(KD):
                    nc.vector.scalar_tensor_tensor(x[:, m, :], acc[:, m, :], gate[:, m, :], x[:, m, :], ALU.mult, ALU.add)


def peer(nc, name, x, mods, col, w_q, keys_dram, w_u, w_v, iota, ident, upcoming=None):
    with Stage(nc, name) as st:
        pair = st.sb("hi", [P, KD, T], F32R), st.sb("lo", [P, KD, T], F32R)
        chosen = [st.sb(f"chosen{i}", [P, T]) for i in range(3)]
        with Stage(nc, name + "_pick") as sel:
            ahead = Ahead(nc, sel, "wq", w_q)
            with Stage(nc, name + "_in") as tmp:
                modulate(nc, name + "_h", tmp.sb("h", [P, KD, T]), pair, x, mods, 3 * KD, (col,), ahead)
            top, index = sel.sb("top", [P, NT, 2 * PEER_H, TOPK]), sel.sb("index", [P, NT, 2 * PEER_H, TOPK], U32)
            best_keys(nc, name + "_keys", ahead, pair, keys_dram, top, index)
            for tile in range(NT):
                select_experts(nc, f"{name}_select{tile}", top[:, tile], index[:, tile], tile, chosen, iota, ident,
                               upcoming and (*upcoming[:4], upcoming[4] + tile * Conditioning.GROUPS))
        gmat = st.sb("gmat", [P, T, N_KEYS])
        spread_weights(nc, name + "_spread", chosen, iota, gmat)
        dense_experts(nc, name + "_dense", pair, w_u, w_v, gmat, x, mods[:, 5 * KD:, col:col + 1])


VECTORS = [("c", KD), ("ada_b", 2 * 6 * KD), ("ln_g", 4 * KD), ("ln_b", 4 * KD), ("lb_raw", H), ("norm_g", 1),
           ("pool_scale", KD), ("conv", 2 * KF * 4), ("sinks", A_HEADS), ("c_2", KD * 2), ("b_mod_2", 2 * 6 * KD),
           ("ln_w_2", 4 * KD), ("ln_b_2", 4 * KD), ("ab_norm_w_2", H), ("sinks_2", A_HEADS), ("gla_gate_b_2", 2 * H),
           ("gla_norm_w_2", KD)]
CONSTANTS = [("ones", P), ("mean_of_p", P), ("mean_of_d", P), ("ident", P), ("iota", P)]
Q_ORDER = [h for c in range(GQA) for h in (c, GQA + c)]


def offsets(fields):
    at, out = 0, {}
    for name, n in fields:
        out[name] = (at, at + n)
        at += n
    return out, at


def first_block(nc, d, x, vec, con):
    with Stage(nc, "first") as blk:
        mods = blk.sb("mods", [P, 6 * KD, 1])
        h, z = blk.sb("h", [P, KD, T]), blk.sb("z", [P, KD, T])
        pair = blk.sb("h_hi", [P, KD, T], F32R), blk.sb("h_lo", [P, KD, T], F32R)
        c = vec("c").unsqueeze(2)
        ln = lambda layer, i: (vec("ln_g")[:, (2 * layer + i) * KD:(2 * layer + i + 1) * KD],
                               vec("ln_b")[:, (2 * layer + i) * KD:(2 * layer + i + 1) * KD])
        conv = lambda layer: vec("conv").rearrange("p (l f j) -> p l f j", l=2, j=4)[:, layer]
        ada_b = lambda layer: vec("ada_b")[:, layer * 6 * KD:(layer + 1) * 6 * KD]

        modulation(nc, "mod0", c, d["ada_w"][0], ada_b(0), mods, con("ident"))
        with Stage(nc, "in00") as st:
            ahead = Ahead(nc, st, "in", d["ab_w_in"])
            modulate(nc, "h00", h, pair, x, mods, 0, (0,), ahead)
            even_mixer(nc, d, ahead, pair, z, mods, vec, con)
        layer_norm(nc, "ln00", x, z, h, T, *ln(0, 0), con("mean_of_d"))
        with Stage(nc, "in01") as st:
            ahead = Ahead(nc, st, "up", d["w_up"][0])
            modulate(nc, "h01", h, pair, x, mods, 3 * KD, (0,), ahead)
            conv_ffn(nc, "ffn0", pair, ahead, conv(0), d["w_down"][0], z, mods[:, 5 * KD:, :])
        layer_norm(nc, "ln01", x, z, h, T, *ln(0, 1), con("mean_of_d"))

        modulation(nc, "mod1", c, d["ada_w"][1], ada_b(1), mods, con("ident"))
        modulate(nc, "h10", h, pair, x, mods, 0, (0,))
        pool_mixer(nc, "pool", h, d["pool_w"], vec("pool_scale"), d["inv_count"], z, mods[:, 2 * KD:3 * KD, :], x)
        layer_norm(nc, "ln10", x, z, h, T, *ln(1, 0), con("mean_of_d"), residual=False)
        with Stage(nc, "in11") as st:
            ahead = Ahead(nc, st, "up", d["w_up"][1])
            modulate(nc, "h11", h, pair, x, mods, 3 * KD, (0,), ahead)
            conv_ffn(nc, "ffn1", pair, ahead, conv(1), d["w_down"][1], z, mods[:, 5 * KD:, :])
        layer_norm(nc, "ln11", x, z, h, T, *ln(1, 1), con("mean_of_d"))


def hgrn_gates(nc, name, f, k, g, lb_raw):
    with Stage(nc, name) as st:
        share, lb, rest = st.sb("share", [P, H]), st.sb("lb", [P, H]), st.sb("rest", [P, H])
        s_step, s_sig, s_exp, s_clamped = st.sem("step"), st.sem("sig"), st.sem("exp"), st.sem("clamped")
        with nc.Block() as block:
            @block.scalar
            def _(act):
                nc.scalar.activation(k, f, ACT.Sigmoid, scale=-1.0).then_inc(s_sig, 1)
                act.wait_ge(s_sig, 1)
                nc.scalar.activation(f, f, ACT.Sigmoid).then_inc(s_sig, 1)
                act.wait_ge(s_step, 1)
                nc.scalar.activation(share[:], share[:], ACT.Exp).then_inc(s_exp, 1)
                act.wait_ge(s_clamped, 1)
                nc.scalar.activation(g, f, ACT.Ln)

            @block.vector
            def _(dve):
                step = Steps(dve, s_step)
                step.done(nc.vector.tensor_tensor(share[:], lb_raw, lb_raw, ALU.subtract))
                dve.wait_ge(s_exp, 1)
                step.link(nc.vector.reciprocal(lb[:], share[:]))
                step.link(nc.vector.tensor_tensor(share[:], share[:], lb[:], ALU.mult))
                step.link(nc.vector.tensor_tensor(lb[:], share[:], share[:], ALU.subtract))
                step.link(nc.vector.tensor_scalar(rest[:], lb[:], -1.0, 1.0, ALU.mult, ALU.add))
                dve.wait_ge(s_sig, 2)
                for h in range(H):
                    step.done(nc.vector.tensor_scalar(k[:, h, :], k[:, h, :], rest[:, h:h + 1], None, ALU.mult))
                    step.done(nc.vector.tensor_scalar(f[:, h, :], f[:, h, :], rest[:, h:h + 1], lb[:, h:h + 1], ALU.mult, ALU.add))
                step.wait()
                nc.vector.tensor_scalar(f, f, LN_MIN, None, ALU.max).then_inc(s_clamped, 1)


def even_mixer(nc, d, ahead, h, z, mods, vec, con):
    with Stage(nc, "mixer") as mix:
        cat = mix.sb("cat", [P, KD, T])
        qk = mix.sb("qk", [P, GQA + 1, T])
        v = mix.sb("v", [P, NT, 2 * P + 3 * P])
        positions, perm = mix.sb("positions", [P, T], I32), mix.sb("perm", [P, P])
        inv_freq, mask = mix.sb("inv_freq", [P, 1]), mix.sb("mask", [P, 2 * P])
        with Stage(nc, "hgrn") as st:
            q, f, gate, k, g = (st.sb(n, [P, H, T]) for n in ("q", "f", "gate", "k", "g"))
            o = st.sb("o", [P, H, T])
            at, off = st.sb("at", [P, H * NT, P]), st.sb("off", [P, H, P])
            masks = st.sb("masks", [P, LEVELS + 1, P], I32)

            project(nc, "ab_in", ahead, KD, h, T, [(H, copy_to(nc, q)), (H, copy_to(nc, f)),
                                                          (H, copy_to(nc, gate, ACT.Silu)), (GQA + 1, copy_to(nc, qk))],
                    [(masks[:], d["levels"][0]), (positions[:], d["positions"]), (perm[:], d["perm"]),
                     (inv_freq[:], d["inv_freq"]), (mask[:], d["swa_mask"])])
            token_major(nc, "ab_v", d["ab_w_v"], 5 * P, h, T, v)
            hgrn_gates(nc, "gates", f[:], k[:], g[:], vec("lb_raw"))
            decayed_scores(nc, "hgrn_scores", q[:], k[:], [(g[:], False)], [masks], at[:], [off[:]])
            weighted_values(nc, "hgrn_values", [v[:, i, 0:4 * P] for i in range(NT)], P, at, [off], o)
            head_norm(nc, "hgrn_norm", o, cat[:, 0:H, :], gate, lambda c: vec("norm_g"), 1, T, RMS_EPS, con("mean_of_p"))
        with Stage(nc, "swa") as st:
            cos, sin = st.sb("cos", [P, T]), st.sb("sin", [P, T])
            rope_tables(nc, "tables", positions[:], inv_freq[:], cos[:], sin[:])
            rope(nc, "rope", qk[:], perm[:], cos[:], sin[:])
            values = [v[:, i, 4 * P:5 * P].rearrange("p (g e) -> p g e", g=2) for i in range(NT)]
            attention(nc, "swa_attention",
                      [(lambda c: qk[:, c, 0:P], [qk[:, GQA, 0:P]], values[0:1], mask[:, P:2 * P], slice(0, P)),
                       (lambda c: qk[:, c, P:2 * P], [qk[:, GQA, :]], values, mask[:], slice(P, 2 * P))],
                      vec("sinks"), cat[:, H:, :], con("ident"))
        cat_pair = mix.sb("cat_hi", [P, KD, T], F32R), mix.sb("cat_lo", [P, KD, T], F32R)
        ahead = Ahead(nc, mix, "out", d["ab_w_out"], raw=ahead.raw)
        split(nc, "cat_split", cat, cat_pair, ahead)
        project(nc, "ab_out", ahead, KD, cat_pair, T, [(KD, gate_to(nc, z, mods[:, 2 * KD:3 * KD, :]))])


def second_block(nc, d, x, out, vec, con):
    with Stage(nc, "second") as blk:
        mods = [blk.sb(f"mods2{layer}", [P, 6 * KD, 2]) for layer in range(2)]
        lat = slice(T, 2 * T)
        c = vec("c_2").rearrange("p (k n) -> p k n", n=2)
        ln = lambda layer, i: (vec("ln_w_2")[:, (2 * layer + i) * KD:(2 * layer + i + 1) * KD],
                               vec("ln_b_2")[:, (2 * layer + i) * KD:(2 * layer + i + 1) * KD])
        bias = lambda layer: vec("b_mod_2")[:, layer * 6 * KD:(layer + 1) * 6 * KD]
        streams = x[:, :, 0:T], x[:, :, lat]

        def peer_layer(layer, stream, upcoming=None):
            peer(nc, f"peer{layer}{stream}", streams[stream], mods[layer], stream, d["peer_wq"][layer], d["peer_keys"][layer],
                 d["peer_u"][layer], d["peer_v"][layer], con("iota"), con("ident"), upcoming)

        modulation(nc, "mod20", c, d["w_mod"][0], bias(0), mods[0], con("ident"))
        for layer, mixer in enumerate((mixer_ab, mixer_c)):
            with Stage(nc, f"mix{layer}") as st:
                h = st.sb("h", [P, KD, 2 * T])
                pair = st.sb("h_hi", [P, KD, 2 * T], F32R), st.sb("h_lo", [P, KD, 2 * T], F32R)
                ahead = Ahead(nc, st, "in", d[("ab_w_in_2", "gla_w_k_2")[layer]])
                modulate(nc, f"h2{layer}", h, pair, x, mods[layer], 0, (0, 1), ahead)
                mixer(nc, d, ahead, h, pair, mods[layer], vec, con)
                if layer == 0:
                    with Stage(nc, "norm20") as norm:
                        layer_norm(nc, "ln20", x, h, norm.sb("sq", [P, KD, 2 * T]), 2 * T, *ln(0, 0), con("mean_of_d"))
                else:
                    with Stage(nc, "norm30") as norm:
                        layer_norm(nc, "ln30", streams[1], h[:, :, lat], norm.sb("sq", [P, KD, T]), T, *ln(1, 0), con("mean_of_d"))
            if layer == 0:
                for stream in range(2):
                    peer_layer(0, stream, (c, d["w_mod"][1], bias(1), mods[1], stream * NT * Conditioning.GROUPS))
            else:
                peer_layer(1, 1)
            which = x if layer == 0 else streams[1]
            t = which.shape[2]
            with Stage(nc, f"norm{layer}1") as norm:
                layer_norm(nc, f"ln{layer + 2}1", which, which, norm.sb("sq", [P, KD, t]), t, *ln(layer, 1), con("mean_of_d"),
                           residual=False)
        store(nc, "store", out, streams[1])


def store(nc, name, out, src):
    with Stage(nc, name) as st:
        s_stored = st.sem("stored")
        with nc.Block() as block:
            @block.sync
            def _(sp):
                sp.dma_start(out, src).then_inc(s_stored, 16)
                sp.wait_ge(s_stored, 16)


def mixer_ab(nc, d, ahead, h, pair, mods, vec, con):
    lat = slice(T, 2 * T)
    with Stage(nc, "mixab") as mix:
        cat = mix.sb("cat", [P, KD, 2 * T])
        qk = mix.sb("qk", [P, GQA + 1, 2 * T])
        v = mix.sb("v", [P, 2 * NT, 5 * P])
        perm, tables, mask = mix.sb("perm", [P, P]), mix.sb("tables", [P, 2, T]), mix.sb("mask", [P, NT, 2 * T])
        with Stage(nc, "mlstm") as st:
            q, k, gate, o = (st.sb(n, [P, H, 2 * T]) for n in ("q", "k", "gate", "o"))
            rows = [[st.sb(f"row{a}{b}", [H, 2 * T]) for b in range(2)] for a in range(2)]
            u_cols = st.sb("u_cols", [P, 4, 2, H])
            w_gates, gate_b = st.sb("w_gates", [P, KD, 4 * H]), st.sb("gate_b", [H, 4])
            masks, select = st.sb("masks", [P, 2, NT, T]), st.sb("select", [H, H, P])

            project(nc, "ab2_in", ahead, KD, pair, 2 * T,
                    [(H, copy_to(nc, q)), (H, copy_to(nc, k)), (H, copy_to(nc, gate, ACT.Sigmoid)), (GQA + 1, copy_to(nc, qk))],
                    [(w_gates[:], d["ab_w_gates_2"]), (gate_b[:], d["ab_gate_b_2"]), (masks[:], d["causal"]),
                     (select[:], d["select"]), (perm[:], d["perm_2"]), (tables[:], d["axial"]), (mask[:], d["window"])])
            token_major(nc, "ab2_v", d["ab_w_v_2"], 5 * P, pair, 2 * T, v)
            log_sigmoid_rows(nc, "gate_rows", h, w_gates, gate_b, rows, u_cols, con("ident"))
            mlstm(nc, "mlstm_scan", q, k, v, rows, u_cols, masks, select, con("ones"), o)
            head_norm(nc, "mlstm_norm", o, cat[:, 0:H, :], gate, lambda c: vec("ab_norm_w_2")[:, c:c + 1], 1, 2 * T,
                      LN_EPS, con("mean_of_p"))
        with Stage(nc, "window") as st:
            rope(nc, "rope2", qk[:, :, lat], perm[:], tables[:, 0, :], tables[:, 1, :])
            values = [v[:, i, 4 * P:5 * P].rearrange("p (g e) -> p g e", g=2) for i in range(2 * NT)]
            tiles = [(lambda c, a=i * P: qk[:, c, a:a + P], [qk[:, GQA, 0:T]] + [qk[:, GQA, lat]] * (i >= NT),
                      values if i >= NT else values[0:NT], mask[:, i - NT, :] if i >= NT else None, slice(i * P, (i + 1) * P))
                     for i in range(2 * NT)]
            attention(nc, "window_attention", tiles, vec("sinks_2"), cat[:, H:, :], con("ident"))
        cat_pair = mix.sb("cat_hi", [P, KD, 2 * T], F32R), mix.sb("cat_lo", [P, KD, 2 * T], F32R)
        ahead = Ahead(nc, mix, "out", d["ab_w_out_2"], raw=ahead.raw)
        split(nc, "cat2_split", cat, cat_pair, ahead)
        project(nc, "ab2_out", ahead, KD, cat_pair, 2 * T, [(KD, gate_to(nc, h, mods[:, 2 * KD:3 * KD, :]))])


def mixer_c(nc, d, ahead, h, pair, mods, vec, con):
    lat = slice(T, 2 * T)
    with Stage(nc, "mixc") as mix:
        gate = mix.sb("gate", [P, KD, T])
        o = mix.sb("o", [P, KD, T])
        with Stage(nc, "gla") as st:
            q = st.sb("q", [P, H, T])
            k = [st.sb(f"k{i}", [P, H, T]) for i in range(2)]
            v = st.sb("v", [P, 2 * NT, KD * P])
            la = [[st.sb(f"la{a}{b}", [P, H, T]) for b in range(2)] for a in range(2)]

            def k_to(index, psum):
                nc.scalar.activation(k[0][:, bass.ds(index, 1), :], psum[:, 0:T].unsqueeze(1), ACT.Copy)
                return nc.scalar.activation(k[1][:, bass.ds(index, 1), :], psum[:, lat].unsqueeze(1), ACT.Copy)
            w_low, gate_up = st.sb("w_low", [P, KD, 32]), st.sb("gate_up", [16, 2, H * P])
            masks = [st.sb(f"masks{i}", [P, LEVELS + 1, P], I32) for i in range(2)]
            project(nc, "gla_k", ahead, KD, pair, 2 * T, [(H, k_to)],
                    [(w_low[:], d["gla_w_low_2"]), (gate_up[:], d["gla_gate_up_2"]), (masks[0][:], d["levels"][0]),
                     (masks[1][:], d["levels"][1])])
            project(nc, "gla_qg", d["gla_w_qg_2"], KD, part(pair, slice(None), slice(None), lat), T,
                    [(H, copy_to(nc, q, scale=P ** -0.5)), (KD, copy_to(nc, gate, ACT.Silu))])
            token_major(nc, "gla_v", d["gla_w_v_2"], KD * P, pair, 2 * T, v)
            with Stage(nc, "decays") as dec:
                low = dec.sb("low", [16, 2, 2 * T])
                acc = dec.ps("acc", [P, 2, 2 * T])
                s_low, s_copied = dec.sem("low"), dec.sem("copied")
                with nc.Block() as block:
                    @block.tensor
                    def _(pe):
                        for n in range(2):
                            for kc in range(KD):
                                ins = nc.tensor.matmul(acc[0:16, n, :], w_low[:, kc, n * 16:(n + 1) * 16], h[:, kc, :],
                                                       start=(kc == 0), stop=(kc == KD - 1))
                        ins.then_inc(s_low, 1)

                    @block.scalar
                    def _(act):
                        act.wait_ge(s_low, 1)
                        nc.scalar.activation(low[:], acc[0:16], ACT.Copy).then_inc(s_copied, 1)
                gla_decays(nc, "gla_decays", low, gate_up, vec("gla_gate_b_2").rearrange("p (d h) -> p d h", d=2),
                           [[a[:] for a in row] for row in la])
            with Stage(nc, "scores") as sc:
                at, offs = sc.sb("at", [P, H * NT, P]), [sc.sb(f"off{i}", [P, H, P]) for i in range(2)]
                ctx_at = sc.sb("ctx_at", [P, 2, H, T])
                decayed_scores(nc, "gla_scores", q[:], k[1][:], [(la[0][1][:], False), (la[1][1][:], True)], masks, at[:],
                               [a[:] for a in offs], (k[0][:], [la[0][0], la[1][0]], ctx_at))
                weighted_values(nc, "gla_values", [v[:, NT + i, :] for i in range(NT)], 2 * P, at, offs, o,
                                ([v[:, i, :] for i in range(NT)], ctx_at))
        y = mix.sb("y", [P, KD, T])
        head_norm(nc, "gla_norm", o, y, gate, lambda c: vec("gla_norm_w_2")[:, c:c + 1], 2, T, LN_EPS, con("mean_of_p"))
        y_pair = mix.sb("y_hi", [P, KD, T], F32R), mix.sb("y_lo", [P, KD, T], F32R)
        ahead = Ahead(nc, mix, "out", d["gla_w_out_2"], raw=ahead.raw)
        split(nc, "y_split", y, y_pair, ahead)
        project(nc, "gla_out", ahead, KD, y_pair, T, [(KD, gate_to(nc, h[:, :, lat], mods[:, 2 * KD:3 * KD, 1:2]))])


def program(nc, d, out):
    vec_at, n_vec = offsets(VECTORS)
    con_at, n_con = offsets(CONSTANTS)
    with Stage(nc, "all") as st:
        vectors, constants = st.sb("vectors", [P, n_vec]), st.sb("constants", [P, n_con])
        x = st.sb("x", [P, KD, 2 * T])
        vec = lambda name: vectors[:, vec_at[name][0]:vec_at[name][1]]
        con = lambda name: constants[:, con_at[name][0]:con_at[name][1]]
        load(nc, "load_all", [(vectors[:], d["vectors"]), (constants[:], d["constants"]), (x[:, :, 0:T], d["ctx"]), (x[:, :, T:], d["x"])])
        first_block(nc, d, x[:, :, T:], vec, con)
        second_block(nc, d, x, out, vec, con)


def columns(v):
    return np.ascontiguousarray(np.reshape(v, (-1, P)).T)


def chunked(w):
    kc, mo = w.shape[0] // P, w.shape[1] // P
    return np.ascontiguousarray(w.reshape(kc, P, mo, P).transpose(2, 1, 0, 3).reshape(mo, P, kc * P))


def streamed(w):
    half = w.shape[0] // P // 2
    return w.reshape(2, half, P, -1, 512).transpose(3, 0, 2, 1, 4).reshape(-1, P, half, 512)


def feature_major(x):
    return np.ascontiguousarray(x.reshape(x.shape[0], -1, P).transpose(2, 1, 0))


def constants_of_shapes():
    f = np.float32
    i = np.arange(P)
    con = np.concatenate([np.ones((P, P)), np.full((P, P), 1 / P), np.full((P, P), 1 / D), np.eye(P),
                          np.broadcast_to(i, (P, P))], 1).astype(f)
    s, t = i[:, None], i[None, :]
    levels = np.zeros((2, P, LEVELS + 1, P), np.int32)
    levels[:, :, 0, :] = s == t
    for level in range(1, LEVELS + 1):
        half = 2 ** (level - 1)
        same = s // (2 * half) == t // (2 * half)
        levels[0, :, level, :] = same & (s // half % 2 == 0) & (t // half % 2 == 1)
        levels[1, :, level, :] = levels[0, :, level, :].T
    masked = lambda keep: np.where(keep, 0.0, MASKED).astype(f)
    rel = s + P - np.arange(2 * P)[None, :]
    swa_mask = masked((rel >= 0) & (rel < P))
    tt = np.arange(T)
    causal = np.stack([masked((tt[:, None] <= tt[None, :])), masked(tt[:, None] >= tt[None, :])])
    causal = causal.reshape(2, NT, P, T).transpose(2, 0, 1, 3)
    window = np.zeros((NT, P, 2 * T), f)
    window[:, :, T:] = masked(np.abs(tt[:, None] - tt[None, :]) <= P).reshape(NT, P, T)
    select = np.zeros((H, H, P), f)
    select[np.arange(H), np.arange(H), :] = 1
    inv_count = np.stack([1.0 / np.minimum(tt + 1, w) for w in POOL_WINDOWS]).astype(f)
    dim = i % A_DIM
    rope_dim = A_DIM // 4
    inv = f(500000.0) ** (-np.arange(0, rope_dim, 2, dtype=f) / f(rope_dim))
    inv_freq = np.where(dim < rope_dim, inv[dim % (rope_dim // 2)], 0.0).astype(f)[:, None]
    perm = np.zeros((P, P), f)
    for r in range(P):
        if dim[r] < rope_dim // 2:
            perm[r, r + rope_dim // 2] = -1
        elif dim[r] < rope_dim:
            perm[r, r - rope_dim // 2] = 1
    n_freq = A_DIM // 4
    inv2 = f(10000.0) ** (-np.arange(n_freq, dtype=f) / f(n_freq))
    ang = np.concatenate([(tt // 64).astype(f)[:, None] * inv2, (tt % 64).astype(f)[:, None] * inv2], -1).astype(f)
    axial = np.stack([np.cos(ang).T[dim // 2], np.sin(ang).T[dim // 2]], 1).astype(f)
    perm_2 = np.zeros((P, P), f)
    perm_2[i[0::2], i[1::2]] = -1
    perm_2[i[1::2], i[0::2]] = 1
    return {"constants": con, "levels": levels, "swa_mask": swa_mask, "causal": causal,
            "window": window.transpose(1, 0, 2), "select": select,
            "inv_count": np.broadcast_to(inv_count, (P,) + inv_count.shape), "inv_freq": inv_freq,
            "perm": perm.T, "axial": axial, "perm_2": perm_2.T}


def lay_out(a):
    w = {}
    w["x"], w["ctx"] = feature_major(a["x"][0]), feature_major(a["ctx_2"][0])
    w["positions"] = np.broadcast_to(a["positions"], (P, T))
    w["ada_w"] = np.stack([streamed(m) for m in a["ada_w"]])
    w["w_mod"] = np.stack([streamed(m) for m in a["w_mod_2"]])
    heads = lambda m: m.reshape(m.shape[0], A_HEADS, A_DIM)[:, Q_ORDER].reshape(m.shape[0], -1)
    cut = lambda m, widths: np.split(m, np.cumsum(widths)[:-1], axis=1)
    aq, af, ai, ag, bq, bk, bv = cut(a["ab_w_in"][0], [512, 512, 512, 512, 512, 128, 128])
    w["ab_w_in"] = chunked(np.concatenate([aq, af, ag, heads(bq), bk], 1))
    w["ab_w_v"] = np.concatenate([ai, bv], 1).reshape(KD, P, -1)
    w["ab_w_out"] = chunked(a["ab_w_out"][0])
    w["pool_w"] = a["pool_w"][0].reshape(4, 2, P, 2, P).transpose(2, 0, 3, 1, 4).reshape(P, KD, 2, P)
    up = a["ffn_w_up"].reshape(2, D, 2, KF, P).transpose(0, 1, 3, 2, 4).reshape(2, D, -1)
    w["w_up"] = np.stack([chunked(m) for m in up])
    w["w_down"] = np.stack([chunked(m) for m in a["ffn_w_down"]])
    mq, mk, mv, mo, mg, q2, k2, v2 = cut(a["ab_w_in_2"][0], [512, 512, 512, 512, 16, 512, 128, 128])
    w["ab_w_in_2"] = chunked(np.concatenate([mq, mk, mo, heads(q2), k2], 1))
    w["ab_w_v_2"] = np.concatenate([mv, v2], 1).reshape(KD, P, -1)
    w["ab_w_gates_2"] = mg.reshape(KD, P, 16).transpose(1, 0, 2)
    w["ab_gate_b_2"] = a["ab_gate_b_2"][0].reshape(4, H).T
    w["ab_w_out_2"] = chunked(a["ab_w_out_2"][0])
    gq, gk, gv, gg, glow = cut(a["gla_w_in_2"][0], [512, 512, 1024, 1024, 32])
    w["gla_w_k_2"], w["gla_w_qg_2"] = chunked(gk), chunked(np.concatenate([gq, gg], 1))
    w["gla_w_v_2"] = gv.reshape(KD, P, -1)
    w["gla_w_low_2"] = glow.reshape(KD, P, 32).transpose(1, 0, 2)
    w["gla_gate_up_2"] = a["gla_gate_up_2"][0].transpose(1, 0, 2)
    w["gla_w_out_2"] = chunked(a["gla_w_out_2"][0])
    w["peer_wq"] = np.stack([chunked(m) for m in a["peer_wq_2"]])
    w["peer_keys"] = a["peer_keys_2"].reshape(2, 2 * PEER_H, N_KEYS, P).transpose(0, 3, 1, 2)
    w["peer_u"] = a["peer_u_2"].reshape(2, N_KEYS, N_KEYS, KD, P).transpose(0, 2, 4, 3, 1).reshape(2, N_KEYS, P, D)
    w["peer_v"] = a["peer_v_2"].reshape(2, N_KEYS, N_KEYS, D)
    spread = lambda v: np.broadcast_to(np.reshape(v, (1, -1)), (P, np.size(v)))
    conv = np.concatenate([a["ffn_conv_w"], a["ffn_conv_b"][:, None, :]], 1)
    vectors = {
        "c": columns(a["c"]), "ada_b": columns(a["ada_b"]), "ln_g": columns(a["ln_g"]), "ln_b": columns(a["ln_b"]),
        "lb_raw": columns(a["hgrn_lb_raw"]), "norm_g": columns(a["hgrn_norm_g"]), "pool_scale": columns(a["pool_scale"]),
        "conv": conv.reshape(2, 4, KF, P).transpose(3, 0, 2, 1).reshape(P, -1), "sinks": spread(a["attn_sinks"]),
        "c_2": np.stack([columns(a["c_ctx_2"]), columns(a["c_2"])], 2).reshape(P, -1), "b_mod_2": columns(a["b_mod_2"]),
        "ln_w_2": columns(a["ln_w_2"]), "ln_b_2": columns(a["ln_b_2"]), "ab_norm_w_2": columns(a["ab_norm_w_2"]),
        "sinks_2": spread(a["ab_sink_2"]), "gla_gate_b_2": columns(a["gla_gate_b_2"]),
        "gla_norm_w_2": columns(a["gla_norm_w_2"])}
    w["vectors"] = np.concatenate([vectors[name] for name, _ in VECTORS], 1)
    w.update(constants_of_shapes())
    return {name: np.ascontiguousarray(v) for name, v in w.items()}


def kernel(**inputs):
    import concourse.bacc as bacc
    from concourse.bass_utils import run_bass_kernel_spmd

    arrays = lay_out({name: np.asarray(v) for name, v in inputs.items()})
    nc = bacc.Bacc("TRN2", target_bir_lowering=False, num_devices=1)
    d = {name: nc.dram_tensor(f"in_{name}", v.shape, mybir.dt.from_np(v.dtype), kind="ExternalInput").ap()
         for name, v in arrays.items()}
    out = nc.dram_tensor("out", (P, KD, T), F32, kind="ExternalOutput").ap()
    program(nc, d, out)
    run = run_bass_kernel_spmd(nc, [{f"in_{name}": v for name, v in arrays.items()}], core_ids=[0])
    y = np.asarray(run.results[0]["out"])
    return np.ascontiguousarray(y.transpose(2, 1, 0).reshape(1, T, D))
```
